# Optimizing a Trainium2 kernel written in Bass

```python
import math
import jax, jax.numpy as jnp
from jax import lax
import numpy as np

D_MODEL = 1024
BATCH = 1
SEQ = 1024
DEPTH = 1
DEC_BATCH = 8
DEC_SEQ = 1
PAST_LEN = 2048
PAGE_SIZE = 128

N_META = 16
MIX_WIDTH = D_MODEL
EPS = 1e-6
HG_WIDTH = MIX_WIDTH // 2
HG_HEADS = 4
HG_DV = HG_WIDTH // HG_HEADS
HG_DK = 128
HG_QK = HG_HEADS * HG_DK
CHUNK = 128
SUB = 16
NS = CHUNK // SUB
SW_WIDTH = MIX_WIDTH - HG_WIDTH
SW_HEAD_DIM = 64
SW_HEADS = SW_WIDTH // SW_HEAD_DIM
SW_KV_HEADS = 2
SW_GROUP = SW_HEADS // SW_KV_HEADS
WINDOW = 128
SW_SCALE = SW_HEAD_DIM ** -0.5
ROPE_THETA = 10000.0
IN_SPLITS = (HG_QK, HG_QK, HG_WIDTH, HG_WIDTH,
             SW_HEADS * SW_HEAD_DIM, SW_KV_HEADS * SW_HEAD_DIM, SW_KV_HEADS * SW_HEAD_DIM)
IN_WIDTH = sum(IN_SPLITS)
PEER_HEADS = 8
N_KEYS = 128
N_EXPERTS = N_KEYS * N_KEYS
PEER_TOPK = 16
D_KEY = 128
PEER_BLOCK = 128

kernel_name = "hymba_hgrn2_swa_sink_peer_step"

F32 = jnp.float32

def rmsnorm(x, g):
    xf = x.astype(F32)
    y = xf * lax.rsqrt(jnp.mean(xf * xf, axis=-1, keepdims=True) + EPS)
    return (y * g.astype(F32)).astype(x.dtype)

def rotary(x, pos):
    half = x.shape[-1] // 2
    inv = ROPE_THETA ** (-jnp.arange(half, dtype=F32) * 2.0 / x.shape[-1])
    ang = pos.astype(F32)[:, None] * inv[None, :]
    cos = jnp.cos(ang)[:, None, :]
    sin = jnp.sin(ang)[:, None, :]
    xf = x.astype(F32)
    x1, x2 = xf[..., :half], xf[..., half:]
    return jnp.concatenate([x1 * cos - x2 * sin, x2 * cos + x1 * sin], axis=-1).astype(x.dtype)

def split_proj(p):
    out = []
    start = 0
    for size in IN_SPLITS:
        out.append(p[..., start:start + size])
        start += size
    return out

def hgrn_features(q_raw, f_raw, i_raw, lb):
    b_, s_ = q_raw.shape[:2]
    q = jax.nn.silu(q_raw.astype(F32)).reshape(b_, s_, HG_HEADS, HG_DK)
    f = (lb + (1.0 - lb) * jax.nn.sigmoid(f_raw.astype(F32))).reshape(b_, s_, HG_HEADS, HG_DK)
    k = 1.0 - f
    v = i_raw.astype(F32).reshape(b_, s_, HG_HEADS, HG_DV)
    return q, f, k, v

def hgrn_chunk_step(s, inp):
    q, g, k, v = inp
    lead = q.shape[:2]
    b = jnp.cumsum(g, axis=-2)
    b_last = b[..., -1:, :]
    o = jnp.einsum('bhck,bhkv->bhcv', q * jnp.exp(b), s)
    qs = q.reshape(*lead, NS, SUB, HG_DK)
    ks = k.reshape(*lead, NS, SUB, HG_DK)
    vs = v.reshape(*lead, NS, SUB, HG_DV)
    bs = b.reshape(*lead, NS, SUB, HG_DK)
    b_end = bs[..., -1, :]
    b_start = jnp.concatenate([jnp.zeros_like(b_end[..., :1, :]), b_end[..., :-1, :]], axis=-2)
    q_in = qs * jnp.exp(bs - b_start[..., None, :])
    k_in = ks * jnp.exp(b_end[..., None, :] - bs)
    sub_ids = jnp.arange(NS)
    earlier = sub_ids[None, :] < sub_ids[:, None]
    gap = b_start[..., :, None, :] - b_end[..., None, :, :]
    decay = jnp.exp(jnp.where(earlier[:, :, None], gap, -jnp.inf))
    a_cross = jnp.einsum('bhitk,bhijk,bhjsk->bhitjs', q_in, decay, k_in)
    pos = jnp.arange(SUB)
    causal = pos[None, :] <= pos[:, None]
    rel = bs[..., :, None, :] - bs[..., None, :, :]
    rel_decay = jnp.exp(jnp.where(causal[:, :, None], rel, -jnp.inf))
    a_diag = jnp.einsum('bhitk,bhitsk,bhisk->bhits', qs, rel_decay, ks)
    o_intra = (jnp.einsum('bhitjs,bhjsv->bhitv', a_cross, vs)
               + jnp.einsum('bhits,bhisv->bhitv', a_diag, vs))
    o = o + o_intra.reshape(*lead, CHUNK, HG_DV)
    s_new = (jnp.exp(b_last[..., 0, :])[..., None] * s
             + jnp.einsum('bhck,bhcv->bhkv', k * jnp.exp(b_last - b), v))
    return s_new, o

def hgrn_chunked(q, logf, k, v):
    b_, lp = q.shape[:2]
    nc = lp // CHUNK

    def to_chunks(t):
        return t.reshape(b_, nc, CHUNK, HG_HEADS, t.shape[-1]).transpose(1, 0, 3, 2, 4)

    xs = (to_chunks(q), to_chunks(logf), to_chunks(k), to_chunks(v))
    s0 = jnp.zeros((b_, HG_HEADS, HG_DK, HG_DV), F32)
    s_fin, o = lax.scan(hgrn_chunk_step, s0, xs)
    o = o.transpose(1, 0, 3, 2, 4).reshape(b_, lp, HG_HEADS, HG_DV)
    return o, s_fin

def hgrn_token_step(s, inp):
    q, f, k, v = inp
    s = f[..., None] * s + k[..., None] * v[..., None, :]
    return s, jnp.einsum('bhk,bhkv->bhv', q, s)

def hgrn_readout(o, gate, gnorm):
    b_, s_ = o.shape[:2]
    o = o * lax.rsqrt(jnp.mean(o * o, axis=-1, keepdims=True) + EPS) * gnorm.astype(F32)
    return o.reshape(b_, s_, HG_WIDTH) * jax.nn.silu(gate.astype(F32))

def sink_softmax(s, sink_b):
    sink_b = sink_b.astype(F32)
    m = jnp.maximum(jnp.max(s, axis=-1, keepdims=True), sink_b)
    p = jnp.exp(s - m)
    return p / (jnp.sum(p, axis=-1, keepdims=True) + jnp.exp(sink_b - m))

def swa_prompt(q, k, v, valid, sink):
    b_, lp = q.shape[:2]
    nb = lp // WINDOW
    qb = q.reshape(b_, nb, WINDOW, SW_KV_HEADS, SW_GROUP, SW_HEAD_DIM)
    kb = k.reshape(b_, nb, WINDOW, SW_KV_HEADS, SW_HEAD_DIM)
    vb = v.reshape(b_, nb, WINDOW, SW_KV_HEADS, SW_HEAD_DIM)

    def prev(t):
        return jnp.pad(t, ((0, 0), (1, 0)) + ((0, 0),) * (t.ndim - 2))[:, :-1]

    kk = jnp.concatenate([prev(kb), kb], axis=2)
    vv = jnp.concatenate([prev(vb), vb], axis=2)
    valid_b = valid.reshape(nb, WINDOW)
    kvalid = jnp.concatenate([jnp.pad(valid_b, ((1, 0), (0, 0)))[:-1], valid_b], axis=1)
    qi = jnp.arange(WINDOW)[:, None] + WINDOW
    si = jnp.arange(2 * WINDOW)[None, :]
    band = (si <= qi) & (si >= qi - WINDOW)
    mask = band[None] & kvalid[:, None, :]
    s = jnp.einsum('bnqkgd,bnskd->bnkgqs', qb, kk, preferred_element_type=F32) * SW_SCALE
    s = jnp.where(mask[None, :, None, None], s, -jnp.inf)
    p = sink_softmax(s, sink.reshape(SW_KV_HEADS, SW_GROUP)[:, :, None, None])
    o = jnp.einsum('bnkgqs,bnskd->bnqkgd', p, vv.astype(F32))
    return o.reshape(b_, lp, SW_HEADS * SW_HEAD_DIM)

def swa_sample(q, k_new, v_new, ck, cv, sink):
    bd, s_ = q.shape[:2]
    wb = ck.shape[1]
    kk = jnp.concatenate([ck, k_new], axis=1)
    vv = jnp.concatenate([cv, v_new], axis=1)
    kpos = PAST_LEN - wb + jnp.arange(wb + s_)
    qpos = PAST_LEN + jnp.arange(s_)
    mask = (kpos[None, :] <= qpos[:, None]) & (kpos[None, :] >= qpos[:, None] - WINDOW)
    qg = q.reshape(bd, s_, SW_KV_HEADS, SW_GROUP, SW_HEAD_DIM)
    s = jnp.einsum('bqkgd,bskd->bkgqs', qg, kk, preferred_element_type=F32) * SW_SCALE
    s = jnp.where(mask[None, None, None], s, -jnp.inf)
    p = sink_softmax(s, sink.reshape(SW_KV_HEADS, SW_GROUP)[:, :, None, None])
    o = jnp.einsum('bkgqs,bskd->bqkgd', p, vv.astype(F32)).reshape(bd, s_, SW_HEADS * SW_HEAD_DIM)
    return o, kk[:, -wb:], vv[:, -wb:]

def mixer_prompt(h, lb, w_in, gnorm, sink, w_out):
    b_, l_ = h.shape[:2]
    pad = CHUNK - N_META
    lp = l_ + pad
    proj = jnp.einsum('bld,de->ble', h, w_in)
    proj = jnp.pad(proj, ((0, 0), (pad, 0), (0, 0)))
    valid = jnp.arange(lp) >= pad
    pos = jnp.arange(lp) - pad
    hq, hf, hi, hg, aq, ak, av = split_proj(proj)
    q, f, k, v = hgrn_features(hq, hf, hi, lb)
    vmask = valid[None, :, None, None]
    k = jnp.where(vmask, k, 0.0)
    logf = jnp.where(vmask, jnp.log(f), 0.0)
    o, s_fin = hgrn_chunked(q, logf, k, v)
    o_hg = hgrn_readout(o[:, pad:], hg[:, pad:], gnorm)
    aq = rotary(aq.reshape(b_, lp, SW_HEADS, SW_HEAD_DIM), pos)
    ak = rotary(ak.reshape(b_, lp, SW_KV_HEADS, SW_HEAD_DIM), pos)
    av = av.reshape(b_, lp, SW_KV_HEADS, SW_HEAD_DIM)
    o_sw = swa_prompt(aq, ak, av, valid, sink)[:, pad:]
    mix = jnp.concatenate([o_hg.astype(h.dtype), o_sw.astype(h.dtype)], axis=-1)
    y = jnp.einsum('ble,ed->bld', mix, w_out)
    wb = min(WINDOW, PAST_LEN)
    return y, s_fin, ak[:, -wb:], av[:, -wb:]

def mixer_sample(h, s0, ck, cv, lb, w_in, gnorm, sink, w_out):
    bd, s_ = h.shape[:2]
    proj = jnp.einsum('bld,de->ble', h, w_in)
    hq, hf, hi, hg, aq, ak, av = split_proj(proj)
    q, f, k, v = hgrn_features(hq, hf, hi, lb)
    tr = lambda t: jnp.swapaxes(t, 0, 1)
    s_new, o = lax.scan(hgrn_token_step, s0.astype(F32), (tr(q), tr(f), tr(k), tr(v)))
    o_hg = hgrn_readout(tr(o), hg, gnorm)
    pos = PAST_LEN + jnp.arange(s_)
    aq = rotary(aq.reshape(bd, s_, SW_HEADS, SW_HEAD_DIM), pos)
    ak = rotary(ak.reshape(bd, s_, SW_KV_HEADS, SW_HEAD_DIM), pos)
    av = av.reshape(bd, s_, SW_KV_HEADS, SW_HEAD_DIM)
    o_sw, k_buf, v_buf = swa_sample(aq, ak, av, ck.astype(ak.dtype), cv.astype(av.dtype), sink)
    mix = jnp.concatenate([o_hg.astype(h.dtype), o_sw.astype(h.dtype)], axis=-1)
    y = jnp.einsum('ble,ed->bld', mix, w_out)
    return y, s_new.astype(s0.dtype), k_buf.astype(ck.dtype), v_buf.astype(cv.dtype)

def peer_block(xb, wq, keys, u, v):
    t_ = xb.shape[0]
    qh = jnp.einsum('td,de->te', xb, wq, preferred_element_type=F32).reshape(t_, PEER_HEADS, 2, D_KEY)
    sc = jnp.einsum('thpd,hpnd->thpn', qh, keys.astype(F32))
    top_s, top_i = lax.top_k(sc, PEER_TOPK)
    cand = top_s[:, :, 0, :, None] + top_s[:, :, 1, None, :]
    best_s, best_c = lax.top_k(cand.reshape(t_, PEER_HEADS, PEER_TOPK * PEER_TOPK), PEER_TOPK)
    idx1 = jnp.take_along_axis(top_i[:, :, 0], best_c // PEER_TOPK, axis=-1)
    idx2 = jnp.take_along_axis(top_i[:, :, 1], best_c % PEER_TOPK, axis=-1)
    expert = idx1 * N_KEYS + idx2
    gate = jax.nn.softmax(best_s, axis=-1)
    u_sel = u[expert]
    act = jax.nn.gelu(jnp.einsum('td,thkd->thk', xb, u_sel, preferred_element_type=F32), approximate=False)
    v_sel = v[expert]
    return jnp.einsum('thk,thkd->td', gate * act, v_sel.astype(F32))

def peer(h, wq, keys, u, v):
    shp = h.shape
    xt = h.reshape(-1, shp[-1])
    n = xt.shape[0]
    nblk = -(-n // PEER_BLOCK)
    xt = jnp.pad(xt, ((0, nblk * PEER_BLOCK - n), (0, 0))).reshape(nblk, PEER_BLOCK, shp[-1])
    out = lax.map(lambda xb: peer_block(xb, wq, keys, u, v), xt)
    return out.reshape(-1, shp[-1])[:n].reshape(shp).astype(h.dtype)

def setup_inputs(seed: int = 0) -> dict:
    key = jax.random.key(seed)
    ks = jax.random.split(key, 20)
    wb = min(WINDOW, PAST_LEN)

    def nrm(k, shape, scale):
        return jax.random.normal(k, shape, F32) * scale

    return {
        "x_prompt": nrm(ks[0], (BATCH, SEQ, D_MODEL), 1.0),
        "x_sample": nrm(ks[1], (DEC_BATCH, DEC_SEQ, D_MODEL), 1.0),
        "state_hgrn": nrm(ks[2], (DEPTH, DEC_BATCH, HG_HEADS, HG_DK, HG_DV), 0.5),
        "cache_k": nrm(ks[3], (DEPTH, DEC_BATCH, wb, SW_KV_HEADS, SW_HEAD_DIM), 1.0),
        "cache_v": nrm(ks[4], (DEPTH, DEC_BATCH, wb, SW_KV_HEADS, SW_HEAD_DIM), 1.0),
        "meta_tokens": nrm(ks[5], (N_META, D_MODEL), 1.0),
        "lb_logits": nrm(ks[6], (DEPTH + 1, HG_QK), 0.5),
        "norm_mix": 1.0 + nrm(ks[7], (DEPTH, D_MODEL), 0.02),
        "w_in": nrm(ks[8], (DEPTH, D_MODEL, IN_WIDTH), D_MODEL ** -0.5),
        "hgrn_norm": 1.0 + nrm(ks[9], (DEPTH, HG_HEADS, HG_DV), 0.02),
        "attn_sink": nrm(ks[10], (DEPTH, SW_HEADS), 0.5),
        "w_out": nrm(ks[11], (DEPTH, MIX_WIDTH, D_MODEL), MIX_WIDTH ** -0.5),
        "norm_ffn": 1.0 + nrm(ks[12], (DEPTH, D_MODEL), 0.02),
        "peer_wq": nrm(ks[13], (DEPTH, D_MODEL, PEER_HEADS * 2 * D_KEY), D_MODEL ** -0.5),
        "peer_keys": nrm(ks[14], (DEPTH, PEER_HEADS, 2, N_KEYS, D_KEY), D_KEY ** -0.5),
        "peer_u": nrm(ks[15], (DEPTH, N_EXPERTS, D_MODEL), D_MODEL ** -0.5),
        "peer_v": nrm(ks[16], (DEPTH, N_EXPERTS, D_MODEL), PEER_HEADS ** -0.5),
        "norm_final": 1.0 + nrm(ks[17], (D_MODEL,), 0.02),
    }

def reference(x_prompt, x_sample, state_hgrn, cache_k, cache_v, meta_tokens, lb_logits, norm_mix, w_in,
              hgrn_norm, attn_sink, w_out, norm_ffn, peer_wq, peer_keys, peer_u, peer_v, norm_final):
    lower = jnp.cumsum(jax.nn.softmax(lb_logits.astype(F32), axis=0), axis=0)
    meta = jnp.broadcast_to(meta_tokens[None].astype(x_prompt.dtype), (x_prompt.shape[0], N_META, D_MODEL))
    hp = jnp.concatenate([meta, x_prompt], axis=1)
    hs = x_sample
    sp_list, kp_list, vp_list, ss_list, ks_list, vs_list = [], [], [], [], [], []
    for layer in range(DEPTH):
        a_p, s_p, k_p, v_p = mixer_prompt(rmsnorm(hp, norm_mix[layer]), lower[layer], w_in[layer],
                                          hgrn_norm[layer], attn_sink[layer], w_out[layer])
        a_s, s_s, k_s, v_s = mixer_sample(rmsnorm(hs, norm_mix[layer]), state_hgrn[layer], cache_k[layer],
                                          cache_v[layer], lower[layer], w_in[layer], hgrn_norm[layer],
                                          attn_sink[layer], w_out[layer])
        hp = hp + a_p
        hs = hs + a_s
        hp = hp + peer(rmsnorm(hp, norm_ffn[layer]), peer_wq[layer], peer_keys[layer], peer_u[layer], peer_v[layer])
        hs = hs + peer(rmsnorm(hs, norm_ffn[layer]), peer_wq[layer], peer_keys[layer], peer_u[layer], peer_v[layer])
        sp_list.append(s_p.astype(state_hgrn.dtype))
        kp_list.append(k_p.astype(cache_k.dtype))
        vp_list.append(v_p.astype(cache_v.dtype))
        ss_list.append(s_s)
        ks_list.append(k_s)
        vs_list.append(v_s)
    y_prompt = rmsnorm(hp[:, N_META:], norm_final)
    y_sample = rmsnorm(hs, norm_final)
    new_state_hgrn_prompt = jnp.stack(sp_list)
    new_cache_k_prompt = jnp.stack(kp_list)
    new_cache_v_prompt = jnp.stack(vp_list)
    new_state_hgrn_sample = jnp.stack(ss_list)
    new_cache_k_sample = jnp.stack(ks_list)
    new_cache_v_sample = jnp.stack(vs_list)
    return (y_prompt, y_sample, new_state_hgrn_prompt, new_cache_k_prompt, new_cache_v_prompt,
            new_state_hgrn_sample, new_cache_k_sample, new_cache_v_sample)


_drawn_inputs = setup_inputs


def setup_inputs(seed=0):
    import zlib

    import numpy as np

    out = dict(_drawn_inputs(seed))
    spreads = {}
    factors = {'hgrn_norm': 7.905, 'attn_sink': 34.16, 'norm_final': 23.675, 'norm_ffn': 9.876}
    for name, (base, spread) in spreads.items():
        noise = np.random.default_rng([zlib.crc32(name.encode()), seed]).standard_normal(out[name].shape)
        drawn = base * np.exp(spread * noise) if base else spread * noise
        out[name] = __import__('jax').numpy.asarray(drawn.astype(out[name].dtype))
    for name, factor in factors.items():
        out[name] = (out[name] * factor).astype(out[name].dtype)
    return out
```

```python
from contextlib import ExitStack

import numpy as np

import concourse.bass as bass
from concourse import mybir

F32 = mybir.dt.float32
U32 = mybir.dt.uint32
I32 = mybir.dt.int32
ALU = mybir.AluOpType
ACT = mybir.ActivationFunctionType
AX = mybir.AxisListType

P = 128
DM = 1024
KT = DM // P
NB = 8
META = 16
NS = 8
HH = 4
DK = 128
HW = HH * DK
SH = 8
KV = 2
HD = 64
GQ = SH // KV
WIN = 128
EPS = 1e-6
SCALE = HD ** -0.5
OFF_Q, OFF_F, OFF_I, OFF_G = 0, HW, 2 * HW, 3 * HW
OFF_AQ, OFF_AK = 4 * HW, 4 * HW + SH * HD
IN_W = OFF_AK + 2 * KV * HD
LEVELS = 7
GRAMS = LEVELS + 1
PH = 8
TOPK = 16
NKEY = 128
NEXP = NKEY * NKEY
SLOTS = PH * TOPK
RING = 8
DIAGS = 4
LOW = -3.0e38


def standalone(eng, idle):
    eng.sem_inc(idle, 1)


def mixer_program(nc, io):
    with ExitStack() as ctx:
        def sb(name, shape, dt=F32):
            return ctx.enter_context(nc.sbuf_tensor("a_" + name, shape, dt))

        def sem(name):
            return ctx.enter_context(nc.semaphore("a_" + name))

        def bank(name):
            return ctx.enter_context(nc.psum_tensor("a_" + name, [P, 512], F32))

        w_in = sb("w_in", [P, KT, IN_W])
        ident = sb("ident", [P, P])
        lmask = sb("lmask", [P, GRAMS, P], I32)
        reset = sb("reset", [P, HH, P])
        gmix = sb("gmix", [P, DM])
        gnorm = sb("gnorm", [P, HW])
        sinkb = sb("sinkb", [P, SH])
        sinkc = sb("sinkc", [SH, 1])
        lbl = sb("lbl", [P, 2, HH])
        lbw = sb("lbw", [P, 4, HH])
        lb, oml = lbw[:, 2, :], lbw[:, 3, :]
        xs = sb("xs", [P, DM])
        xn = sb("xn", [P, DM])
        xT = sb("xT", [P, KT, P])
        ss = sb("ss", [P, 3])
        rope = sb("rope", [P, 2, HD // 2])
        wmask = sb("wmask", [P, 2 * WIN])
        ef = sb("ef", [P, HH, P])
        ff = sb("ff", [P, HH, P])
        kk = sb("kk", [P, HH, P])
        qq = sb("qq", [P, HH, P])
        bb = sb("bb", [P, HH, P])
        dd = sb("dd", [P, 2, HH, P])
        mm = sb("mm", [P, 2, HH, P])
        at = sb("at", [P, HH, P])
        eb = sb("eb", [P, HH, P])
        qb = sb("qb", [P, HH, P])
        ket = sb("ket", [P, HH, DK])
        st = sb("st", [P, HH, DK])
        vv = sb("vv", [P, HW])
        gg = sb("gg", [P, 2, HW])
        rs = sb("rs", [P, 3, HH])
        mixh = sb("mixh", [P, HW])
        qk = sb("qk", [P, 5, 2, HD])
        rt = sb("rt", [P, 2, 10, HD])
        qkr = sb("qkr", [P, 5, 2, HD])
        qT = sb("qT", [P, 4, P])
        kT = sb("kT", [P, 2, WIN])
        va = sb("va", [P, 2, KV * HD])
        sm = sb("sm", [P, SH, 2 * WIN])
        pT = sb("pT", [P, SH, 2, P])
        mx = sb("mx", [P, 6, SH])
        mixa = sb("mixa", [P, SH * HD])
        mixT = sb("mixT", [P, KT, P])

        s0 = sb("s0", [P, NS * HH, DK])
        sel = mm[0:NS].rearrange("p a h c -> p (a h) c")
        qd = sb("qd", [P, HH, NS * NS])
        qbd = sb("qbd", [P, NS, SH])
        sx = sb("sx", [SH, 6, NS])
        rn = sb("rn", [NS, NS, SH])
        vnd = sb("vnd", [NS, KV, 2, HD])
        kc = pT[:, 0:4].rearrange("p h a c -> p (h a) c")
        kcT = pT[:, 4:8].rearrange("p h a c -> p (h a) c")
        v2 = sm[:].rearrange("p h c -> p (h c)").rearrange("p (b s r d) -> p b s r d", b=NS, s=KV, r=2)
        sc = rt[0:SH].rearrange("p a b c -> p (a b c)")[:, 0:NS * (WIN + 1)].rearrange("p (b c) -> p b c", b=NS)
        pTs = qb[:].rearrange("p h c -> p (h c)")[:, 0:NS * SH]

        T0, T1, P0, P1, P2, P3, P4, P5 = (bank(n) for n in ("T0", "T1", "P0", "P1", "P2", "P3", "P4", "P5"))
        GB = [P0, P1]

        def bank4(b):
            return b[:].rearrange("p (h c) -> p h c", h=4)

        c_in, w_fq, w_rest = sem("c_in"), sem("w_fq"), sem("w_rest")
        x_in, side_in = sem("x_in"), sem("side_in")
        s_in, mix_out, s_out = sem("s_in"), sem("mix_out"), sem("s_out")
        names = ("r_ready xn_ready pe_xT xT_ready pe_F pe_Q pe_AQ pe_AKV pe_V pe_G ef_ready f_ready lf_ready eq_ready "
                 "q_ready b_ready eb_ready D_ready E_ready M_ready pe_gram A_ready qk_ready rot_ready pe_qkT qkT_ready "
                 "v_ready eg_ready gg_ready pe_S sm_ready m_ready p_ready den_ready kd_ready ke_exp ke_ready pe_KET "
                 "ket_ready pe_dS pe_O st_ready ro_ready rr_ready mixh_ready pe_PT pT_ready pe_Oa mixa_ready pe_mix "
                 "mixT_ready lb_ready sam_ready pe_sam act_sam idle").split()
        S = {n: sem(n) for n in names}
        idle = S["idle"]
        NC_IN = 8
        NS_IN = 7

        block = ctx.enter_context(nc.Block())

        @block.sync
        def _(sp):
            sp.dma_start(xs[:], io["x_all"][0:P, :]).then_inc(x_in, 16)
            w = io["w_in"].rearrange("(k p) n -> p k n", p=P)
            for dst, src in ((ident[:], io["ident"]), (gmix[:], io["norm_mix"].broadcast_to([P, DM])),
                             (lbl[:], io["lb_logits"].rearrange("l (h p) -> p l h", p=P)),
                             (reset[:], io["reset"].rearrange("p (h c) -> p h c", h=HH)),
                             (lmask[:], io["level_masks"].rearrange("p (g c) -> p g c", g=GRAMS)),
                             (gnorm[:], io["hgrn_norm"].broadcast_to([P, HW])),
                             (sinkb[:], io["attn_sink"].broadcast_to([P, SH])),
                             (sinkc[:], io["attn_sink"].rearrange("a h -> h a"))):
                with nc.allow_non_contiguous_dma(reason="a few small constants"):
                    sp.dma_start(dst, src).then_inc(c_in, 16)
            for lo, hi, s in ((OFF_Q, OFF_I, w_fq), (OFF_I, IN_W, w_rest)):
                for k in range(0, KT, 2):
                    sp.dma_start(w_in[:, k:k + 2, lo:hi], w[:, k:k + 2, lo:hi]).then_inc(s, 16)
            sp.dma_start(s0[:], io["state_s"].rearrange("n k v -> k n v")).then_inc(s_in, 16)
            sp.dma_start(sel, io["sel"].rearrange("p (b c) -> p b c", b=NS)).then_inc(s_in, 16)
            sp.dma_start(kc, io["cache_k"].rearrange("b w c -> w b c")).then_inc(s_in, 16)
            for s in range(KV):
                for r in range(2):
                    sp.dma_start(v2[:, :, s, r, :], io["cache_v"].rearrange("b w c -> w b c")[:, :, s * HD:(s + 1) * HD]).then_inc(s_in, 16)
            sp.dma_start(rope[:], io["rope"][0:P].rearrange("p (a c) -> p a c", a=2)).then_inc(side_in, 16)
            sp.dma_start(wmask[:], io["wmask"][0:P, :]).then_inc(side_in, 16)
            for dst, src in (("new_k_s", "cache_k"), ("new_v_s", "cache_v")):
                sp.dma_start(io[dst][:, 0:WIN - 1, :], io[src][:, 1:WIN, :]).then_inc(s_out, 16)
            sp.wait_ge(S["rot_ready"], 1)
            sp.dma_start(io["new_k_s"][:, WIN - 1, :], qkr[0:NS, 4, :, :].rearrange("p a c -> p (a c)")).then_inc(s_out, 16)
            sp.wait_ge(S["qk_ready"], 1)
            sp.dma_start(io["new_v_s"][:, WIN - 1, :], va[0:NS, 1, :]).then_inc(s_out, 16)
            sp.wait_ge(S["sam_ready"], 1 + NS)
            sp.dma_start(io["new_state_s"].rearrange("n k v -> k n v"), s0[:]).then_inc(s_out, 16)
            sp.wait_ge(S["xn_ready"], 1)
            sp.dma_start(xs[:], io["x_all"][P:2 * P, :]).then_inc(x_in, 16)
            sp.wait_ge(S["mixT_ready"], 1)
            sp.dma_start(io["mix_scratch"][NB], mixT[:]).then_inc(mix_out, 16)
            with sp.Fori(0, NB) as i:
                sp.wait_ge(S["mixa_ready"], i + 1)
                sp.dma_start(rope[:], io["rope"][bass.ds((i + 1) * P, P), :].rearrange("p (a c) -> p a c", a=2)).then_inc(side_in, 16)
                sp.dma_start(wmask[:], io["wmask"][bass.ds(i * P, P), :]).then_inc(side_in, 16)
                sp.wait_ge(S["xn_ready"], i + 2)
                sp.dma_start(xs[:], io["x_all"][bass.ds((i + 2) * P, P), :]).then_inc(x_in, 16)
                sp.wait_ge(S["mixT_ready"], i + 2)
                sp.dma_start(io["mix_scratch"][bass.ds(i, 1)].rearrange("a p k c -> (a p) k c"), mixT[:]).then_inc(mix_out, 16)
            sp.wait_ge(S["st_ready"], NB + 1)
            sp.dma_start(io["new_state_p"].rearrange("h p v -> p h v"), st[:]).then_inc(s_out, 16)
            sp.dma_start(io["new_k_p"], qkr[:, 4, :, :].rearrange("p a c -> p (a c)")).then_inc(s_out, 16)
            sp.dma_start(io["new_v_p"], va[:, 1, :]).then_inc(s_out, 16)
            sp.wait_ge(s_out, 16 * 8)
            sp.wait_ge(mix_out, 16 * (NB + 1))
            sp.wait_ge(x_in, 16 * (NB + 2))

        def sampled_pe(pe):
            pe.wait_ge(S["v_ready"], 1)
            pe.wait_ge(s_in, 16 * NS_IN)
            for b in range(NS):
                if b >= 2:
                    pe.wait_ge(S["sam_ready"], b)
                pe.matmul((P4, P5)[b % 2][:], sel[:, b, :], vv[0:NS, :], start=True, stop=True).then_inc(S["pe_sam"], 1)
            pe.wait_ge(S["sam_ready"], 1 + NS)
            for h in range(HH):
                for b in range(NS):
                    m = pe.matmul(P2[0:NS, h * P:(h + 1) * P], qd[:, h, b * NS:(b + 1) * NS], s0[:, b * HH + h, :],
                                  start=(b == 0), stop=(b == NS - 1))
            m.then_inc(S["pe_O"], 1)
            pe.wait_ge(S["qkT_ready"], 1)
            for b in range(NS):
                m = pe.transpose((T0, T1)[b // 4][:, (b % 4) * P:(b % 4 + 1) * P], kc[:, b, :], ident[:])
            m.then_inc(S["pe_sam"], 1)
            pe.wait_ge(S["act_sam"], 1)
            pe.wait_ge(S["st_ready"], 1)
            for b in range(NS):
                pe.matmul((P4, P5)[b // 4][0:SH, (b % 4) * P:(b % 4 + 1) * P], qbd[:, b, :], kcT[:, b, :], start=True, stop=True)
                m = pe.matmul(P3[0:SH, b:b + 1], qbd[:, b, :], kT[:, 1, b:b + 1], start=True, stop=True)
            m.then_inc(S["pe_sam"], 1)
            pe.wait_ge(S["sam_ready"], 3 + NS)
            for b in range(NS):
                pe.transpose(T0[:, b * SH:(b + 1) * SH], sc[:, b, 0:WIN], ident[0:SH, 0:SH])
            pe.transpose(T1[0:NS, 0:SH], sc[:, :, WIN], ident[0:SH, 0:SH]).then_inc(S["pe_sam"], 1)
            pe.wait_ge(S["act_sam"], 3)
            pe.wait_ge(S["sam_ready"], 4 + NS)
            for b in range(NS):
                for s in range(KV):
                    lo = b * SH + s * GQ
                    pe.matmul(P4[:, lo:lo + GQ], v2[:, b, s].rearrange("p r d -> p (r d)"), pTs[:, lo:lo + GQ], start=True, stop=False)
                    m = pe.matmul(P4[:, lo:lo + GQ], vnd[:, s].rearrange("p r d -> p (r d)"), rn[:, b, s * GQ:(s + 1) * GQ],
                                  start=False, stop=True)
            m.then_inc(S["pe_sam"], 1)
            pe.wait_ge(S["mixh_ready"], 1)
            for k in range(4):
                m = pe.transpose(T1[:, 64 + k * NS:64 + (k + 1) * NS], mixh[0:NS, k * P:(k + 1) * P], ident[0:NS, 0:NS])
            m.then_inc(S["pe_mix"], 1)

        def sampled_act(act, readout_norm):
            readout_norm(0, NS)
            act.wait_ge(S["pe_sam"], NS + 1)
            act.activation(kcT[:, 0:4, :], bank4(T0), ACT.Copy)
            act.activation(kcT[:, 4:8, :], bank4(T1), ACT.Copy).then_inc(S["act_sam"], 1)
            act.wait_ge(S["sam_ready"], 2 + NS)
            act.activation(sc, sc, ACT.Exp)
            act.activation(sx[:, 2, :], sx[:, 1, :], ACT.Exp, scale=-1.0, bias=sinkc[:]).then_inc(S["act_sam"], 1)
            act.wait_ge(S["pe_sam"], NS + 3)
            act.activation(pTs, T0[:, 0:NS * SH], ACT.Copy).then_inc(S["act_sam"], 1)

        def sampled_vector(v, mix_a):
            v.memset(qd[:], 0.0)
            v.memset(qbd[:], 0.0)
            v.memset(mixT[:], 0.0)
            v.drain()
            v.tensor_copy(qd[:, :, 0:NS * NS:NS + 1], qq[:, :, 0:NS])
            for s in range(KV):
                lo = HD * s
                v.tensor_copy(qbd[lo:lo + HD, :, s * GQ:(s + 1) * GQ], qT[lo:lo + HD, :, 0:NS].rearrange("p j b -> p b j"))
            v.wait_ge(S["qk_ready"], 1)
            for r in range(2):
                m = v.tensor_copy(vnd[:, :, r, :], va[0:NS, 1, :].rearrange("p (s d) -> p s d", s=KV))
            m.then_inc(S["sam_ready"], 1)
            v.wait_ge(s_in, 16 * NS_IN)
            for b in range(NS):
                for h in range(HH):
                    v.tensor_scalar(s0[:, b * HH + h, :], s0[:, b * HH + h, :], ff[:, h, b:b + 1], None, ALU.mult)
            v.drain()
            for b in range(NS):
                v.wait_ge(S["pe_sam"], b + 1)
                for h in range(HH):
                    m = v.scalar_tensor_tensor(out=s0[:, b * HH + h, :], in0=(P4, P5)[b % 2][:, h * P:(h + 1) * P],
                                               scalar=kk[:, h, b:b + 1], in1=s0[:, b * HH + h, :], op0=ALU.mult, op1=ALU.add)
                m.then_inc(S["sam_ready"], 1)
            mix_a(0, NS)
            v.wait_ge(S["pe_sam"], NS + 2)
            for a, b in enumerate((P4, P5)):
                v.tensor_scalar(sc[:, 4 * a:4 * a + 4, 0:WIN], bank4(b)[0:SH], SCALE, None, ALU.mult)
            v.tensor_scalar(sc[:, :, WIN], P3[0:SH, 0:NS], SCALE, None, ALU.mult)
            v.drain()
            v.tensor_reduce(sx[:, 0, :], sc, AX.X, ALU.max)
            v.drain()
            v.tensor_scalar(sx[:, 1, :], sx[:, 0, :], sinkc[:], None, ALU.max)
            v.drain()
            v.tensor_tensor(sc, sc, sx[:, 1, :].rearrange("p (b c) -> p b c", c=1).broadcast_to([SH, NS, WIN + 1]),
                            ALU.subtract).then_inc(S["sam_ready"], 1)
            v.wait_ge(S["act_sam"], 2)
            v.tensor_reduce(sx[:, 3, :], sc, AX.X, ALU.add)
            v.drain()
            v.tensor_tensor(sx[:, 4, :], sx[:, 3, :], sx[:, 2, :], ALU.add)
            v.drain()
            v.reciprocal(sx[:, 5, :], sx[:, 4, :])
            v.drain()
            v.tensor_tensor(sc, sc, sx[:, 5, :].rearrange("p (b c) -> p b c", c=1).broadcast_to([SH, NS, WIN + 1]),
                            ALU.mult).then_inc(S["sam_ready"], 1)
            v.wait_ge(S["pe_sam"], NS + 3)
            v.tensor_tensor(rn[:], T1[0:NS, 0:SH].rearrange("p (a h) -> p a h", a=1).broadcast_to([NS, NS, SH]),
                            ident[0:NS, 0:NS].rearrange("p (b a) -> p b a", a=1).broadcast_to([NS, NS, SH]), ALU.mult)\
                .then_inc(S["sam_ready"], 1)
            v.wait_ge(S["pe_sam"], NS + 4)
            for r in range(2):
                lo = HD * r
                v.tensor_copy(mixT[lo:lo + HD, 4:8, 0:NS],
                              P4[lo:lo + HD, 0:NS * SH].rearrange("p (b j r) -> p r j b", b=NS, r=2)[:, r])
            v.wait_ge(S["pe_mix"], 1)
            v.tensor_copy(mixT[:, 0:4, 0:NS], T1[:, 64:64 + 4 * NS].rearrange("p (k b) -> p k b", k=4)).then_inc(S["mixT_ready"], 1)
            v.drain()
            v.tensor_copy(sx[:, 0, :], sx[:, 1, :]).then_inc(S["mixa_ready"], 1)

        @block.tensor
        def _(pe):
            def x_transposes(t):
                pe.wait_ge(S["xn_ready"], t + 1)
                for k in range(KT):
                    m = pe.transpose((T0 if k < 4 else T1)[:, (k % 4) * P:(k % 4 + 1) * P], xn[:, k * P:(k + 1) * P], ident[:])
                m.then_inc(S["pe_xT"], 1)

            def feature_projection(out, off, done):
                for h in range(HH):
                    for k in range(KT):
                        m = pe.matmul(out[:, h * P:(h + 1) * P], w_in[:, k, off + h * P:off + (h + 1) * P], xT[:, k, :],
                                      start=(k == 0), stop=(k == KT - 1))
                m.then_inc(done, 1)

            def token_projection(out, off, width, done):
                for k in range(KT):
                    m = pe.matmul(out[:, 0:width], xT[:, k, :], w_in[:, k, off:off + width], start=(k == 0), stop=(k == KT - 1))
                m.then_inc(done, 1)

            def gram(t, g):
                if g < LEVELS:
                    pe.wait_ge(S["M_ready"], LEVELS * (t - 1) + g + 1)
                if g >= 2:
                    pe.wait_ge(S["A_ready"], GRAMS * (t - 1) + g - 1)
                for h in range(HH):
                    a = mm[:, g % 2, h, :] if g < LEVELS else kk[:, h, :]
                    b = mm[:, g % 2, h, :] if g < LEVELS else qq[:, h, :]
                    m = pe.matmul(GB[g % 2][:, h * P:(h + 1) * P], a, b, start=True, stop=True)
                m.then_inc(S["pe_gram"], 1)

            def qk_transposes(t):
                pe.wait_ge(S["rot_ready"], t + 1)
                for j in range(5):
                    m = pe.transpose(T0[:, j * P:(j + 1) * P] if j < 4 else T1[:, 0:P],
                                     qkr[:, j, :, :].rearrange("p a c -> p (a c)"), ident[:])
                m.then_inc(S["pe_qkT"], 1)

            def scores(t, n):
                if n == 0:
                    pe.wait_ge(S["qkT_ready"], t + 1)
                else:
                    pe.wait_ge(S["sm_ready"], 2 * (t - 1) + 1)
                for s, out in enumerate((P4, P5)):
                    for a in range(2):
                        lo = HD * s
                        m = pe.matmul(out[:, a * 256:(a + 1) * 256], qT[lo:lo + HD, 2 * n + a, :],
                                      kT[lo:lo + HD, :, :].rearrange("p a c -> p (a c)"), start=True, stop=True)
                m.then_inc(S["pe_S"], 1)

            def state_products(t):
                pe.wait_ge(S["ke_ready"], t + 1)
                for h in range(HH):
                    m = pe.transpose(T0[:, h * P:(h + 1) * P], at2[:, h, :], ident[:])
                m.then_inc(S["pe_KET"], 1)
                pe.wait_ge(S["ket_ready"], t + 1)
                pe.wait_ge(S["gg_ready"], t + 1)
                for h in range(HH):
                    m = pe.matmul(P3[:, h * P:(h + 1) * P], ket[:, h, :], vv[:, h * P:(h + 1) * P], start=True, stop=True)
                m.then_inc(S["pe_dS"], 1)

            def readout(t):
                pe.wait_ge(S["A_ready"], GRAMS * t)
                for h in range(HH):
                    pe.matmul(P2[:, h * P:(h + 1) * P], qb[:, h, :], st[:, h, :], start=True, stop=False)
                    m = pe.matmul(P2[:, h * P:(h + 1) * P], at[:, h, :], vv[:, h * P:(h + 1) * P], start=False, stop=True)
                m.then_inc(S["pe_O"], 1)

            def p_transposes(t, n):
                if n == 0:
                    pe.wait_ge(S["p_ready"], t)
                if n >= 2:
                    pe.wait_ge(S["pT_ready"], 4 * (t - 1) + n - 1)
                b = T0 if n % 2 == 0 else T1
                for a in range(4):
                    h, kb = 2 * n + a // 2, a % 2
                    m = pe.transpose(b[:, a * P:(a + 1) * P], sm[:, h, kb * P:(kb + 1) * P], ident[:])
                m.then_inc(S["pe_PT"], 1)

            def values(t):
                pe.wait_ge(S["pT_ready"], 4 * t)
                for h in range(SH):
                    lo = HD * (h // GQ)
                    for kb in range(2):
                        m = pe.matmul(P0[:, h * HD:(h + 1) * HD], pT[:, h, kb, :], va[:, kb, lo:lo + HD],
                                      start=(kb == 0), stop=(kb == 1))
                m.then_inc(S["pe_Oa"], 1)

            def mix_transposes(t):
                pe.wait_ge(S["mixh_ready"], t + 1)
                for k in range(4):
                    pe.transpose(T0[:, k * P:(k + 1) * P], mixh[:, k * P:(k + 1) * P], ident[:])
                pe.wait_ge(S["mixa_ready"], t + 1)
                for k in range(4):
                    m = pe.transpose(T1[:, k * P:(k + 1) * P], mixa[:, k * P:(k + 1) * P], ident[:])
                m.then_inc(S["pe_mix"], 1)

            at2 = dd[:, 0]
            pe.wait_ge(c_in, 16 * NC_IN)
            x_transposes(0)
            pe.wait_ge(S["xT_ready"], 1)
            pe.wait_ge(w_fq, 64)
            feature_projection(P0, OFF_F, S["pe_F"])
            feature_projection(P1, OFF_Q, S["pe_Q"])
            pe.wait_ge(w_rest, 64)
            token_projection(P4, OFF_AQ, 512, S["pe_AQ"])
            token_projection(P5, OFF_AK, 256, S["pe_AKV"])
            qk_transposes(0)
            token_projection(P2, OFF_I, 512, S["pe_V"])
            token_projection(P3, OFF_G, 512, S["pe_G"])
            state_products(0)
            sampled_pe(pe)

            with pe.Fori(1, NB + 1) as t:
                x_transposes(t)
                pe.wait_ge(S["xT_ready"], t + 1)
                feature_projection(P0, OFF_F, S["pe_F"])
                feature_projection(P1, OFF_Q, S["pe_Q"])
                token_projection(P4, OFF_AQ, 512, S["pe_AQ"])
                token_projection(P5, OFF_AK, 256, S["pe_AKV"])
                pe.wait_ge(S["q_ready"], t + 1)
                gram(t, 0)
                gram(t, 1)
                qk_transposes(t)
                token_projection(P2, OFF_I, 512, S["pe_V"])
                gram(t, 2)
                gram(t, 3)
                scores(t, 0)
                token_projection(P3, OFF_G, 512, S["pe_G"])
                gram(t, 4)
                gram(t, 5)
                scores(t, 1)
                gram(t, 6)
                gram(t, 7)
                state_products(t)
                readout(t)
                for n in range(4):
                    p_transposes(t, n)
                values(t)
                mix_transposes(t)

        @block.scalar
        def _(act):
            def norm(t):
                act.wait_ge(x_in, 16 * t + 16)
                if not isinstance(t, int):
                    act.wait_ge(S["pe_xT"], t)
                act.activation(xn[:], xs[:], ACT.Square, accum_out=ss[:, 0:1])
                act.drain()
                act.activation(ss[:, 1:2], ss[:, 0:1], ACT.Ln, bias=EPS, scale=1.0 / DM)
                act.drain()
                act.activation(ss[:, 2:3], ss[:, 1:2], ACT.Exp, scale=-0.5).then_inc(S["r_ready"], 1)
                act.wait_ge(S["pe_xT"], t + 1)
                act.activation(xT[:, 0:4, :], bank4(T0), ACT.Copy)
                act.activation(xT[:, 4:8, :], bank4(T1), ACT.Copy).then_inc(S["xT_ready"], 1)
                act.drain()

            def features(t):
                act.wait_ge(S["pe_F"], t + 1)
                act.activation(ef[:], bank4(P0), ACT.Exp, scale=-1.0).then_inc(S["ef_ready"], 1)
                act.wait_ge(S["pe_Q"], t + 1)
                act.activation(eb[:], bank4(P1), ACT.Exp, scale=-1.0).then_inc(S["eq_ready"], 1)
                act.wait_ge(S["f_ready"], t + 1)
                act.activation(ef[:], ff[:], ACT.Ln).then_inc(S["lf_ready"], 1)
                act.drain()

            def decay(t):
                act.wait_ge(S["b_ready"], t)
                act.activation(eb[:], bb[:], ACT.Exp).then_inc(S["eb_ready"], 1)
                act.drain()

            def level_exp(t, g):
                act.wait_ge(S["D_ready"], LEVELS * (t - 1) + g + 1)
                act.activation(dd[:, g % 2], dd[:, g % 2], ACT.Exp).then_inc(S["E_ready"], 1)
                act.drain()

            def take_qk(t):
                act.wait_ge(S["pe_AQ"], t + 1)
                act.activation(qk[:, 0:4, :, :].rearrange("p j s c -> p s j c"),
                               P4[:].rearrange("p (s j c) -> p s j c", s=2, j=4), ACT.Copy)
                act.wait_ge(S["pe_AKV"], t + 1)
                act.activation(qk[:, 4, :, :].rearrange("p s c -> p (s c)"), P5[:, 0:128], ACT.Copy)
                act.activation(va[:, 1, :], P5[:, 128:256], ACT.Copy).then_inc(S["qk_ready"], 1)
                act.drain()

            def take_qkT(t):
                act.wait_ge(S["pe_qkT"], t + 1)
                act.activation(qT[:], bank4(T0), ACT.Copy)
                act.activation(kT[:, 1, :], T1[:, 0:P], ACT.Copy).then_inc(S["qkT_ready"], 1)
                act.drain()

            def take_v(t):
                act.wait_ge(S["pe_V"], t + 1)
                act.activation(vv[:], P2[:], ACT.Copy).then_inc(S["v_ready"], 1)
                act.drain()

            def gate_exp(t):
                act.wait_ge(S["pe_G"], t + 1)
                act.activation(gg[:, 0, :], P3[:], ACT.Exp, scale=-1.0).then_inc(S["eg_ready"], 1)
                act.drain()

            def end_decay(t):
                act.wait_ge(S["kd_ready"], t + 1)
                act.activation(dd[:, 1], dd[:, 1], ACT.Exp).then_inc(S["ke_exp"], 1)
                act.wait_ge(S["pe_KET"], t + 1)
                act.activation(ket[:], bank4(T0), ACT.Copy).then_inc(S["ket_ready"], 1)
                act.drain()

            def softmax(t):
                act.wait_ge(S["m_ready"], t)
                for h in range(SH):
                    act.activation(sm[:, h, :], sm[:, h, :], ACT.Exp, bias=mx[:, 2, h:h + 1], accum_out=mx[:, 3, h:h + 1])
                act.activation(mx[:, 4, :], mx[:, 4, :], ACT.Exp).then_inc(S["p_ready"], 1)
                act.drain()

            def readout_norm(t, n):
                act.wait_ge(S["pe_O"], t + 1)
                act.wait_ge(S["gg_ready"], t + 1)
                for h in range(HH):
                    act.activation(gg[0:n, 0, h * P:(h + 1) * P], P2[0:n, h * P:(h + 1) * P], ACT.Square,
                                   accum_out=rs[0:n, 0, h:h + 1])
                act.drain()
                act.activation(rs[0:n, 1, :], rs[0:n, 0, :], ACT.Ln, bias=EPS, scale=1.0 / DK)
                act.drain()
                act.activation(rs[0:n, 2, :], rs[0:n, 1, :], ACT.Exp, scale=-0.5).then_inc(S["rr_ready"], 1)
                act.drain()

            def take_pT(t, n):
                act.wait_ge(S["pe_PT"], 4 * (t - 1) + n + 1)
                act.activation(pT[:, 2 * n:2 * n + 2, :, :].rearrange("p h a c -> p (h a) c"),
                               bank4(T0 if n % 2 == 0 else T1), ACT.Copy).then_inc(S["pT_ready"], 1)
                act.drain()

            def take_mix(t):
                act.wait_ge(S["pe_mix"], t + 1)
                act.wait_ge(mix_out, 16 * t)
                act.activation(mixT[:, 0:4, :], bank4(T0), ACT.Copy)
                act.activation(mixT[:, 4:8, :], bank4(T1), ACT.Copy).then_inc(S["mixT_ready"], 1)
                act.drain()

            act.preload_act_table_set("natural_log_exp_and_others")
            act.wait_ge(c_in, 16 * NC_IN)
            act.wait_ge(S["lb_ready"], 1)
            act.activation(lbw[:, 0:2, :], lbw[:, 0:2, :], ACT.Exp).then_inc(S["lb_ready"], 1)
            norm(0)
            features(0)
            take_qk(0)
            take_qkT(0)
            take_v(0)
            gate_exp(0)
            end_decay(0)
            sampled_act(act, readout_norm)

            with act.Fori(1, NB + 1) as t:
                norm(t)
                features(t)
                decay(t)
                level_exp(t, 0)
                level_exp(t, 1)
                take_qk(t)
                level_exp(t, 2)
                take_qkT(t)
                level_exp(t, 3)
                take_v(t)
                level_exp(t, 4)
                gate_exp(t)
                level_exp(t, 5)
                level_exp(t, 6)
                softmax(t)
                end_decay(t)
                readout_norm(t, P)
                for n in range(4):
                    take_pT(t, n)
                take_mix(t)

        @block.vector
        def _(v):
            def norm(t):
                v.wait_ge(S["r_ready"], t + 1)
                v.scalar_tensor_tensor(out=xn[:], in0=xs[:], scalar=ss[:, 2:3], in1=gmix[:], op0=ALU.mult,
                                       op1=ALU.mult).then_inc(S["xn_ready"], 1)
                v.drain()

            def features(t):
                v.wait_ge(S["ef_ready"], t + 1)
                v.tensor_scalar(ff[:], ef[:], 1.0, None, ALU.add)
                v.drain()
                v.reciprocal(kk[:], ff[:])
                v.drain()
                for h in range(HH):
                    m = v.tensor_scalar(ff[:, h, :], kk[:, h, :], oml[:, h:h + 1], lb[:, h:h + 1], ALU.mult, ALU.add)
                m.then_inc(S["f_ready"], 1)
                v.wait_ge(S["eq_ready"], t + 1)
                v.tensor_scalar(qq[:], eb[:], 1.0, None, ALU.add)
                v.drain()
                v.tensor_scalar(kk[:], ff[:], -1.0, 1.0, ALU.mult, ALU.add)
                v.reciprocal(qb[:], qq[:])
                v.drain()
                v.tensor_tensor(qq[:], qb[:], bank4(P1), ALU.mult).then_inc(S["q_ready"], 1)
                v.drain()

            def cumulate(t):
                v.wait_ge(S["lf_ready"], t + 1)
                v.tensor_tensor_scan(bb[:].rearrange("p h c -> p (h c)"), reset[:].rearrange("p h c -> p (h c)"),
                                     ef[:].rearrange("p h c -> p (h c)"), 0.0, ALU.mult, ALU.add).then_inc(S["b_ready"], 1)
                v.drain()

            def halves(x, g):
                half = P >> (g + 1)
                y = x.rearrange("p h c -> p (h c)").rearrange("p (n a c) -> p n a c", a=2, c=half)
                return y[:, :, 0, :], y[:, :, 1, :], half

            def level_gap(t, g):
                bl, br, half = halves(bb[:], g)
                dl, dr, _ = halves(dd[:, g % 2], g)
                mid = bl[:, :, half - 1:half].broadcast_to([P, bl.shape[1], half])
                v.tensor_tensor(dl, mid, bl, ALU.subtract)
                v.tensor_tensor(dr, br, mid, ALU.subtract).then_inc(S["D_ready"], 1)
                v.drain()

            def level_operands(t, g):
                v.wait_ge(S["E_ready"], LEVELS * (t - 1) + g + 1)
                if g >= 2:
                    v.wait_ge(S["pe_gram"], GRAMS * (t - 1) + g - 1)
                el, er, _ = halves(dd[:, g % 2], g)
                kl, _, _ = halves(kk[:], g)
                _, qr, _ = halves(qq[:], g)
                ml, mr, _ = halves(mm[:, g % 2], g)
                v.tensor_tensor(ml, el, kl, ALU.mult)
                v.tensor_tensor(mr, er, qr, ALU.mult).then_inc(S["M_ready"], 1)
                v.drain()

            def level_take(t, g):
                v.wait_ge(S["pe_gram"], GRAMS * (t - 1) + g + 1)
                mask = lmask[:, g:g + 1, :].broadcast_to([P, HH, P])
                if g == 0:
                    v.tensor_tensor(at[:], bank4(GB[0]), mask, ALU.mult).then_inc(S["A_ready"], 1)
                else:
                    standalone(v, idle)
                    v.copy_predicated(at[:], mask, bank4(GB[g % 2])).then_inc(S["A_ready"], 1)
                v.drain()

            def rotate(t):
                v.wait_ge(S["qk_ready"], t + 1)
                v.wait_ge(side_in, 32 * t + 32)
                x = qk[:].rearrange("p j s c -> p (j s) c")
                lo, hi = x[:, :, 0:32], x[:, :, 32:64]
                o = qkr[:].rearrange("p j s c -> p (j s) c")
                cos, sin = (rope[:, a:a + 1, :].broadcast_to([P, 10, 32]) for a in (0, 1))
                v.tensor_tensor(rt[:, 0, :, 0:32], lo, cos, ALU.mult)
                v.tensor_tensor(rt[:, 0, :, 32:64], hi, cos, ALU.mult)
                v.tensor_tensor(rt[:, 1, :, 0:32], hi, sin, ALU.mult)
                v.tensor_tensor(rt[:, 1, :, 32:64], lo, sin, ALU.mult)
                v.drain()
                v.tensor_tensor(o[:, :, 0:32], rt[:, 0, :, 0:32], rt[:, 1, :, 0:32], ALU.subtract)
                v.tensor_tensor(o[:, :, 32:64], rt[:, 0, :, 32:64], rt[:, 1, :, 32:64], ALU.add).then_inc(S["rot_ready"], 1)
                v.drain()

            def mask_scores(t, n):
                v.wait_ge(S["pe_S"], 2 * (t - 1) + n + 1)
                for s, b in enumerate((P4, P5)):
                    h = GQ * s + 2 * n
                    m = v.scalar_tensor_tensor(out=sm[:, h:h + 2, :], in0=b[:].rearrange("p (a c) -> p a c", a=2), scalar=SCALE,
                                               in1=wmask[:].rearrange("p (a c) -> p a c", a=1).broadcast_to([P, 2, 2 * WIN]),
                                               op0=ALU.mult, op1=ALU.add)
                m.then_inc(S["sm_ready"], 1)
                v.drain()

            def row_max(t):
                v.drain()
                v.tensor_reduce(mx[:, 0, :], sm[:], AX.X, ALU.max)
                v.drain()
                v.tensor_tensor(mx[:, 1, :], mx[:, 0, :], sinkb[:], ALU.max)
                v.drain()
                v.tensor_scalar(mx[:, 2, :], mx[:, 1, :], -1.0, None, ALU.mult)
                v.tensor_tensor(mx[:, 4, :], sinkb[:], mx[:, 1, :], ALU.subtract).then_inc(S["m_ready"], 1)
                v.drain()

            def end_gap(t):
                v.tensor_tensor(dd[:, 1], bb[:, :, P - 1:P].broadcast_to([P, HH, P]), bb[:], ALU.subtract).then_inc(S["kd_ready"], 1)
                v.drain()

            def query_decay(t):
                v.wait_ge(S["eb_ready"], t)
                v.tensor_tensor(qb[:], qq[:], eb[:], ALU.mult)
                v.drain()

            def end_keys(t):
                v.wait_ge(S["ke_exp"], t + 1)
                v.tensor_tensor(dd[:, 0], kk[:], dd[:, 1], ALU.mult).then_inc(S["ke_ready"], 1)
                v.drain()

            def gate(t):
                v.wait_ge(S["eg_ready"], t + 1)
                v.tensor_scalar(gg[:, 1, :], gg[:, 0, :], 1.0, None, ALU.add)
                v.drain()
                v.reciprocal(gg[:, 0, :], gg[:, 1, :])
                v.drain()
                v.tensor_tensor(gg[:, 1, :], gg[:, 0, :], P3[:], ALU.mult)
                v.drain()
                v.tensor_tensor(gg[:, 1, :], gg[:, 1, :], gnorm[:], ALU.mult).then_inc(S["gg_ready"], 1)
                v.drain()

            def new_state(t):
                v.wait_ge(S["pe_dS"], t + 1)
                v.wait_ge(S["pe_O"], t + 1)
                for h in range(HH):
                    m = v.scalar_tensor_tensor(out=st[:, h, :], in0=st[:, h, :], scalar=eb[:, h, P - 1:P],
                                               in1=P3[:, h * P:(h + 1) * P], op0=ALU.mult, op1=ALU.add)
                m.then_inc(S["st_ready"], 1)
                v.drain()

            def mix_a(t, n):
                v.wait_ge(S["rr_ready"], t + 1)
                for h in range(HH):
                    m = v.scalar_tensor_tensor(out=mixh[0:n, h * P:(h + 1) * P], in0=P2[0:n, h * P:(h + 1) * P],
                                               scalar=rs[0:n, 2, h:h + 1], in1=gg[0:n, 1, h * P:(h + 1) * P],
                                               op0=ALU.mult, op1=ALU.mult)
                m.then_inc(S["mixh_ready"], 1)
                v.drain()

            def mix_b(t):
                v.wait_ge(S["p_ready"], t)
                v.tensor_tensor(mx[:, 5, :], mx[:, 3, :], mx[:, 4, :], ALU.add)
                v.drain()
                v.reciprocal(mx[:, 0, :], mx[:, 5, :])
                v.drain()
                v.wait_ge(S["pe_Oa"], t)
                v.tensor_tensor(mixa[:].rearrange("p (h c) -> p h c", h=SH), P0[:].rearrange("p (h c) -> p h c", h=SH),
                                mx[:, 0, :].rearrange("p (h c) -> p h c", c=1).broadcast_to([P, SH, HD]), ALU.mult).then_inc(S["mixa_ready"], 1)
                v.tensor_copy(kT[:, 0, :], kT[:, 1, :])
                v.tensor_copy(va[:, 0, :], va[:, 1, :])
                v.drain()

            v.wait_ge(c_in, 16 * NC_IN)
            v.tensor_tensor(lbw[:, 2, :], lbl[:, 0, :], lbl[:, 1, :], ALU.max)
            v.drain()
            v.tensor_tensor(lbw[:, 0:2, :], lbl[:], lbw[:, 2:3, :].broadcast_to([P, 2, HH]), ALU.subtract).then_inc(S["lb_ready"], 1)
            v.wait_ge(S["lb_ready"], 2)
            v.tensor_tensor(lbw[:, 1, :], lbw[:, 0, :], lbw[:, 1, :], ALU.add)
            v.drain()
            v.reciprocal(lbw[:, 3, :], lbw[:, 1, :])
            v.drain()
            v.tensor_tensor(lb, lbw[:, 0, :], lbw[:, 3, :], ALU.mult)
            v.drain()
            v.tensor_scalar(oml, lb, -1.0, 1.0, ALU.mult, ALU.add)
            norm(0)
            features(0)
            v.wait_ge(S["lf_ready"], 1)
            v.memset(bb[:], 0.0)
            v.memset(ef[:, :, 0:P - META], 0.0)
            v.drain()
            v.tensor_tensor_scan(bb[:].rearrange("p h c -> p (h c)"), reset[:].rearrange("p h c -> p (h c)"),
                                 ef[:].rearrange("p h c -> p (h c)"), 0.0, ALU.mult, ALU.add)
            v.drain()
            end_gap(0)
            rotate(0)
            v.wait_ge(S["ke_exp"], 1)
            v.memset(dd[:, 0, :, 0:P - META], 0.0)
            v.tensor_tensor(dd[:, 0, :, P - META:P], kk[:, :, P - META:P], dd[:, 1, :, P - META:P], ALU.mult).then_inc(S["ke_ready"], 1)
            gate(0)
            v.wait_ge(S["pe_dS"], 1)
            v.tensor_copy(st[:], bank4(P3)).then_inc(S["st_ready"], 1)
            v.wait_ge(S["qkT_ready"], 1)
            v.tensor_copy(kT[:, 0, :], kT[:, 1, :])
            v.tensor_copy(va[:, 0, :], va[:, 1, :])
            sampled_vector(v, mix_a)

            with v.Fori(1, NB + 1) as t:
                norm(t)
                features(t)
                cumulate(t)
                level_gap(t, 0)
                level_gap(t, 1)
                level_operands(t, 0)
                level_gap(t, 2)
                level_operands(t, 1)
                rotate(t)
                level_take(t, 0)
                level_gap(t, 3)
                level_operands(t, 2)
                level_take(t, 1)
                level_gap(t, 4)
                level_operands(t, 3)
                level_take(t, 2)
                mask_scores(t, 0)
                level_gap(t, 5)
                level_operands(t, 4)
                level_take(t, 3)
                level_gap(t, 6)
                level_operands(t, 5)
                gate(t)
                level_take(t, 4)
                mask_scores(t, 1)
                level_operands(t, 6)
                level_take(t, 5)
                row_max(t)
                end_gap(t)
                query_decay(t)
                level_take(t, 6)
                level_take(t, 7)
                end_keys(t)
                new_state(t)
                mix_a(t, P)
                mix_b(t)


def peer_program(nc, io):
    with ExitStack() as ctx:
        def sb(name, shape, dt=F32):
            return ctx.enter_context(nc.sbuf_tensor("b_" + name, shape, dt))

        def sem(name):
            return ctx.enter_context(nc.semaphore("b_" + name))

        def bank(name, n=1):
            return ctx.enter_context(nc.psum_tensor("b_" + name, [P, 512 * n], F32))

        w_out = sb("w_out", [P, KT, DM])
        wk = sb("wk", [P, KT, 2 * PH * NKEY])
        ring = sb("ring", [P, RING, 2 * DM])
        ident = sb("ident", [P, P])
        gffn = sb("gffn", [P, DM])
        gfin = sb("gfin", [P, DM])
        mixT = sb("mixT", [P, KT, P])
        hn = sb("hn", [P, DM])
        xbn = sb("xbn", [P, DM])
        xbT = sb("xbT", [P, KT, P])
        xbc = sb("xbc", [P, DM])
        yo = sb("yo", [P, DM])
        diag = sb("diag", [P, DIAGS, P])
        dots = sb("dots", [P, 2, TOPK])
        ge = sb("ge", [P, 2, TOPK])
        wt = sb("wt", [P, 2, TOPK])
        nrm = sb("nrm", [P, 6])
        tops = sb("tops", [P, 2, TOPK])
        topi = sb("topi", [P, 2, TOPK], U32)
        topf = sb("topf", [P, 2, TOPK])
        rest = sb("rest", [P, 256])
        cand = sb("cand", [P, TOPK, TOPK])
        bc = sb("bc", [P, TOPK], U32)
        ab = sb("ab", [P, 2, TOPK], U32)
        hot = sb("hot", [P, 2, TOPK, TOPK])
        pick = sb("pick", [P, 2, TOPK])
        iota = sb("iota", [P, TOPK])
        best = sb("best", [P, PH, TOPK])
        idx = sb("idx", [P, PH, TOPK], U32)
        gate = sb("gate", [P, PH, TOPK])
        gsum = sb("gsum", [P, 2, PH])
        icur = sb("icur", [P, 2, TOPK], U32)
        gcur = sb("gcur", [P, 2, TOPK])
        sel = sb("sel", [NS, NS, P])

        ab_T = icur[:].rearrange("p a c -> p (a c)")[:, 0:NS]
        gate_T = gcur[:].rearrange("p a c -> p (a c)")[:, 0:NS]
        wd = hot[:].rearrange("p a b c -> p (a b c)")[:, 0:NS * NS]

        Y, O = bank("Y", 2), bank("O", 2)
        SC = [bank("SA"), bank("SB")]

        c_in, w_in, k_in = sem("c_in"), sem("w_in"), [sem(f"k_in{a}") for a in range(2)]
        prep_in, y_out = sem("prep_in"), sem("y_out")
        g_in = [sem(f"g_in{r}") for r in range(RING)]
        names = ("pe_wk wk_taken pe_op h_ready r_ready xb_ready pe_xbT xbT_ready pe_sc top_done idx_ready gate_ready "
                 "dot_done diag_ready slot_free pe_res y_free gd_ready ge_ready fr_ready y_ready xbc_ready "
                 "yo_free iT_ready pe_iT last_idx pe_xb last_dot last_ge last_w idle").split()
        S = {n: sem(n) for n in names}
        idle = S["idle"]
        NC_IN = 5
        PART = 32
        STEPS = SLOTS // PART

        block = ctx.enter_context(nc.Block())

        @block.sync
        def _(sp):
            sp.dma_start(ring[:, RING - 1, :], io["keys_T"]).then_inc(c_in, 16)
            for dst, src in ((ident[:], io["ident"]), (gffn[:], io["norm_ffn"].broadcast_to([P, DM])),
                             (gfin[:], io["norm_final"].broadcast_to([P, DM])), (sel[:], io["sel"].rearrange("p (b c) -> p b c", b=NS))):
                sp.dma_start(dst, src).then_inc(c_in, 16)
            for a in range(2):
                sp.dma_start(ring[:, a, 0:DM], io["wq_T"][a * P:(a + 1) * P, :]).then_inc(k_in[a], 16)
            with sp.Fori(1, PH) as h:
                for a in range(2):
                    sp.wait_ge(S["pe_wk"], 2 * h + a - 1)
                    sp.dma_start(ring[:, a, 0:DM], io["wq_T"][bass.ds((h * 2 + a) * P, P), :]).then_inc(k_in[a], 16)
            sp.dma_start(w_out[:], io["w_out"].rearrange("(k p) n -> p k n", p=P)).then_inc(w_in, 16)

            def prepare(n):
                if not isinstance(n, int):
                    sp.wait_ge(S["pe_op"], n)
                sp.dma_start(mixT[:], io["mix_scratch"][bass.ds(n, 1)].rearrange("a p k c -> (a p) k c")).then_inc(prep_in, 16)
                if not isinstance(n, int):
                    sp.wait_ge(S["pe_res"], n)
                sp.dma_start(hn[:], io["x_all"][bass.ds((n + 1) * P, P), :]).then_inc(prep_in, 16)

            prepare(0)
            with sp.Fori(0, NB) as c:
                prepare(c + 1)
                sp.wait_ge(S["y_ready"], c + 1)
                sp.dma_start(io["y_p"][bass.ds(c * P, P), :], yo[:]).then_inc(y_out, 16)
                sp.wait_ge(y_out, 16 * c + 16)
                sp.sem_inc(S["yo_free"], 1)
            sp.wait_ge(S["y_ready"], NB + 1)
            sp.dma_start(io["y_s"], yo[0:NS, :]).then_inc(y_out, 16)
            sp.wait_ge(y_out, 16 * (NB + 1))

        @block.gpsimd
        def _(pool):
            def gather(j, q):
                p, r = q // TOPK, q % RING
                if q % TOPK == 0:
                    pool.wait_ge(S["idx_ready"], 2 * j + p + 1)
                pool.wait_ge(S["slot_free"], PART * j + q + 1)
                standalone(pool, idle)
                pool.indirect_dma_start(ring[:, r, :], None, io["uv"],
                                        bass.IndirectOffsetOnAxis(ap=icur[:, p, q % TOPK:q % TOPK + 1], axis=0),
                                        bounds_check=NEXP - 1, oob_is_err=False).then_inc(g_in[r], 16)

            pool.iota(iota[:], [[1, TOPK]], base=0, channel_multiplier=0,
                      allow_small_or_imprecise_dtypes=True).then_inc(S["iT_ready"], 1)
            with pool.Fori(0, NB * STEPS) as j:
                for q in range(PART):
                    gather(j, q)
            pool.wait_ge(S["last_idx"], 1)
            pool.wait_ge(S["slot_free"], RING + NB * SLOTS)
            for b in range(NS):
                pool.indirect_dma_start(ring[:, b, :], None, io["uv"],
                                        bass.IndirectOffsetOnAxis(ap=ab_T[:, b:b + 1], axis=0),
                                        bounds_check=NEXP - 1, oob_is_err=False).then_inc(g_in[b], 16)

        @block.tensor
        def _(pe):
            def key_weights(h, a):
                pe.wait_ge(k_in[a], 16 * h)
                pe.wait_ge(S["wk_taken"], 2 * h + a - 1)
                for k in range(KT):
                    m = pe.matmul((O, Y)[a][:, k * P:(k + 1) * P], ring[:, a, k * P:(k + 1) * P],
                                  ring[:, RING - 1, bass.ds((h * 2 + (a - 2)) * P, P)], start=True, stop=True)
                m.then_inc(S["pe_wk"], 1)

            def out_projection(k):
                for a in range(2):
                    m = pe.matmul(O[:, a * 512:(a + 1) * 512], mixT[:, k, :], w_out[:, k, a * 512:(a + 1) * 512],
                                  start=(k == 0), stop=(k == KT - 1))
                if k == KT - 1:
                    m.then_inc(S["pe_op"], 1)

            def x_transposes(n):
                pe.wait_ge(S["xb_ready"], n + 1)
                for k in range(KT):
                    m = pe.transpose(O[:, k * P:(k + 1) * P], xbn[:, k * P:(k + 1) * P], ident[:])
                m.then_inc(S["pe_xbT"], 1)

            def scores(n, h, s):
                pe.wait_ge(S["xbT_ready"], n + 1)
                pe.wait_ge(S["top_done"], n * PH + h + 1)
                for k in range(KT):
                    m = pe.matmul(SC[s][:, 0:2 * NKEY], xbT[:, k, :], wk[:, k, bass.ds(h * 2 * NKEY, 2 * NKEY)],
                                  start=(k == 0), stop=(k == KT - 1))
                m.then_inc(S["pe_sc"], 1)

            def residual(c):
                pe.wait_ge(S["xb_ready"], c + 1)
                pe.wait_ge(S["y_free"], c + 1)
                for a in range(2):
                    m = pe.matmul(Y[:, a * 512:(a + 1) * 512], ident[:], hn[:, a * 512:(a + 1) * 512], start=True, stop=False,
                                  skip_group_check=True)
                m.then_inc(S["pe_res"], 1)

            def apply(j, q):
                pe.wait_ge(S["diag_ready"], PART * j + q + 1)
                for a in range(2):
                    m = pe.matmul(Y[:, a * 512:(a + 1) * 512], diag[:, q % DIAGS, :], ring[:, q % RING, DM + a * 512:DM + (a + 1) * 512],
                                  start=False, stop=False, skip_group_check=True)
                m.then_inc(S["slot_free"], 1)

            pe.sem_inc(S["slot_free"], RING)
            pe.sem_inc(S["y_free"], 1)
            pe.sem_inc(S["top_done"], 2)
            pe.wait_ge(c_in, 16 * NC_IN)
            pe.sem_inc(S["wk_taken"], 2)
            with pe.Fori(1, PH + 1) as h:
                for a in range(2):
                    key_weights(h, a)
            pe.wait_ge(w_in, 16)
            pe.wait_ge(prep_in, 32)
            pe.wait_ge(S["wk_taken"], 2 + 2 * PH)
            for k in range(KT):
                out_projection(k)
            x_transposes(0)
            with pe.Fori(0, PH // 2) as j:
                scores(0, 2 * j, 0)
                scores(0, 2 * j + 1, 1)

            with pe.Fori(0, NB) as c:
                residual(c)
                for q in range(PART):
                    if q == 0:
                        pe.wait_ge(prep_in, 32 * c + 64)
                    if 1 <= q <= KT:
                        out_projection(q - 1)
                    if q == 15:
                        x_transposes(c + 1)
                    if q == 18:
                        scores(c + 1, 0, 0)
                    if q == 26:
                        scores(c + 1, 1, 1)
                    apply(c * STEPS, q)
                with pe.Fori(1, STEPS) as j:
                    for q in range(PART):
                        if q == 2:
                            scores(c + 1, 2 * j, 0)
                        if q == 18:
                            scores(c + 1, 2 * j + 1, 1)
                        apply(c * STEPS + j, q)

            pe.wait_ge(S["iT_ready"], 2)
            pe.transpose(SC[0][:, 0:NS], rest[0:NS, 0:P], ident[0:NS, 0:NS])
            pe.transpose(SC[0][:, NS:2 * NS], gate[0:NS].rearrange("p h c -> p (h c)"), ident[0:NS, 0:NS]).then_inc(S["pe_iT"], 1)
            pe.wait_ge(S["y_free"], NB + 1)
            for a in range(2):
                pe.matmul(Y[0:NS, a * 512:(a + 1) * 512], ident[0:NS, 0:NS], hn[0:NS, a * 512:(a + 1) * 512], start=True, stop=False,
                          skip_group_check=True)
            for b in range(NS):
                if b >= 1:
                    pe.wait_ge(S["last_dot"], b)
                for a in range(2):
                    m = pe.matmul(O[:, a * 512:(a + 1) * 512], sel[:, b, :], xbn[0:NS, a * 512:(a + 1) * 512], start=True, stop=True)
                m.then_inc(S["pe_xb"], 1)
            pe.wait_ge(S["last_w"], 1)
            for b in range(NS):
                for a in range(2):
                    m = pe.matmul(Y[0:NS, a * 512:(a + 1) * 512], wd[:, b * NS:(b + 1) * NS], ring[:, b, DM + a * 512:DM + (a + 1) * 512],
                                  start=False, stop=(b == NS - 1), skip_group_check=True)
            m.then_inc(S["slot_free"], 1)

        @block.scalar
        def _(act):
            def norm(n):
                act.wait_ge(S["h_ready"], n + 1)
                act.wait_ge(S["xbc_ready"], n + 1)
                act.activation(xbn[:], hn[:], ACT.Square, accum_out=nrm[:, 0:1])
                act.drain()
                act.preload_act_table_set("natural_log_exp_and_others")
                act.activation(nrm[:, 1:2], nrm[:, 0:1], ACT.Ln, bias=EPS, scale=1.0 / DM)
                act.drain()
                act.activation(nrm[:, 2:3], nrm[:, 1:2], ACT.Exp, scale=-0.5).then_inc(S["r_ready"], 1)

            def take_xbT(n):
                act.wait_ge(S["pe_xbT"], n + 1)
                act.activation(xbT[:].rearrange("p k c -> p (k c)"), O[:], ACT.Copy).then_inc(S["xbT_ready"], 1)

            def weigh(j, q):
                p, k = q // TOPK, q % TOPK
                if k == 0:
                    act.wait_ge(S["gate_ready"], 2 * j + p + 1)
                act.wait_ge(S["dot_done"], PART * j + q + 1)
                act.activation(ge[:, p, k:k + 1], dots[:, p, k:k + 1], ACT.Gelu)
                act.drain()
                act.activation(wt[:, p, k:k + 1], ge[:, p, k:k + 1], ACT.Copy, scale=gcur[:, p, k:k + 1])
                act.drain()
                act.wait_ge(S["slot_free"], PART * j + q + 1 + RING - DIAGS)
                act.activation(diag[:, q % DIAGS, :], ident[:], ACT.Copy, scale=wt[:, p, k:k + 1]).then_inc(S["diag_ready"], 1)

            def gate_exp(n):
                act.preload_act_table_set("natural_log_exp_and_others")
                act.wait_ge(S["gd_ready"], n + 1)
                act.activation(gate[:], gate[:], ACT.Exp).then_inc(S["ge_ready"], 1)

            def final_norm(c, n):
                if isinstance(c, int):
                    act.wait_ge(S["slot_free"], SLOTS * NB + RING + 1)
                else:
                    act.wait_ge(S["slot_free"], SLOTS * c + SLOTS + RING)
                act.wait_ge(S["yo_free"], c + 1)
                act.activation(yo[0:n, :], Y[0:n, :], ACT.Square, accum_out=nrm[0:n, 3:4])
                act.drain()
                act.preload_act_table_set("natural_log_exp_and_others")
                act.activation(nrm[0:n, 4:5], nrm[0:n, 3:4], ACT.Ln, bias=EPS, scale=1.0 / DM)
                act.drain()
                act.activation(nrm[0:n, 5:6], nrm[0:n, 4:5], ACT.Exp, scale=-0.5).then_inc(S["fr_ready"], 1)

            act.sem_inc(S["yo_free"], 1)
            with act.Fori(1, PH + 1) as h:
                for a in range(2):
                    act.wait_ge(S["pe_wk"], 2 * h + a - 1)
                    act.activation(wk[:, :, bass.ds((h * 2 + (a - 2)) * P, P)], (O, Y)[a][:].rearrange("p (k c) -> p k c", k=KT),
                                   ACT.Copy).then_inc(S["wk_taken"], 1)
            norm(0)
            take_xbT(0)
            gate_exp(0)
            with act.Fori(0, NB) as c:
                for q in range(PART):
                    if q == 11:
                        norm(c + 1)
                    if q == 17:
                        take_xbT(c + 1)
                    weigh(c * STEPS, q)
                with act.Fori(1, STEPS) as j:
                    for q in range(PART):
                        weigh(c * STEPS + j, q)
                gate_exp(c + 1)
                final_norm(c, P)
            act.wait_ge(S["last_dot"], NS)
            act.activation(ge[:, 0, 0:NS], dots[:, 0, 0:NS], ACT.Gelu).then_inc(S["last_ge"], 1)
            final_norm(NB, NS)

        @block.vector
        def _(v):
            def add_residual(n):
                v.wait_ge(prep_in, 32 * n + 32)
                v.wait_ge(S["pe_op"], n + 1)
                v.tensor_tensor(hn[:], hn[:], O[:], ALU.add).then_inc(S["h_ready"], 1)

            def norm(n):
                v.wait_ge(S["r_ready"], n + 1)
                v.scalar_tensor_tensor(out=xbn[:], in0=hn[:], scalar=nrm[:, 2:3], in1=gffn[:], op0=ALU.mult,
                                       op1=ALU.mult).then_inc(S["xb_ready"], 1)

            def top16(vals, nums, src, width):
                tmp = rest[:, 0:width]
                v.max(vals[:, 0:8], src)
                v.drain()
                v.max_index(nums[:, 0:8], vals[:, 0:8], src)
                v.match_replace(tmp, vals[:, 0:8], src, LOW)
                v.drain()
                v.max(vals[:, 8:16], tmp)
                v.drain()
                v.max_index(nums[:, 8:16], vals[:, 8:16], tmp)
                v.drain()

            def choose(n, h, s):
                v.wait_ge(S["pe_sc"], n * PH + h + 1)
                standalone(v, idle)
                for p in range(2):
                    top16(tops[:, p, :], topi[:, p, :], SC[s][:, p * NKEY:(p + 1) * NKEY], NKEY)
                v.tensor_copy(topf[:], topi[:]).then_inc(S["top_done"], 1)
                a0 = tops[:, 0, :].rearrange("p (a b) -> p a b", b=1).broadcast_to([P, TOPK, TOPK])
                v.tensor_tensor(cand[:], a0, tops[:, 1:2, :].broadcast_to([P, TOPK, TOPK]), ALU.add)
                v.drain()
                b16 = pick[:, 0, :]
                top16(b16, bc[:], cand[:].rearrange("p a b -> p (a b)"), TOPK * TOPK)
                v.tensor_copy(best[:, bass.ds(h, 1), :], pick[:, 0:1, :])
                v.tensor_scalar(ab[:, 0, :], bc[:], 4, None, ALU.logical_shift_right)
                v.tensor_scalar(ab[:, 1, :], bc[:], TOPK - 1, None, ALU.bitwise_and)
                v.drain()
                full = [P, 2, TOPK, TOPK]
                v.tensor_tensor(hot[:], ab[:].rearrange("p a (k i) -> p a k i", i=1).broadcast_to(full),
                                iota[:].rearrange("p (a k i) -> p a k i", a=1, k=1).broadcast_to(full), ALU.is_equal)
                v.drain()
                v.tensor_tensor(hot[:], hot[:], topf[:].rearrange("p a (k i) -> p a k i", k=1).broadcast_to(full), ALU.mult)
                v.drain()
                v.tensor_reduce(pick[:], hot[:], AX.X, ALU.add)
                v.drain()
                v.scalar_tensor_tensor(out=idx[:, bass.ds(h, 1), :], in0=pick[:, 0:1, :], scalar=float(NKEY), in1=pick[:, 1:2, :],
                                       op0=ALU.mult, op1=ALU.add)
                v.drain()

            def gates(n):
                v.tensor_tensor(gate[:], best[:], best[:, :, 0:1].broadcast_to([P, PH, TOPK]), ALU.subtract).then_inc(S["gd_ready"], 1)
                v.wait_ge(S["ge_ready"], n + 1)
                v.tensor_reduce(gsum[:, 0, :], gate[:], AX.X, ALU.add)
                v.drain()
                v.reciprocal(gsum[:, 1, :], gsum[:, 0, :])
                v.drain()
                v.tensor_tensor(gate[:], gate[:], gsum[:, 1, :].rearrange("p (h c) -> p h c", c=1).broadcast_to([P, PH, TOPK]), ALU.mult)
                v.drain()

            def next_indices(h, p):
                v.tensor_copy(icur[:, p:p + 1, :], idx[:, bass.ds(h, 1), :]).then_inc(S["idx_ready"], 1)

            def next_gates(h, p):
                v.tensor_copy(gcur[:, p:p + 1, :], gate[:, bass.ds(h, 1), :]).then_inc(S["gate_ready"], 1)

            def dot(j, q):
                r = q % RING
                v.wait_ge(g_in[r], (PART // RING * j + q // RING + 1) * 16)
                v.tensor_tensor_reduce(ring[:, r, 0:DM], ring[:, r, 0:DM], xbc[:], 1.0, 0.0, ALU.mult, ALU.add,
                                       dots[:, q // TOPK, q % TOPK:q % TOPK + 1]).then_inc(S["dot_done"], 1)

            def final_scale(c, n):
                v.wait_ge(S["fr_ready"], c + 1)
                v.scalar_tensor_tensor(out=yo[0:n, :], in0=Y[0:n, :], scalar=nrm[0:n, 5:6], in1=gfin[0:n, :], op0=ALU.mult,
                                       op1=ALU.mult).then_inc(S["y_ready"], 1)
                v.drain()
                v.tensor_copy(gsum[:, 0, :], gsum[:, 1, :]).then_inc(S["y_free"], 1)

            v.wait_ge(c_in, 16 * NC_IN)
            v.wait_ge(S["iT_ready"], 1)
            v.tensor_copy(gsum[:, 0, :], ident[:, 0:PH]).then_inc(S["xbc_ready"], 1)
            add_residual(0)
            norm(0)
            with v.Fori(0, PH // 2) as j:
                for s in range(2):
                    choose(0, 2 * j + s, s)
            gates(0)
            next_indices(0, 0)

            with v.Fori(0, NB) as c:
                v.drain()
                v.tensor_copy(xbc[:], xbn[:]).then_inc(S["xbc_ready"], 1)
                next_indices(1, 1)
                next_gates(0, 0)
                v.drain()
                for q in range(PART):
                    if q == 16:
                        next_indices(2, 0)
                        next_gates(1, 1)
                        v.drain()
                    dot(c * STEPS, q)
                    if q == 9:
                        add_residual(c + 1)
                    if q == 12:
                        norm(c + 1)
                    if q == 23:
                        choose(c + 1, 0, 0)
                choose(c + 1, 1, 1)
                with v.Fori(1, STEPS) as j:
                    for q in range(PART):
                        if q == 0:
                            next_indices(2 * j + 1, 1)
                            next_gates(2 * j, 0)
                            v.drain()
                        if q == 16:
                            next_indices((2 * j + 2) % PH, 0)
                            next_gates(2 * j + 1, 1)
                            v.drain()
                        dot(c * STEPS + j, q)
                        if q == 15:
                            choose(c + 1, 2 * j, 0)
                    choose(c + 1, 2 * j + 1, 1)
                gates(c + 1)
                final_scale(c, P)

            v.tensor_copy(rest[0:NS, 0:P], idx[0:NS].rearrange("p h c -> p (h c)")).then_inc(S["iT_ready"], 1)
            v.memset(wd, 0.0)
            v.wait_ge(S["pe_iT"], 1)
            v.tensor_copy(ab_T, SC[0][:, 0:NS])
            v.drain()
            v.tensor_copy(gate_T, SC[0][:, NS:2 * NS]).then_inc(S["last_idx"], 1)
            for b in range(NS):
                v.wait_ge(g_in[b], 16 * (NB * SLOTS // RING + 1))
                v.wait_ge(S["pe_xb"], b + 1)
                v.tensor_tensor_reduce(ring[:, b, 0:DM], ring[:, b, 0:DM], O[:], 1.0, 0.0, ALU.mult, ALU.add,
                                       dots[:, 0, b:b + 1]).then_inc(S["last_dot"], 1)
            v.wait_ge(S["last_ge"], 1)
            v.tensor_tensor(wd[:, 0:NS * NS:NS + 1], ge[:, 0, 0:NS], gate_T, ALU.mult).then_inc(S["last_w"], 1)
            final_scale(NB, NS)


def constants():
    tok = np.arange(P)
    masks = []
    for g in range(LEVELS):
        half = P >> (g + 1)
        same = (tok[:, None] // (2 * half)) == (tok[None, :] // (2 * half))
        masks.append(same & (tok[:, None] % (2 * half) < half) & (tok[None, :] % (2 * half) >= half))
    masks.append(tok[:, None] == tok[None, :])
    inv = np.float32(10000.0) ** (-np.arange(HD // 2, dtype=np.float32) * np.float32(2.0) / np.float32(HD))
    pos = np.arange((NB + 1) * P) - (P - META)
    pos[:NS] = 2048
    ang = pos.astype(np.float32)[:, None] * inv.astype(np.float32)[None, :]
    key, far = np.arange(2 * WIN)[None, :], -1.0e30
    wmask = np.zeros((NB, P, 2 * WIN), np.float32)
    wmask[:] = np.where((key <= tok[:, None] + WIN) & (key >= tok[:, None]), 0.0, far)
    wmask[0, :, 0:P - META] = far
    sel = np.zeros((NS, NS, P), np.float32)
    sel[np.arange(NS), np.arange(NS)] = 1.0
    reset = np.ones((P, HH, P), np.float32)
    reset[:, :, 0] = 0.0
    return {
        "ident": np.eye(P, dtype=np.float32),
        "level_masks": np.concatenate([m.astype(np.int32) for m in masks], axis=1),
        "rope": np.concatenate([np.cos(ang), np.sin(ang)], axis=1).astype(np.float32),
        "wmask": wmask.reshape(NB * P, 2 * WIN),
        "sel": sel.reshape(NS, NS * P),
        "reset": reset.reshape(P, HW),
    }


def lay_out(x_prompt, x_sample, state_hgrn, cache_k, cache_v, meta_tokens, lb_logits, norm_mix, w_in,
            hgrn_norm, attn_sink, w_out, norm_ffn, peer_wq, peer_keys, peer_u, peer_v, norm_final):
    a = {k: np.asarray(v) for k, v in locals().items()}
    tile0 = np.zeros((P, DM), np.float32)
    tile0[:NS] = a["x_sample"].reshape(NS, DM)
    sampled = tile0.copy()
    tile0[P - META:] = a["meta_tokens"]
    return {
        "x_all": np.concatenate([tile0, a["x_prompt"].reshape(NB * P, DM), sampled]),
        "state_s": a["state_hgrn"].reshape(NS * HH, DK, DK),
        "cache_k": a["cache_k"].reshape(NS, WIN, KV * HD),
        "cache_v": a["cache_v"].reshape(NS, WIN, KV * HD),
        "lb_logits": a["lb_logits"].reshape(2, HW),
        "norm_mix": a["norm_mix"].reshape(1, DM),
        "w_in": a["w_in"].reshape(DM, IN_W),
        "hgrn_norm": a["hgrn_norm"].reshape(1, HW),
        "attn_sink": a["attn_sink"].reshape(1, SH),
        "w_out": a["w_out"].reshape(DM, DM),
        "norm_ffn": a["norm_ffn"].reshape(1, DM),
        "wq_T": np.ascontiguousarray(a["peer_wq"].reshape(DM, 2 * PH * NKEY).T),
        "keys_T": np.ascontiguousarray(a["peer_keys"].reshape(2 * PH, NKEY, P).transpose(2, 0, 1).reshape(P, 2 * PH * NKEY)),
        "uv": np.concatenate([a["peer_u"].reshape(NEXP, DM), a["peer_v"].reshape(NEXP, DM)], axis=1),
        "norm_final": a["norm_final"].reshape(1, DM),
        **constants(),
    }


OUTS = {
    "y_p": (NB * P, DM), "y_s": (NS, DM), "new_state_p": (HH, DK, DK), "new_k_p": (WIN, KV * HD), "new_v_p": (WIN, KV * HD),
    "new_state_s": (NS * HH, DK, DK), "new_k_s": (NS, WIN, KV * HD), "new_v_s": (NS, WIN, KV * HD),
}


def program(nc, arrays, debug=False):
    io = {n: nc.dram_tensor(n, a.shape, mybir.dt.from_np(a.dtype), kind="ExternalInput").ap() for n, a in arrays.items()}
    io |= {n: nc.dram_tensor(n, s, F32, kind="ExternalOutput").ap() for n, s in OUTS.items()}
    scratch = {"kind": "ExternalOutput"} if debug else {}
    io["mix_scratch"] = nc.dram_tensor("mix_scratch", [NB + 1, P, KT, P], F32, **scratch).ap()
    mixer_program(nc, io)
    peer_program(nc, io)


def kernel(**inputs):
    from concourse import bacc
    from concourse.bass_utils import run_bass_kernel_spmd

    arrays = lay_out(**inputs)
    nc = bacc.Bacc("TRN2", target_bir_lowering=False, num_devices=1)
    program(nc, arrays)
    r = run_bass_kernel_spmd(nc, [arrays], core_ids=[0]).results[0]
    return (r["y_p"].reshape(1, NB * P, DM), r["y_s"].reshape(NS, 1, DM),
            r["new_state_p"].reshape(1, 1, HH, DK, DK), r["new_k_p"].reshape(1, 1, WIN, KV, HD),
            r["new_v_p"].reshape(1, 1, WIN, KV, HD), r["new_state_s"].reshape(1, NS, HH, DK, DK),
            r["new_k_s"].reshape(1, NS, WIN, KV, HD), r["new_v_s"].reshape(1, NS, WIN, KV, HD))
```

```python
from contextlib import ExitStack

import numpy as np

import concourse.bass as bass
from concourse import mybir

F32 = mybir.dt.float32
U32 = mybir.dt.uint32
I32 = mybir.dt.int32
ALU = mybir.AluOpType
ACT = mybir.ActivationFunctionType
AX = mybir.AxisListType

P = 128
DM = 1024
KT = DM // P
NB = 8
META = 16
NS = 8
HH = 4
DK = 128
HW = HH * DK
SH = 8
KV = 2
HD = 64
GQ = SH // KV
WIN = 128
EPS = 1e-6
SCALE = HD ** -0.5
OFF_Q, OFF_F, OFF_I, OFF_G = 0, HW, 2 * HW, 3 * HW
OFF_AQ, OFF_AK = 4 * HW, 4 * HW + SH * HD
IN_W = OFF_AK + 2 * KV * HD
LEVELS = 7
GRAMS = LEVELS + 1
PH = 8
TOPK = 16
NKEY = 128
NEXP = NKEY * NKEY
SLOTS = PH * TOPK
RING = 8
DIAGS = 4
LOW = -3.0e38


def standalone(eng, idle):
    eng.sem_inc(idle, 1)


def mixer_program(nc, io):
    with ExitStack() as ctx:
        def sb(name, shape, dt=F32):
            return ctx.enter_context(nc.sbuf_tensor("a_" + name, shape, dt))

        def sem(name):
            return ctx.enter_context(nc.semaphore("a_" + name))

        def bank(name):
            return ctx.enter_context(nc.psum_tensor("a_" + name, [P, 512], F32))

        w_in = sb("w_in", [P, KT, IN_W])
        ident = sb("ident", [P, P])
        lmask = sb("lmask", [P, GRAMS, P], I32)
        reset = sb("reset", [P, HH, P])
        gmix = sb("gmix", [P, DM])
        gnorm = sb("gnorm", [P, HW])
        sinkb = sb("sinkb", [P, SH])
        sinkc = sb("sinkc", [SH, 1])
        lbl = sb("lbl", [P, 2, HH])
        lbw = sb("lbw", [P, 4, HH])
        lb, oml = lbw[:, 2, :], lbw[:, 3, :]
        xs = sb("xs", [P, DM])
        xn_all = sb("xn", [P, DM + NS])
        xn = xn_all[:, 0:DM]
        xT = sb("xT", [P, KT, P])
        ss = sb("ss", [P, 3])
        rope = sb("rope", [P, 2, HD // 2])
        wmask = sb("wmask", [P, 2 * WIN])
        ef = sb("ef", [P, HH, P])
        ff = sb("ff", [P, HH, P])
        kk = sb("kk", [P, HH, P])
        qq = sb("qq", [P, HH, P])
        bb = sb("bb", [P, HH, P])
        dd = sb("dd", [P, 2, HH, P])
        mm = sb("mm", [P, 2, HH, P])
        at = sb("at", [P, HH, P])
        eb = sb("eb", [P, HH, P])
        qb = sb("qb", [P, HH, P])
        ket = sb("ket", [P, HH, DK])
        st = sb("st", [P, HH, DK])
        vv = sb("vv", [P, HW])
        gg = sb("gg", [P, 2, HW])
        sjunk = sb("sjunk", [P, HW], mybir.dt.bfloat16)
        rs = sb("rs", [P, 3, HH])
        sq = sb("sq", [P, HH, P])
        qr = sb("qr", [P, HH, P])
        vr = sb("vr", [P, KV * HD])
        mixr = sb("mixr", [P, 2 * 10 * HD])
        mixh, mixa = mixr[:, 0:HW], mixr[:, HW:2 * HW]
        qk = sb("qk", [P, 5, 2, HD])
        rt = mixr[:].rearrange("p (a b c) -> p a b c", a=2, b=10)
        qkr = sb("qkr", [P, 5, 2, HD])
        qT = sb("qT", [P, 4, P])
        kT = sb("kT", [P, 2, WIN])
        va = sb("va", [P, 2, KV * HD])
        sm = sb("sm", [P, SH, 2 * WIN])
        pT = sb("pT", [P, SH, 2, P])
        mx = sb("mx", [P, 6, SH])
        mixT = sb("mixT", [P, KT, P])

        s0 = sb("s0", [P, NS * HH, DK])
        sel = mm[0:NS].rearrange("p a h c -> p (a h) c")
        qd = sb("qd", [P, HH, NS * NS])
        qbd = sb("qbd", [P, NS, SH])
        sx = sb("sx", [SH, 6, NS])
        rn = sb("rn", [NS, NS, SH])
        vnd = sb("vnd", [NS, KV, 2, HD])
        kc = pT[:, 0:4].rearrange("p h a c -> p (h a) c")
        kcT = pT[:, 4:8].rearrange("p h a c -> p (h a) c")
        v2 = sm[:].rearrange("p h c -> p (h c)").rearrange("p (b s r d) -> p b s r d", b=NS, s=KV, r=2)
        sc = xn_all[0:SH, :].rearrange("p (b c) -> p b c", b=NS)
        pTs = qb[:].rearrange("p h c -> p (h c)")[:, 0:NS * SH]

        T0, T1, FA, FB, G0, G1, S0, S1 = (bank(n) for n in ("T0", "T1", "FA", "FB", "G0", "G1", "S0", "S1"))
        OO, DS, OA = S0, S1, G1
        GB = [G0, G1]

        def bank4(b):
            return b[:].rearrange("p (h c) -> p h c", h=4)

        c_in, w_fq, w_rest = sem("c_in"), sem("w_fq"), sem("w_rest")
        x_in, side_in = sem("x_in"), sem("side_in")
        s_in, mix_out, s_out = sem("s_in"), sem("mix_out"), sem("s_out")
        names = ("r_ready xn_ready pe_xT xT_ready pe_F pe_Q pe_AQ pe_AKV pe_V pe_G ef_ready f_ready lf_ready eq_ready "
                 "q_ready b_ready eb_ready D_ready E_ready M_ready pe_gram A_ready qk_ready rot_ready va_ready pe_qkT qkT_ready "
                 "v_ready eg_ready gg_ready pe_S sm_ready m_ready p_ready den_ready kd_ready ke_exp ke_ready pe_KET "
                 "ket_ready pe_dS pe_O st_ready ro_ready rr_ready mixh_ready pe_PT pT_ready pe_Oa mixa_ready pe_mix "
                 "mixT_ready lb_ready sam_ready pe_sam act_sam idle").split()
        S = {n: sem(n) for n in names}
        idle = S["idle"]
        NC_IN = 8
        NS_IN = 7

        block = ctx.enter_context(nc.Block())

        @block.sync
        def _(sp):
            sp.dma_start(xs[:], io["x_all"][0:P, :]).then_inc(x_in, 16)
            w = io["w_in"].rearrange("(k p) n -> p k n", p=P)
            for dst, src in ((ident[:], io["ident"]), (gmix[:], io["norm_mix"].broadcast_to([P, DM])),
                             (lbl[:], io["lb_logits"].rearrange("l (h p) -> p l h", p=P)),
                             (reset[:], io["reset"].rearrange("p (h c) -> p h c", h=HH)),
                             (lmask[:], io["level_masks"].rearrange("p (g c) -> p g c", g=GRAMS)),
                             (gnorm[:], io["hgrn_norm"].broadcast_to([P, HW])),
                             (sinkb[:], io["attn_sink"].broadcast_to([P, SH])),
                             (sinkc[:], io["attn_sink"].rearrange("a h -> h a"))):
                with nc.allow_non_contiguous_dma(reason="a few small constants"):
                    sp.dma_start(dst, src).then_inc(c_in, 16)
            for lo, hi, s in ((OFF_Q, OFF_I, w_fq), (OFF_I, IN_W, w_rest)):
                for k in range(0, KT, 2):
                    sp.dma_start(w_in[:, k:k + 2, lo:hi], w[:, k:k + 2, lo:hi]).then_inc(s, 16)
            sp.dma_start(s0[:], io["state_s"].rearrange("n k v -> k n v")).then_inc(s_in, 16)
            sp.dma_start(sel, io["sel"].rearrange("p (b c) -> p b c", b=NS)).then_inc(s_in, 16)
            sp.dma_start(kc, io["cache_k"].rearrange("b w c -> w b c")).then_inc(s_in, 16)
            for s in range(KV):
                for r in range(2):
                    sp.dma_start(v2[:, :, s, r, :], io["cache_v"].rearrange("b w c -> w b c")[:, :, s * HD:(s + 1) * HD]).then_inc(s_in, 16)
            sp.dma_start(rope[:], io["rope"][0:P].rearrange("p (a c) -> p a c", a=2)).then_inc(side_in, 16)
            sp.dma_start(wmask[:], io["wmask"][0:P, :]).then_inc(side_in, 16)
            for dst, src in (("new_k_s", "cache_k"), ("new_v_s", "cache_v")):
                sp.dma_start(io[dst][:, 0:WIN - 1, :], io[src][:, 1:WIN, :]).then_inc(s_out, 16)
            sp.wait_ge(S["rot_ready"], 1)
            sp.dma_start(io["new_k_s"][:, WIN - 1, :], qkr[0:NS, 4, :, :].rearrange("p a c -> p (a c)")).then_inc(s_out, 16)
            sp.wait_ge(S["va_ready"], 1)
            sp.dma_start(io["new_v_s"][:, WIN - 1, :], va[0:NS, 1, :]).then_inc(s_out, 16)
            sp.wait_ge(S["sam_ready"], 1 + NS)
            sp.dma_start(io["new_state_s"].rearrange("n k v -> k n v"), s0[:]).then_inc(s_out, 16)
            sp.wait_ge(S["xn_ready"], 1)
            sp.dma_start(xs[:], io["x_all"][P:2 * P, :]).then_inc(x_in, 16)
            sp.wait_ge(S["xn_ready"], 2)
            sp.dma_start(xs[:], io["x_all"][2 * P:3 * P, :]).then_inc(x_in, 16)

            def loads(i, more):
                sp.wait_ge(S["xn_ready"], i + 3)
                sp.dma_start(rope[:], io["rope"][bass.ds((i + 1) * P, P), :].rearrange("p (a c) -> p a c", a=2)).then_inc(side_in, 16)
                sp.dma_start(wmask[:], io["wmask"][bass.ds(i * P, P), :]).then_inc(side_in, 16)
                if more:
                    sp.dma_start(xs[:], io["x_all"][bass.ds((i + 3) * P, P), :]).then_inc(x_in, 16)

            def store(t):
                sp.wait_ge(S["mixT_ready"], t + 1)
                sp.dma_start(io["mix_scratch"][bass.ds(t - 1, 1)].rearrange("a p k c -> (a p) k c"), mixT[:]).then_inc(mix_out, 16)

            loads(0, True)
            sp.wait_ge(S["mixT_ready"], 1)
            sp.dma_start(io["mix_scratch"][NB], mixT[:]).then_inc(mix_out, 16)
            with sp.Fori(1, NB - 1) as i:
                loads(i, True)
                store(i)
            loads(NB - 1, False)
            store(NB - 1)
            store(NB)
            sp.wait_ge(S["st_ready"], NB + 1)
            sp.dma_start(io["new_state_p"].rearrange("h p v -> p h v"), st[:]).then_inc(s_out, 16)
            sp.dma_start(io["new_k_p"], qkr[:, 4, :, :].rearrange("p a c -> p (a c)")).then_inc(s_out, 16)
            sp.dma_start(io["new_v_p"], va[:, 1, :]).then_inc(s_out, 16)
            sp.wait_ge(s_out, 16 * 8)
            sp.wait_ge(mix_out, 16 * (NB + 1))
            sp.wait_ge(x_in, 16 * (NB + 2))

        def sampled_pe(pe):
            pe.wait_ge(S["v_ready"], 1)
            pe.wait_ge(s_in, 16 * NS_IN)
            for b in range(NS):
                if b >= 2:
                    pe.wait_ge(S["sam_ready"], b)
                pe.matmul((G0, G1)[b % 2][:], sel[:, b, :], vv[0:NS, :], start=True, stop=True).then_inc(S["pe_sam"], 1)
            pe.wait_ge(S["sam_ready"], 1 + NS)
            for h in range(HH):
                for b in range(NS):
                    m = pe.matmul(OO[0:NS, h * P:(h + 1) * P], qd[:, h, b * NS:(b + 1) * NS], s0[:, b * HH + h, :],
                                  start=(b == 0), stop=(b == NS - 1))
            m.then_inc(S["pe_O"], 1)
            pe.wait_ge(S["qkT_ready"], 1)
            for b in range(NS):
                m = pe.transpose((T0, T1)[b // 4][:, (b % 4) * P:(b % 4 + 1) * P], kc[:, b, :], ident[:])
            m.then_inc(S["pe_sam"], 1)
            pe.wait_ge(S["act_sam"], 1)
            for b in range(NS):
                pe.matmul((G0, G1)[b // 4][0:SH, (b % 4) * P:(b % 4 + 1) * P], qbd[:, b, :], kcT[:, b, :], start=True, stop=True)
                m = pe.matmul(FB[0:SH, b:b + 1], qbd[:, b, :], kT[:, 1, b:b + 1], start=True, stop=True)
            m.then_inc(S["pe_sam"], 1)
            pe.wait_ge(S["sam_ready"], 3 + NS)
            for b in range(NS):
                pe.transpose(T0[:, b * SH:(b + 1) * SH], sc[:, b, 0:WIN], ident[0:SH, 0:SH])
            pe.transpose(T1[0:NS, 0:SH], sc[:, :, WIN], ident[0:SH, 0:SH]).then_inc(S["pe_sam"], 1)
            pe.wait_ge(S["act_sam"], 3)
            pe.wait_ge(S["sam_ready"], 4 + NS)
            for b in range(NS):
                for s in range(KV):
                    lo = b * SH + s * GQ
                    pe.matmul(G0[:, lo:lo + GQ], v2[:, b, s].rearrange("p r d -> p (r d)"), pTs[:, lo:lo + GQ], start=True, stop=False)
                    m = pe.matmul(G0[:, lo:lo + GQ], vnd[:, s].rearrange("p r d -> p (r d)"), rn[:, b, s * GQ:(s + 1) * GQ],
                                  start=False, stop=True)
            m.then_inc(S["pe_sam"], 1)
            pe.wait_ge(S["mixh_ready"], 1)
            for k in range(4):
                m = pe.transpose(T1[:, 64 + k * NS:64 + (k + 1) * NS], mixh[0:NS, k * P:(k + 1) * P], ident[0:NS, 0:NS])
            m.then_inc(S["pe_mix"], 1)

        def sampled_act(act, readout_norm):
            readout_norm(0, NS)
            act.wait_ge(S["pe_sam"], NS + 1)
            act.activation(kcT[:, 0:4, :], bank4(T0), ACT.Copy)
            act.activation(kcT[:, 4:8, :], bank4(T1), ACT.Copy).then_inc(S["act_sam"], 1)
            act.wait_ge(S["sam_ready"], 2 + NS)
            act.activation(sc, sc, ACT.Exp)
            act.activation(sx[:, 2, :], sx[:, 1, :], ACT.Exp, scale=-1.0, bias=sinkc[:]).then_inc(S["act_sam"], 1)
            act.wait_ge(S["pe_sam"], NS + 3)
            act.activation(pTs, T0[:, 0:NS * SH], ACT.Copy).then_inc(S["act_sam"], 1)

        def sampled_vector(v, mix_a):
            v.memset(qd[:], 0.0)
            v.memset(qbd[:], 0.0)
            v.memset(mixT[:], 0.0)
            v.drain()
            v.tensor_copy(qd[:, :, 0:NS * NS:NS + 1], qq[:, :, 0:NS])
            for s in range(KV):
                lo = HD * s
                v.tensor_copy(qbd[lo:lo + HD, :, s * GQ:(s + 1) * GQ], qT[lo:lo + HD, :, 0:NS].rearrange("p j b -> p b j"))
            v.wait_ge(S["qk_ready"], 1)
            for r in range(2):
                m = v.tensor_copy(vnd[:, :, r, :], va[0:NS, 1, :].rearrange("p (s d) -> p s d", s=KV))
            m.then_inc(S["sam_ready"], 1)
            v.wait_ge(s_in, 16 * NS_IN)
            for b in range(NS):
                for h in range(HH):
                    v.tensor_scalar(s0[:, b * HH + h, :], s0[:, b * HH + h, :], ff[:, h, b:b + 1], None, ALU.mult)
            v.drain()
            for b in range(NS):
                v.wait_ge(S["pe_sam"], b + 1)
                for h in range(HH):
                    m = v.scalar_tensor_tensor(out=s0[:, b * HH + h, :], in0=(G0, G1)[b % 2][:, h * P:(h + 1) * P],
                                               scalar=kk[:, h, b:b + 1], in1=s0[:, b * HH + h, :], op0=ALU.mult, op1=ALU.add)
                m.then_inc(S["sam_ready"], 1)
            mix_a(0, NS)
            v.wait_ge(S["pe_sam"], NS + 2)
            for a, b in enumerate((G0, G1)):
                v.tensor_scalar(sc[:, 4 * a:4 * a + 4, 0:WIN], bank4(b)[0:SH], SCALE, None, ALU.mult)
            v.tensor_scalar(sc[:, :, WIN], FB[0:SH, 0:NS], SCALE, None, ALU.mult)
            v.drain()
            v.tensor_reduce(sx[:, 0, :], sc, AX.X, ALU.max)
            v.drain()
            v.tensor_scalar(sx[:, 1, :], sx[:, 0, :], sinkc[:], None, ALU.max)
            v.drain()
            v.tensor_tensor(sc, sc, sx[:, 1, :].rearrange("p (b c) -> p b c", c=1).broadcast_to([SH, NS, WIN + 1]),
                            ALU.subtract).then_inc(S["sam_ready"], 1)
            v.wait_ge(S["act_sam"], 2)
            v.tensor_reduce(sx[:, 3, :], sc, AX.X, ALU.add)
            v.drain()
            v.tensor_tensor(sx[:, 4, :], sx[:, 3, :], sx[:, 2, :], ALU.add)
            v.drain()
            v.reciprocal(sx[:, 5, :], sx[:, 4, :])
            v.drain()
            v.tensor_tensor(sc, sc, sx[:, 5, :].rearrange("p (b c) -> p b c", c=1).broadcast_to([SH, NS, WIN + 1]),
                            ALU.mult).then_inc(S["sam_ready"], 1)
            v.wait_ge(S["pe_sam"], NS + 3)
            v.tensor_tensor(rn[:], T1[0:NS, 0:SH].rearrange("p (a h) -> p a h", a=1).broadcast_to([NS, NS, SH]),
                            ident[0:NS, 0:NS].rearrange("p (b a) -> p b a", a=1).broadcast_to([NS, NS, SH]), ALU.mult)\
                .then_inc(S["sam_ready"], 1)
            v.wait_ge(S["pe_sam"], NS + 4)
            for r in range(2):
                lo = HD * r
                v.tensor_copy(mixT[lo:lo + HD, 4:8, 0:NS],
                              G0[lo:lo + HD, 0:NS * SH].rearrange("p (b j r) -> p r j b", b=NS, r=2)[:, r])
            v.wait_ge(S["pe_mix"], 1)
            v.tensor_copy(mixT[:, 0:4, 0:NS], T1[:, 64:64 + 4 * NS].rearrange("p (k b) -> p k b", k=4)).then_inc(S["mixT_ready"], 1)
            v.drain()
            v.tensor_copy(sx[:, 0, :], sx[:, 1, :]).then_inc(S["mixa_ready"], 1)

        @block.tensor
        def _(pe):
            def x_transposes(t):
                pe.wait_ge(S["xn_ready"], t + 1)
                for k in range(KT):
                    m = pe.transpose((T0 if k < 4 else T1)[:, (k % 4) * P:(k % 4 + 1) * P], xn[:, k * P:(k + 1) * P], ident[:])
                m.then_inc(S["pe_xT"], 1)

            def feature_projection(out, off, done):
                for h in range(HH):
                    for k in range(KT):
                        m = pe.matmul(out[:, h * P:(h + 1) * P], w_in[:, k, off + h * P:off + (h + 1) * P], xT[:, k, :],
                                      start=(k == 0), stop=(k == KT - 1))
                m.then_inc(done, 1)

            def token_projection(out, off, width, done):
                for k in range(KT):
                    m = pe.matmul(out[:, 0:width], xT[:, k, :], w_in[:, k, off:off + width], start=(k == 0), stop=(k == KT - 1))
                m.then_inc(done, 1)

            def gram(t, g):
                if g < LEVELS:
                    pe.wait_ge(S["M_ready"], LEVELS * (t - 1) + g + 1)
                if g >= 2:
                    pe.wait_ge(S["A_ready"], GRAMS * (t - 1) + g - 1)
                for h in range(HH):
                    a = mm[:, g % 2, h, :] if g < LEVELS else kk[:, h, :]
                    b = mm[:, g % 2, h, :] if g < LEVELS else qq[:, h, :]
                    m = pe.matmul(GB[g % 2][:, h * P:(h + 1) * P], a, b, start=True, stop=True)
                m.then_inc(S["pe_gram"], 1)

            def qk_transposes(t):
                pe.wait_ge(S["rot_ready"], t + 1)
                for j in range(5):
                    m = pe.transpose(T0[:, j * P:(j + 1) * P] if j < 4 else T1[:, 0:P],
                                     qkr[:, j, :, :].rearrange("p a c -> p (a c)"), ident[:])
                m.then_inc(S["pe_qkT"], 1)

            def scores(t, n):
                if n == 0:
                    pe.wait_ge(S["qkT_ready"], t + 1)
                else:
                    pe.wait_ge(S["sm_ready"], 2 * (t - 1) + 1)
                for s, out in enumerate((S0, S1)):
                    for a in range(2):
                        lo = HD * s
                        m = pe.matmul(out[:, a * 256:(a + 1) * 256], qT[lo:lo + HD, 2 * n + a, :],
                                      kT[lo:lo + HD, :, :].rearrange("p a c -> p (a c)"), start=True, stop=True)
                m.then_inc(S["pe_S"], 1)

            def state_products(t):
                pe.wait_ge(S["ke_ready"], t + 1)
                for h in range(HH):
                    m = pe.transpose(T0[:, h * P:(h + 1) * P], at2[:, h, :], ident[:])
                m.then_inc(S["pe_KET"], 1)
                pe.wait_ge(S["ket_ready"], t + 1)
                for h in range(HH):
                    m = pe.matmul(DS[:, h * P:(h + 1) * P], ket[:, h, :], vv[:, h * P:(h + 1) * P], start=True, stop=True)
                m.then_inc(S["pe_dS"], 1)

            def readout(t):
                pe.wait_ge(S["A_ready"], GRAMS * t)
                for h in range(HH):
                    pe.matmul(OO[:, h * P:(h + 1) * P], qb[:, h, :], st[:, h, :], start=True, stop=False)
                    m = pe.matmul(OO[:, h * P:(h + 1) * P], at[:, h, :], vv[:, h * P:(h + 1) * P], start=False, stop=True)
                m.then_inc(S["pe_O"], 1)

            def p_transposes(t, n):
                if n == 0:
                    pe.wait_ge(S["p_ready"], t)
                if n >= 2:
                    pe.wait_ge(S["pT_ready"], 4 * (t - 1) + n - 1)
                b = T0 if n % 2 == 0 else T1
                for a in range(4):
                    h, kb = 2 * n + a // 2, a % 2
                    m = pe.transpose(b[:, a * P:(a + 1) * P], sm[:, h, kb * P:(kb + 1) * P], ident[:])
                m.then_inc(S["pe_PT"], 1)

            def values(t):
                pe.wait_ge(S["pT_ready"], 4 * t)
                for h in range(SH):
                    lo = HD * (h // GQ)
                    for kb in range(2):
                        m = pe.matmul(OA[:, h * HD:(h + 1) * HD], pT[:, h, kb, :], va[:, kb, lo:lo + HD],
                                      start=(kb == 0), stop=(kb == 1))
                m.then_inc(S["pe_Oa"], 1)

            def mix_transposes(t):
                pe.wait_ge(S["mixh_ready"], t + 1)
                for k in range(4):
                    pe.transpose(T0[:, k * P:(k + 1) * P], mixh[:, k * P:(k + 1) * P], ident[:])
                pe.wait_ge(S["mixa_ready"], t + 1)
                for k in range(4):
                    m = pe.transpose(T1[:, k * P:(k + 1) * P], mixa[:, k * P:(k + 1) * P], ident[:])
                m.then_inc(S["pe_mix"], 1)

            at2 = dd[:, 0]

            def project_f(n):
                pe.wait_ge(S["xT_ready"], n + 1)
                feature_projection(FA, OFF_F, S["pe_F"])

            def project_q(n):
                feature_projection(FB, OFF_Q, S["pe_Q"])

            def project_aq(n):
                pe.wait_ge(S["ef_ready"], n + 1)
                token_projection(FA, OFF_AQ, 512, S["pe_AQ"])

            def project_akv(n):
                pe.wait_ge(S["eq_ready"], n + 1)
                token_projection(FB, OFF_AK, 256, S["pe_AKV"])

            def project_v(n):
                pe.wait_ge(S["qk_ready"], n + 1)
                token_projection(FA, OFF_I, 512, S["pe_V"])

            def project_g(n):
                token_projection(FB, OFF_G, 512, S["pe_G"])

            pe.wait_ge(c_in, 16 * NC_IN)
            x_transposes(0)
            pe.wait_ge(w_fq, 64)
            project_f(0)
            project_q(0)
            pe.wait_ge(w_rest, 64)
            project_aq(0)
            project_akv(0)
            qk_transposes(0)
            project_v(0)
            project_g(0)
            state_products(0)
            sampled_pe(pe)
            pe.wait_ge(S["mixT_ready"], 1)
            x_transposes(1)
            project_f(1)
            pe.wait_ge(S["gg_ready"], 1)
            project_q(1)
            project_aq(1)
            project_akv(1)
            project_v(1)
            project_g(1)

            def tile(t, behind, ahead):
                if ahead:
                    x_transposes(t + 1)
                pe.wait_ge(S["q_ready"], t + 1)
                gram(t, 0)
                if ahead:
                    pe.wait_ge(S["v_ready"], t + 1)
                    project_f(t + 1)
                if behind:
                    mix_transposes(t - 1)
                gram(t, 1)
                pe.wait_ge(S["mixT_ready"], t)
                qk_transposes(t)
                if ahead:
                    pe.wait_ge(S["gg_ready"], t + 1)
                    project_q(t + 1)
                gram(t, 2)
                gram(t, 3)
                scores(t, 0)
                if ahead:
                    project_aq(t + 1)
                gram(t, 4)
                gram(t, 5)
                scores(t, 1)
                if ahead:
                    project_akv(t + 1)
                gram(t, 6)
                gram(t, 7)
                if ahead:
                    project_v(t + 1)
                pe.wait_ge(S["m_ready"], t)
                state_products(t)
                readout(t)
                if ahead:
                    project_g(t + 1)
                for n in range(4):
                    p_transposes(t, n)
                values(t)

            tile(1, False, True)
            with pe.Fori(2, NB) as t:
                tile(t, True, True)
            tile(NB, True, False)
            mix_transposes(NB)

        @block.scalar
        def _(act):
            def norm(t):
                act.wait_ge(x_in, 16 * t + 16)
                if not isinstance(t, int) or t > 0:
                    act.wait_ge(S["pe_xT"], t)
                act.activation(xn[:], xs[:], ACT.Square, accum_out=ss[:, 0:1])
                act.drain()
                act.activation(ss[:, 1:2], ss[:, 0:1], ACT.Ln, bias=EPS, scale=1.0 / DM)
                act.drain()
                act.activation(ss[:, 2:3], ss[:, 1:2], ACT.Exp, scale=-0.5).then_inc(S["r_ready"], 1)
                act.drain()

            def take_xT(t):
                act.wait_ge(S["pe_xT"], t + 1)
                act.activation(xT[:, 0:4, :], bank4(T0), ACT.Copy)
                act.activation(xT[:, 4:8, :], bank4(T1), ACT.Copy).then_inc(S["xT_ready"], 1)
                act.drain()

            def forget_exp(n):
                act.wait_ge(S["pe_F"], n + 1)
                act.activation(ef[:], bank4(FA), ACT.Exp, scale=-1.0).then_inc(S["ef_ready"], 1)
                act.drain()

            def forget_log(n):
                act.wait_ge(S["f_ready"], n + 1)
                act.activation(ef[:], ff[:], ACT.Ln).then_inc(S["lf_ready"], 1)
                act.drain()

            def query_exp(n):
                act.wait_ge(S["pe_Q"], n + 1)
                act.activation(qr[:], bank4(FB), ACT.Copy)
                act.activation(sq[:], bank4(FB), ACT.Exp, scale=-1.0).then_inc(S["eq_ready"], 1)
                act.drain()

            def decay(t):
                act.wait_ge(S["b_ready"], t)
                act.activation(eb[:], bb[:], ACT.Exp).then_inc(S["eb_ready"], 1)
                act.drain()

            def level_exp(t, g):
                act.wait_ge(S["D_ready"], LEVELS * (t - 1) + g + 1)
                act.activation(dd[:, g % 2], dd[:, g % 2], ACT.Exp).then_inc(S["E_ready"], 1)
                act.drain()

            def take_aq(n):
                act.wait_ge(S["pe_AQ"], n + 1)
                act.activation(qk[:, 0:4, :, :].rearrange("p j s c -> p s j c"),
                               FA[:].rearrange("p (s j c) -> p s j c", s=2, j=4), ACT.Copy)
                act.drain()

            def take_akv(n):
                act.wait_ge(S["pe_AKV"], n + 1)
                act.activation(qk[:, 4, :, :].rearrange("p s c -> p (s c)"), FB[:, 0:128], ACT.Copy)
                act.activation(vr[:], FB[:, 128:256], ACT.Copy).then_inc(S["qk_ready"], 1)
                act.drain()

            def take_qkT(t):
                act.wait_ge(S["pe_qkT"], t + 1)
                act.activation(qT[:], bank4(T0), ACT.Copy)
                act.activation(kT[:, 1, :], T1[:, 0:P], ACT.Copy).then_inc(S["qkT_ready"], 1)
                act.drain()

            def take_v(t):
                act.wait_ge(S["pe_V"], t + 1)
                act.activation(vv[:], FA[:], ACT.Copy).then_inc(S["v_ready"], 1)
                act.drain()

            def gate_exp(t):
                act.wait_ge(S["pe_G"], t + 1)
                act.activation(gg[:, 0, :], FB[:], ACT.Exp, scale=-1.0).then_inc(S["eg_ready"], 1)
                act.drain()

            def end_decay(t):
                act.wait_ge(S["kd_ready"], t + 1)
                act.activation(dd[:, 1], dd[:, 1], ACT.Exp).then_inc(S["ke_exp"], 1)
                act.wait_ge(S["pe_KET"], t + 1)
                act.activation(ket[:], bank4(T0), ACT.Copy).then_inc(S["ket_ready"], 1)
                act.drain()

            def softmax(t):
                act.wait_ge(S["m_ready"], t)
                for h in range(SH):
                    act.activation(sm[:, h, :], sm[:, h, :], ACT.Exp, bias=mx[:, 2, h:h + 1], accum_out=mx[:, 3, h:h + 1])
                act.activation(mx[:, 4, :], mx[:, 4, :], ACT.Exp).then_inc(S["p_ready"], 1)
                act.drain()

            def readout_norm(t, n):
                act.wait_ge(S["pe_O"], t + 1)
                for h in range(HH):
                    act.activation(sjunk[0:n, h * P:(h + 1) * P], OO[0:n, h * P:(h + 1) * P], ACT.Square,
                                   accum_out=rs[0:n, 0, h:h + 1])
                act.drain()
                act.activation(rs[0:n, 1, :], rs[0:n, 0, :], ACT.Ln, bias=EPS, scale=1.0 / DK)
                act.drain()
                act.activation(rs[0:n, 2, :], rs[0:n, 1, :], ACT.Exp, scale=-0.5).then_inc(S["rr_ready"], 1)
                act.drain()

            def take_pT(t, n):
                act.wait_ge(S["pe_PT"], 4 * (t - 1) + n + 1)
                act.activation(pT[:, 2 * n:2 * n + 2, :, :].rearrange("p h a c -> p (h a) c"),
                               bank4(T0 if n % 2 == 0 else T1), ACT.Copy).then_inc(S["pT_ready"], 1)
                act.drain()

            def take_mix(t):
                act.wait_ge(S["pe_mix"], t + 1)
                act.wait_ge(mix_out, 16 * t)
                act.activation(mixT[:, 0:4, :], bank4(T0), ACT.Copy)
                act.activation(mixT[:, 4:8, :], bank4(T1), ACT.Copy).then_inc(S["mixT_ready"], 1)
                act.drain()

            act.preload_act_table_set("natural_log_exp_and_others")
            act.wait_ge(c_in, 16 * NC_IN)
            act.wait_ge(S["lb_ready"], 1)
            act.activation(lbw[:, 0:2, :], lbw[:, 0:2, :], ACT.Exp).then_inc(S["lb_ready"], 1)
            norm(0)
            take_xT(0)
            forget_exp(0)
            query_exp(0)
            forget_log(0)
            take_aq(0)
            take_akv(0)
            take_qkT(0)
            take_v(0)
            gate_exp(0)
            end_decay(0)
            sampled_act(act, readout_norm)
            norm(1)
            take_xT(1)
            act.wait_ge(S["mixa_ready"], 1)
            forget_exp(1)
            query_exp(1)
            forget_log(1)
            take_aq(1)
            take_akv(1)
            take_v(1)
            gate_exp(1)
            norm(2)

            def tile(t, behind, ahead):
                level_exp(t, 0)
                level_exp(t, 1)
                if ahead:
                    take_xT(t + 1)
                level_exp(t, 2)
                if ahead:
                    act.wait_ge(S["b_ready"], t)
                    forget_exp(t + 1)
                if behind:
                    take_mix(t - 1)
                take_qkT(t)
                level_exp(t, 3)
                if ahead:
                    forget_log(t + 1)
                level_exp(t, 4)
                decay(t)
                if ahead:
                    query_exp(t + 1)
                level_exp(t, 5)
                if ahead:
                    take_aq(t + 1)
                level_exp(t, 6)
                if ahead:
                    take_akv(t + 1)
                softmax(t)
                end_decay(t)
                if ahead:
                    norm(t + 2)
                readout_norm(t, P)
                if ahead:
                    take_v(t + 1)
                    gate_exp(t + 1)
                for n in range(4):
                    take_pT(t, n)

            tile(1, False, True)
            with act.Fori(2, NB) as t:
                tile(t, True, True)
            tile(NB, True, False)
            take_mix(NB)

        @block.vector
        def _(v):
            def norm(t):
                v.wait_ge(S["r_ready"], t + 1)
                v.scalar_tensor_tensor(out=xn[:], in0=xs[:], scalar=ss[:, 2:3], in1=gmix[:], op0=ALU.mult,
                                       op1=ALU.mult).then_inc(S["xn_ready"], 1)
                v.drain()

            def forget_gate(n):
                v.wait_ge(S["ef_ready"], n + 1)
                v.tensor_scalar(ef[:], ef[:], 1.0, None, ALU.add)
                v.drain()
                v.reciprocal(ff[:], ef[:])
                v.drain()
                for h in range(HH):
                    m = v.tensor_scalar(ff[:, h, :], ff[:, h, :], oml[:, h:h + 1], lb[:, h:h + 1], ALU.mult, ALU.add)
                m.then_inc(S["f_ready"], 1)
                v.drain()

            def query_sigmoid(n):
                v.wait_ge(S["eq_ready"], n + 1)
                v.tensor_scalar(sq[:], sq[:], 1.0, None, ALU.add)
                v.drain()
                v.reciprocal(sq[:], sq[:])
                v.drain()

            def features(t):
                v.tensor_scalar(kk[:], ff[:], -1.0, 1.0, ALU.mult, ALU.add)
                v.tensor_tensor(qq[:], sq[:], qr[:], ALU.mult).then_inc(S["q_ready"], 1)
                v.drain()

            def take_values(t):
                v.wait_ge(S["qk_ready"], t + 1)
                v.tensor_copy(va[:, 1, :], vr[:]).then_inc(S["va_ready"], 1)
                v.drain()

            def cumulate(t):
                v.wait_ge(S["lf_ready"], t + 1)
                v.tensor_tensor_scan(bb[:].rearrange("p h c -> p (h c)"), reset[:].rearrange("p h c -> p (h c)"),
                                     ef[:].rearrange("p h c -> p (h c)"), 0.0, ALU.mult, ALU.add).then_inc(S["b_ready"], 1)
                v.drain()

            def halves(x, g):
                half = P >> (g + 1)
                y = x.rearrange("p h c -> p (h c)").rearrange("p (n a c) -> p n a c", a=2, c=half)
                return y[:, :, 0, :], y[:, :, 1, :], half

            def level_gap(t, g):
                bl, br, half = halves(bb[:], g)
                dl, dr, _ = halves(dd[:, g % 2], g)
                mid = bl[:, :, half - 1:half].broadcast_to([P, bl.shape[1], half])
                v.tensor_tensor(dl, mid, bl, ALU.subtract)
                v.tensor_tensor(dr, br, mid, ALU.subtract).then_inc(S["D_ready"], 1)
                v.drain()

            def level_operands(t, g):
                v.wait_ge(S["E_ready"], LEVELS * (t - 1) + g + 1)
                if g >= 2:
                    v.wait_ge(S["pe_gram"], GRAMS * (t - 1) + g - 1)
                el, er, _ = halves(dd[:, g % 2], g)
                kl, _, _ = halves(kk[:], g)
                _, qr, _ = halves(qq[:], g)
                ml, mr, _ = halves(mm[:, g % 2], g)
                v.tensor_tensor(ml, el, kl, ALU.mult)
                v.tensor_tensor(mr, er, qr, ALU.mult).then_inc(S["M_ready"], 1)
                v.drain()

            def level_take(t, g):
                v.wait_ge(S["pe_gram"], GRAMS * (t - 1) + g + 1)
                mask = lmask[:, g:g + 1, :].broadcast_to([P, HH, P])
                if g == 0:
                    v.tensor_tensor(at[:], bank4(GB[0]), mask, ALU.mult).then_inc(S["A_ready"], 1)
                else:
                    standalone(v, idle)
                    v.copy_predicated(at[:], mask, bank4(GB[g % 2])).then_inc(S["A_ready"], 1)
                v.drain()

            def rotate(t):
                v.wait_ge(S["qk_ready"], t + 1)
                if not isinstance(t, int) or t > 0:
                    v.wait_ge(S["pe_mix"], t)
                v.wait_ge(side_in, 32 * t + 32)
                x = qk[:].rearrange("p j s c -> p (j s) c")
                lo, hi = x[:, :, 0:32], x[:, :, 32:64]
                o = qkr[:].rearrange("p j s c -> p (j s) c")
                cos, sin = (rope[:, a:a + 1, :].broadcast_to([P, 10, 32]) for a in (0, 1))
                v.tensor_tensor(rt[:, 0, :, 0:32], lo, cos, ALU.mult)
                v.tensor_tensor(rt[:, 0, :, 32:64], hi, cos, ALU.mult)
                v.tensor_tensor(rt[:, 1, :, 0:32], hi, sin, ALU.mult)
                v.tensor_tensor(rt[:, 1, :, 32:64], lo, sin, ALU.mult)
                v.drain()
                v.tensor_tensor(o[:, :, 0:32], rt[:, 0, :, 0:32], rt[:, 1, :, 0:32], ALU.subtract)
                v.tensor_tensor(o[:, :, 32:64], rt[:, 0, :, 32:64], rt[:, 1, :, 32:64], ALU.add).then_inc(S["rot_ready"], 1)
                v.drain()

            def mask_scores(t, n):
                v.wait_ge(S["pe_S"], 2 * (t - 1) + n + 1)
                for s, b in enumerate((S0, S1)):
                    h = GQ * s + 2 * n
                    m = v.scalar_tensor_tensor(out=sm[:, h:h + 2, :], in0=b[:].rearrange("p (a c) -> p a c", a=2), scalar=SCALE,
                                               in1=wmask[:].rearrange("p (a c) -> p a c", a=1).broadcast_to([P, 2, 2 * WIN]),
                                               op0=ALU.mult, op1=ALU.add)
                m.then_inc(S["sm_ready"], 1)
                v.drain()

            def row_max(t):
                v.drain()
                v.tensor_reduce(mx[:, 0, :], sm[:], AX.X, ALU.max)
                v.drain()
                v.tensor_tensor(mx[:, 1, :], mx[:, 0, :], sinkb[:], ALU.max)
                v.drain()
                v.tensor_scalar(mx[:, 2, :], mx[:, 1, :], -1.0, None, ALU.mult)
                v.tensor_tensor(mx[:, 4, :], sinkb[:], mx[:, 1, :], ALU.subtract).then_inc(S["m_ready"], 1)
                v.drain()

            def end_gap(t):
                v.tensor_tensor(dd[:, 1], bb[:, :, P - 1:P].broadcast_to([P, HH, P]), bb[:], ALU.subtract).then_inc(S["kd_ready"], 1)
                v.drain()

            def query_decay(t):
                v.wait_ge(S["eb_ready"], t)
                v.tensor_tensor(qb[:], qq[:], eb[:], ALU.mult)
                v.drain()

            def end_keys(t):
                v.wait_ge(S["ke_exp"], t + 1)
                v.tensor_tensor(dd[:, 0], kk[:], dd[:, 1], ALU.mult).then_inc(S["ke_ready"], 1)
                v.drain()

            def gate(t):
                v.wait_ge(S["eg_ready"], t + 1)
                v.tensor_scalar(gg[:, 1, :], gg[:, 0, :], 1.0, None, ALU.add)
                v.drain()
                v.reciprocal(gg[:, 0, :], gg[:, 1, :])
                v.drain()
                v.tensor_tensor(gg[:, 1, :], gg[:, 0, :], FB[:], ALU.mult)
                v.drain()
                v.tensor_tensor(gg[:, 1, :], gg[:, 1, :], gnorm[:], ALU.mult).then_inc(S["gg_ready"], 1)
                v.drain()

            def new_state(t):
                v.wait_ge(S["pe_dS"], t + 1)
                v.wait_ge(S["pe_O"], t + 1)
                for h in range(HH):
                    m = v.scalar_tensor_tensor(out=st[:, h, :], in0=st[:, h, :], scalar=eb[:, h, P - 1:P],
                                               in1=DS[:, h * P:(h + 1) * P], op0=ALU.mult, op1=ALU.add)
                m.then_inc(S["st_ready"], 1)
                v.drain()

            def mix_a(t, n):
                v.wait_ge(S["rr_ready"], t + 1)
                for h in range(HH):
                    m = v.scalar_tensor_tensor(out=mixh[0:n, h * P:(h + 1) * P], in0=OO[0:n, h * P:(h + 1) * P],
                                               scalar=rs[0:n, 2, h:h + 1], in1=gg[0:n, 1, h * P:(h + 1) * P],
                                               op0=ALU.mult, op1=ALU.mult)
                m.then_inc(S["mixh_ready"], 1)
                v.drain()

            def mix_b(t):
                v.wait_ge(S["p_ready"], t)
                v.tensor_tensor(mx[:, 5, :], mx[:, 3, :], mx[:, 4, :], ALU.add)
                v.drain()
                v.reciprocal(mx[:, 0, :], mx[:, 5, :])
                v.drain()
                v.wait_ge(S["pe_Oa"], t)
                v.tensor_tensor(mixa.rearrange("p (h c) -> p h c", h=SH), OA[:].rearrange("p (h c) -> p h c", h=SH),
                                mx[:, 0, :].rearrange("p (h c) -> p h c", c=1).broadcast_to([P, SH, HD]), ALU.mult).then_inc(S["mixa_ready"], 1)
                v.tensor_copy(kT[:, 0, :], kT[:, 1, :])
                v.tensor_copy(va[:, 0, :], va[:, 1, :])
                v.drain()

            v.wait_ge(c_in, 16 * NC_IN)
            v.tensor_tensor(lbw[:, 2, :], lbl[:, 0, :], lbl[:, 1, :], ALU.max)
            v.drain()
            v.tensor_tensor(lbw[:, 0:2, :], lbl[:], lbw[:, 2:3, :].broadcast_to([P, 2, HH]), ALU.subtract).then_inc(S["lb_ready"], 1)
            v.wait_ge(S["lb_ready"], 2)
            v.tensor_tensor(lbw[:, 1, :], lbw[:, 0, :], lbw[:, 1, :], ALU.add)
            v.drain()
            v.reciprocal(lbw[:, 3, :], lbw[:, 1, :])
            v.drain()
            v.tensor_tensor(lb, lbw[:, 0, :], lbw[:, 3, :], ALU.mult)
            v.drain()
            v.tensor_scalar(oml, lb, -1.0, 1.0, ALU.mult, ALU.add)
            norm(0)
            forget_gate(0)
            query_sigmoid(0)
            features(0)
            take_values(0)
            v.wait_ge(S["lf_ready"], 1)
            v.memset(bb[:], 0.0)
            v.memset(ef[:, :, 0:P - META], 0.0)
            v.drain()
            v.tensor_tensor_scan(bb[:].rearrange("p h c -> p (h c)"), reset[:].rearrange("p h c -> p (h c)"),
                                 ef[:].rearrange("p h c -> p (h c)"), 0.0, ALU.mult, ALU.add)
            v.drain()
            end_gap(0)
            rotate(0)
            v.wait_ge(S["ke_exp"], 1)
            v.memset(dd[:, 0, :, 0:P - META], 0.0)
            v.tensor_tensor(dd[:, 0, :, P - META:P], kk[:, :, P - META:P], dd[:, 1, :, P - META:P], ALU.mult).then_inc(S["ke_ready"], 1)
            gate(0)
            v.wait_ge(S["pe_dS"], 1)
            v.tensor_copy(st[:], bank4(DS)).then_inc(S["st_ready"], 1)
            v.wait_ge(S["qkT_ready"], 1)
            v.tensor_copy(kT[:, 0, :], kT[:, 1, :])
            v.tensor_copy(va[:, 0, :], va[:, 1, :])
            sampled_vector(v, mix_a)

            norm(1)
            forget_gate(1)
            query_sigmoid(1)
            gate(1)
            norm(2)

            def tile(t, behind, ahead):
                features(t)
                cumulate(t)
                level_gap(t, 0)
                level_gap(t, 1)
                level_operands(t, 0)
                if behind:
                    mix_b(t - 1)
                take_values(t)
                level_gap(t, 2)
                level_operands(t, 1)
                level_take(t, 0)
                rotate(t)
                level_gap(t, 3)
                level_operands(t, 2)
                if ahead:
                    forget_gate(t + 1)
                level_take(t, 1)
                level_gap(t, 4)
                level_operands(t, 3)
                level_take(t, 2)
                mask_scores(t, 0)
                level_gap(t, 5)
                level_operands(t, 4)
                level_take(t, 3)
                level_gap(t, 6)
                if ahead:
                    query_sigmoid(t + 1)
                level_operands(t, 5)
                level_take(t, 4)
                mask_scores(t, 1)
                level_operands(t, 6)
                level_take(t, 5)
                row_max(t)
                end_gap(t)
                query_decay(t)
                level_take(t, 6)
                level_take(t, 7)
                end_keys(t)
                if ahead:
                    norm(t + 2)
                new_state(t)
                mix_a(t, P)
                if ahead:
                    gate(t + 1)

            tile(1, False, True)
            with v.Fori(2, NB) as t:
                tile(t, True, True)
            tile(NB, True, False)
            mix_b(NB)


def peer_program(nc, io):
    with ExitStack() as ctx:
        def sb(name, shape, dt=F32):
            return ctx.enter_context(nc.sbuf_tensor("b_" + name, shape, dt))

        def sem(name):
            return ctx.enter_context(nc.semaphore("b_" + name))

        def bank(name, n=1):
            return ctx.enter_context(nc.psum_tensor("b_" + name, [P, 512 * n], F32))

        w_out = sb("w_out", [P, KT, DM])
        wk = sb("wk", [P, KT, 2 * PH * NKEY])
        ring = sb("ring", [P, RING, 2 * DM])
        ident = sb("ident", [P, P])
        gffn = sb("gffn", [P, DM])
        gfin = sb("gfin", [P, DM])
        mixT = sb("mixT", [P, KT, P])
        hn = sb("hn", [P, DM])
        xbn = sb("xbn", [P, DM])
        xbT = sb("xbT", [P, KT, P])
        xbc = sb("xbc", [P, DM])
        yo = sb("yo", [P, DM])
        junk = sb("junk", [P, DM], mybir.dt.bfloat16)
        diag = sb("diag", [P, DIAGS, P])
        dots = sb("dots", [P, 2, TOPK])
        ge = sb("ge", [P, 2, TOPK])
        wt = sb("wt", [P, 2, TOPK])
        nrm = sb("nrm", [P, 6])
        tops = sb("tops", [P, 2, TOPK])
        topi = sb("topi", [P, 2, TOPK], U32)
        topf = sb("topf", [P, 2, TOPK])
        rest = sb("rest", [P, 256])
        cand = sb("cand", [P, TOPK, TOPK])
        bc = sb("bc", [P, TOPK], U32)
        ab = sb("ab", [P, 2, TOPK], U32)
        hot = sb("hot", [P, 2, TOPK, TOPK])
        pick = sb("pick", [P, 2, TOPK])
        iota = sb("iota", [P, TOPK])
        best = sb("best", [P, PH, TOPK])
        idx = sb("idx", [P, PH, TOPK], U32)
        gate = sb("gate", [P, PH, TOPK])
        gsum = sb("gsum", [P, 2, PH])
        icur = sb("icur", [P, 2, TOPK], U32)
        gcur = sb("gcur", [P, 2, TOPK])
        sel = sb("sel", [NS, NS, P])

        ab_T = icur[:].rearrange("p a c -> p (a c)")[:, 0:NS]
        gate_T = gcur[:].rearrange("p a c -> p (a c)")[:, 0:NS]
        wd = hot[:].rearrange("p a b c -> p (a b c)")[:, 0:NS * NS]

        Y, O = bank("Y", 2), bank("O", 2)
        SC = [bank("SA"), bank("SB")]

        c_in, w_in, k_in = sem("c_in"), sem("w_in"), [sem(f"k_in{a}") for a in range(2)]
        mix_in, hn_in, y_out = sem("mix_in"), sem("hn_in"), sem("y_out")
        g_in = [sem(f"g_in{r}") for r in range(RING)]
        names = ("pe_wk wk_taken pe_op h_ready r_ready xb_ready pe_xbT xbT_ready pe_sc top_done idx_ready gate_ready "
                 "dot_done diag_ready slot_free pe_res y_free gd_ready ge_ready fr_ready y_ready xbc_ready "
                 "yo_free iT_ready pe_iT last_idx pe_xb last_dot last_ge last_w idle").split()
        S = {n: sem(n) for n in names}
        idle = S["idle"]
        NC_IN = 5
        PART = 32
        STEPS = SLOTS // PART

        block = ctx.enter_context(nc.Block())

        @block.sync
        def _(sp):
            sp.dma_start(ring[:, RING - 1, :], io["keys_T"]).then_inc(c_in, 16)
            for dst, src in ((ident[:], io["ident"]), (gffn[:], io["norm_ffn"].broadcast_to([P, DM])),
                             (gfin[:], io["norm_final"].broadcast_to([P, DM])), (sel[:], io["sel"].rearrange("p (b c) -> p b c", b=NS))):
                sp.dma_start(dst, src).then_inc(c_in, 16)
            for a in range(2):
                sp.dma_start(ring[:, a, 0:DM], io["wq_T"][a * P:(a + 1) * P, :]).then_inc(k_in[a], 16)
            with sp.Fori(1, PH) as h:
                for a in range(2):
                    sp.wait_ge(S["pe_wk"], 2 * h + a - 1)
                    sp.dma_start(ring[:, a, 0:DM], io["wq_T"][bass.ds((h * 2 + a) * P, P), :]).then_inc(k_in[a], 16)
            sp.dma_start(w_out[:], io["w_out"].rearrange("(k p) n -> p k n", p=P)).then_inc(w_in, 16)

            def load_mixed(n):
                if not isinstance(n, int):
                    sp.wait_ge(S["pe_op"], n)
                sp.dma_start(mixT[:], io["mix_scratch"][bass.ds(n, 1)].rearrange("a p k c -> (a p) k c")).then_inc(mix_in, 16)

            def load_input(n):
                if not isinstance(n, int) or n > 0:
                    sp.wait_ge(S["pe_res"], n)
                sp.dma_start(hn[:], io["x_all"][bass.ds((n + 1) * P, P), :]).then_inc(hn_in, 16)

            load_mixed(0)
            load_input(0)
            sp.wait_ge(S["pe_op"], 1)
            sp.dma_start(mixT[:], io["mix_scratch"][1]).then_inc(mix_in, 16)
            load_input(1)
            with sp.Fori(1, NB) as c:
                load_mixed(c + 1)
                sp.wait_ge(S["y_ready"], c)
                sp.dma_start(io["y_p"][bass.ds((c - 1) * P, P), :], yo[:]).then_inc(y_out, 16)
                load_input(c + 1)
                sp.wait_ge(y_out, 16 * c)
                sp.sem_inc(S["yo_free"], 1)
            sp.wait_ge(S["y_ready"], NB)
            sp.dma_start(io["y_p"][(NB - 1) * P:NB * P, :], yo[:]).then_inc(y_out, 16)
            sp.wait_ge(y_out, 16 * NB)
            sp.sem_inc(S["yo_free"], 1)
            sp.wait_ge(S["y_ready"], NB + 1)
            sp.dma_start(io["y_s"], yo[0:NS, :]).then_inc(y_out, 16)
            sp.wait_ge(y_out, 16 * (NB + 1))

        @block.gpsimd
        def _(pool):
            def gather(j, q):
                p, r = q // TOPK, q % RING
                if q % TOPK == 0:
                    pool.wait_ge(S["idx_ready"], 2 * j + p + 1)
                pool.wait_ge(S["slot_free"], PART * j + q + 1)
                standalone(pool, idle)
                pool.indirect_dma_start(ring[:, r, :], None, io["uv"],
                                        bass.IndirectOffsetOnAxis(ap=icur[:, p, q % TOPK:q % TOPK + 1], axis=0),
                                        bounds_check=NEXP - 1, oob_is_err=False).then_inc(g_in[r], 16)

            pool.iota(iota[:], [[1, TOPK]], base=0, channel_multiplier=0,
                      allow_small_or_imprecise_dtypes=True).then_inc(S["iT_ready"], 1)
            with pool.Fori(0, NB * STEPS) as j:
                for q in range(PART):
                    gather(j, q)
            pool.wait_ge(S["last_idx"], 1)
            pool.wait_ge(S["slot_free"], RING + NB * SLOTS)
            for b in range(NS):
                pool.indirect_dma_start(ring[:, b, :], None, io["uv"],
                                        bass.IndirectOffsetOnAxis(ap=ab_T[:, b:b + 1], axis=0),
                                        bounds_check=NEXP - 1, oob_is_err=False).then_inc(g_in[b], 16)

        @block.tensor
        def _(pe):
            def key_weights(h, a):
                pe.wait_ge(k_in[a], 16 * h)
                pe.wait_ge(S["wk_taken"], 2 * h + a - 1)
                for k in range(KT):
                    m = pe.matmul((O, Y)[a][:, k * P:(k + 1) * P], ring[:, a, k * P:(k + 1) * P],
                                  ring[:, RING - 1, bass.ds((h * 2 + (a - 2)) * P, P)], start=True, stop=True)
                m.then_inc(S["pe_wk"], 1)

            def out_projection(k):
                for a in range(2):
                    m = pe.matmul(O[:, a * 512:(a + 1) * 512], mixT[:, k, :], w_out[:, k, a * 512:(a + 1) * 512],
                                  start=(k == 0), stop=(k == KT - 1))
                if k == KT - 1:
                    m.then_inc(S["pe_op"], 1)

            def x_transposes(n):
                pe.wait_ge(S["xb_ready"], n + 1)
                for k in range(KT):
                    m = pe.transpose(O[:, k * P:(k + 1) * P], xbn[:, k * P:(k + 1) * P], ident[:])
                m.then_inc(S["pe_xbT"], 1)

            def scores(n, h, s):
                pe.wait_ge(S["xbT_ready"], n + 1)
                pe.wait_ge(S["top_done"], n * PH + h + 1)
                for k in range(KT):
                    m = pe.matmul(SC[s][:, 0:2 * NKEY], xbT[:, k, :], wk[:, k, bass.ds(h * 2 * NKEY, 2 * NKEY)],
                                  start=(k == 0), stop=(k == KT - 1))
                m.then_inc(S["pe_sc"], 1)

            def residual(c):
                pe.wait_ge(S["xb_ready"], c + 1)
                pe.wait_ge(S["y_free"], c + 1)
                for a in range(2):
                    m = pe.matmul(Y[:, a * 512:(a + 1) * 512], ident[:], hn[:, a * 512:(a + 1) * 512], start=True, stop=False,
                                  skip_group_check=True)
                m.then_inc(S["pe_res"], 1)

            def apply(j, q):
                pe.wait_ge(S["diag_ready"], PART * j + q + 1)
                for a in range(2):
                    m = pe.matmul(Y[:, a * 512:(a + 1) * 512], diag[:, q % DIAGS, :], ring[:, q % RING, DM + a * 512:DM + (a + 1) * 512],
                                  start=False, stop=False, skip_group_check=True)
                m.then_inc(S["slot_free"], 1)

            pe.sem_inc(S["slot_free"], RING)
            pe.sem_inc(S["y_free"], 1)
            pe.sem_inc(S["top_done"], 2)
            pe.wait_ge(c_in, 16 * NC_IN)
            pe.sem_inc(S["wk_taken"], 2)
            with pe.Fori(1, PH + 1) as h:
                for a in range(2):
                    key_weights(h, a)
            pe.wait_ge(w_in, 16)
            pe.wait_ge(mix_in, 16)
            pe.wait_ge(S["wk_taken"], 2 + 2 * PH)
            for k in range(KT):
                out_projection(k)
            x_transposes(0)
            with pe.Fori(0, PH // 2) as j:
                scores(0, 2 * j, 0)
                scores(0, 2 * j + 1, 1)

            with pe.Fori(0, NB) as c:
                residual(c)
                for q in range(PART):
                    if q == 1:
                        pe.wait_ge(mix_in, 16 * c + 32)
                    if 1 <= q <= KT:
                        out_projection(q - 1)
                    if q == 15:
                        x_transposes(c + 1)
                    if q == 18:
                        scores(c + 1, 0, 0)
                    if q == 25:
                        scores(c + 1, 1, 1)
                    apply(c * STEPS, q)
                with pe.Fori(1, STEPS) as j:
                    for q in range(PART):
                        if q == 2:
                            scores(c + 1, 2 * j, 0)
                        if q == 18:
                            scores(c + 1, 2 * j + 1, 1)
                        apply(c * STEPS + j, q)

            pe.wait_ge(S["iT_ready"], 2)
            pe.transpose(SC[0][:, 0:NS], rest[0:NS, 0:P], ident[0:NS, 0:NS])
            pe.transpose(SC[0][:, NS:2 * NS], gate[0:NS].rearrange("p h c -> p (h c)"), ident[0:NS, 0:NS]).then_inc(S["pe_iT"], 1)
            pe.wait_ge(S["y_free"], NB + 1)
            for a in range(2):
                pe.matmul(Y[0:NS, a * 512:(a + 1) * 512], ident[0:NS, 0:NS], hn[0:NS, a * 512:(a + 1) * 512], start=True, stop=False,
                          skip_group_check=True)
            for b in range(NS):
                if b >= 1:
                    pe.wait_ge(S["last_dot"], b)
                for a in range(2):
                    m = pe.matmul(O[:, a * 512:(a + 1) * 512], sel[:, b, :], xbn[0:NS, a * 512:(a + 1) * 512], start=True, stop=True)
                m.then_inc(S["pe_xb"], 1)
            pe.wait_ge(S["last_w"], 1)
            for b in range(NS):
                for a in range(2):
                    m = pe.matmul(Y[0:NS, a * 512:(a + 1) * 512], wd[:, b * NS:(b + 1) * NS], ring[:, b, DM + a * 512:DM + (a + 1) * 512],
                                  start=False, stop=(b == NS - 1), skip_group_check=True)
            m.then_inc(S["slot_free"], 1)

        @block.scalar
        def _(act):
            def norm(n):
                act.wait_ge(S["h_ready"], n + 1)
                act.wait_ge(S["xbc_ready"], n + 1)
                act.activation(xbn[:], hn[:], ACT.Square, accum_out=nrm[:, 0:1])
                act.drain()
                act.preload_act_table_set("natural_log_exp_and_others")
                act.activation(nrm[:, 1:2], nrm[:, 0:1], ACT.Ln, bias=EPS, scale=1.0 / DM)
                act.drain()
                act.activation(nrm[:, 2:3], nrm[:, 1:2], ACT.Exp, scale=-0.5).then_inc(S["r_ready"], 1)

            def take_xbT(n):
                act.wait_ge(S["pe_xbT"], n + 1)
                act.activation(xbT[:].rearrange("p k c -> p (k c)"), O[:], ACT.Copy).then_inc(S["xbT_ready"], 1)

            def weigh(j, q):
                p, k = q // TOPK, q % TOPK
                if k == 0:
                    act.wait_ge(S["gate_ready"], 2 * j + p + 1)
                act.wait_ge(S["dot_done"], PART * j + q + 1)
                act.activation(ge[:, p, k:k + 1], dots[:, p, k:k + 1], ACT.Gelu)
                act.drain()
                act.activation(wt[:, p, k:k + 1], ge[:, p, k:k + 1], ACT.Copy, scale=gcur[:, p, k:k + 1])
                act.drain()
                act.wait_ge(S["slot_free"], PART * j + q + 1 + RING - DIAGS)
                act.activation(diag[:, q % DIAGS, :], ident[:], ACT.Copy, scale=wt[:, p, k:k + 1]).then_inc(S["diag_ready"], 1)

            def gate_exp(n):
                act.preload_act_table_set("natural_log_exp_and_others")
                act.wait_ge(S["gd_ready"], n + 1)
                act.activation(gate[:], gate[:], ACT.Exp).then_inc(S["ge_ready"], 1)

            def final_norm(c, n):
                if isinstance(c, int):
                    act.wait_ge(S["slot_free"], SLOTS * NB + RING + 1)
                else:
                    act.wait_ge(S["slot_free"], SLOTS * c + SLOTS + RING)
                act.wait_ge(S["yo_free"], c + 1)
                act.activation(yo[0:n, :], Y[0:n, :], ACT.Copy).then_inc(S["y_free"], 1)
                act.drain()
                act.activation(junk[0:n, :], yo[0:n, :], ACT.Square, accum_out=nrm[0:n, 3:4])
                act.drain()
                act.preload_act_table_set("natural_log_exp_and_others")
                act.activation(nrm[0:n, 4:5], nrm[0:n, 3:4], ACT.Ln, bias=EPS, scale=1.0 / DM)
                act.drain()
                act.activation(nrm[0:n, 5:6], nrm[0:n, 4:5], ACT.Exp, scale=-0.5).then_inc(S["fr_ready"], 1)

            act.sem_inc(S["yo_free"], 1)
            with act.Fori(1, PH + 1) as h:
                for a in range(2):
                    act.wait_ge(S["pe_wk"], 2 * h + a - 1)
                    act.activation(wk[:, :, bass.ds((h * 2 + (a - 2)) * P, P)], (O, Y)[a][:].rearrange("p (k c) -> p k c", k=KT),
                                   ACT.Copy).then_inc(S["wk_taken"], 1)
            norm(0)
            take_xbT(0)
            gate_exp(0)
            with act.Fori(0, NB) as c:
                for q in range(PART):
                    if q == 11:
                        norm(c + 1)
                    if q == 17:
                        take_xbT(c + 1)
                    weigh(c * STEPS, q)
                with act.Fori(1, STEPS) as j:
                    for q in range(PART):
                        weigh(c * STEPS + j, q)
                gate_exp(c + 1)
                final_norm(c, P)
            act.wait_ge(S["last_dot"], NS)
            act.activation(ge[:, 0, 0:NS], dots[:, 0, 0:NS], ACT.Gelu).then_inc(S["last_ge"], 1)
            final_norm(NB, NS)

        @block.vector
        def _(v):
            def add_residual(n):
                v.wait_ge(hn_in, 16 * n + 16)
                v.wait_ge(S["pe_op"], n + 1)
                v.tensor_tensor(hn[:], hn[:], O[:], ALU.add).then_inc(S["h_ready"], 1)

            def norm(n):
                v.wait_ge(S["r_ready"], n + 1)
                v.scalar_tensor_tensor(out=xbn[:], in0=hn[:], scalar=nrm[:, 2:3], in1=gffn[:], op0=ALU.mult,
                                       op1=ALU.mult).then_inc(S["xb_ready"], 1)

            def top16(vals, nums, src, width):
                tmp = rest[:, 0:width]
                v.max(vals[:, 0:8], src)
                v.drain()
                v.max_index(nums[:, 0:8], vals[:, 0:8], src)
                v.match_replace(tmp, vals[:, 0:8], src, LOW)
                v.drain()
                v.max(vals[:, 8:16], tmp)
                v.drain()
                v.max_index(nums[:, 8:16], vals[:, 8:16], tmp)
                v.drain()

            def choose(n, h, s):
                v.wait_ge(S["pe_sc"], n * PH + h + 1)
                standalone(v, idle)
                for p in range(2):
                    top16(tops[:, p, :], topi[:, p, :], SC[s][:, p * NKEY:(p + 1) * NKEY], NKEY)
                v.tensor_copy(topf[:], topi[:]).then_inc(S["top_done"], 1)
                a0 = tops[:, 0, :].rearrange("p (a b) -> p a b", b=1).broadcast_to([P, TOPK, TOPK])
                v.tensor_tensor(cand[:], a0, tops[:, 1:2, :].broadcast_to([P, TOPK, TOPK]), ALU.add)
                v.drain()
                b16 = pick[:, 0, :]
                top16(b16, bc[:], cand[:].rearrange("p a b -> p (a b)"), TOPK * TOPK)
                v.tensor_copy(best[:, bass.ds(h, 1), :], pick[:, 0:1, :])
                v.tensor_scalar(ab[:, 0, :], bc[:], 4, None, ALU.logical_shift_right)
                v.tensor_scalar(ab[:, 1, :], bc[:], TOPK - 1, None, ALU.bitwise_and)
                v.drain()
                full = [P, 2, TOPK, TOPK]
                v.tensor_tensor(hot[:], ab[:].rearrange("p a (k i) -> p a k i", i=1).broadcast_to(full),
                                iota[:].rearrange("p (a k i) -> p a k i", a=1, k=1).broadcast_to(full), ALU.is_equal)
                v.drain()
                v.tensor_tensor(hot[:], hot[:], topf[:].rearrange("p a (k i) -> p a k i", k=1).broadcast_to(full), ALU.mult)
                v.drain()
                v.tensor_reduce(pick[:], hot[:], AX.X, ALU.add)
                v.drain()
                v.scalar_tensor_tensor(out=idx[:, bass.ds(h, 1), :], in0=pick[:, 0:1, :], scalar=float(NKEY), in1=pick[:, 1:2, :],
                                       op0=ALU.mult, op1=ALU.add)
                v.drain()

            def gates(n):
                v.tensor_tensor(gate[:], best[:], best[:, :, 0:1].broadcast_to([P, PH, TOPK]), ALU.subtract).then_inc(S["gd_ready"], 1)
                v.wait_ge(S["ge_ready"], n + 1)
                v.tensor_reduce(gsum[:, 0, :], gate[:], AX.X, ALU.add)
                v.drain()
                v.reciprocal(gsum[:, 1, :], gsum[:, 0, :])
                v.drain()
                v.tensor_tensor(gate[:], gate[:], gsum[:, 1, :].rearrange("p (h c) -> p h c", c=1).broadcast_to([P, PH, TOPK]), ALU.mult)
                v.drain()

            def next_indices(h, p):
                v.tensor_copy(icur[:, p:p + 1, :], idx[:, bass.ds(h, 1), :]).then_inc(S["idx_ready"], 1)

            def next_gates(h, p):
                v.tensor_copy(gcur[:, p:p + 1, :], gate[:, bass.ds(h, 1), :]).then_inc(S["gate_ready"], 1)

            def dot(j, q):
                r = q % RING
                v.wait_ge(g_in[r], (PART // RING * j + q // RING + 1) * 16)
                v.tensor_tensor_reduce(ring[:, r, 0:DM], ring[:, r, 0:DM], xbc[:], 1.0, 0.0, ALU.mult, ALU.add,
                                       dots[:, q // TOPK, q % TOPK:q % TOPK + 1]).then_inc(S["dot_done"], 1)

            def final_scale(c, n):
                v.wait_ge(S["fr_ready"], c + 1)
                v.scalar_tensor_tensor(out=yo[0:n, :], in0=yo[0:n, :], scalar=nrm[0:n, 5:6], in1=gfin[0:n, :], op0=ALU.mult,
                                       op1=ALU.mult).then_inc(S["y_ready"], 1)

            v.wait_ge(c_in, 16 * NC_IN)
            v.wait_ge(S["iT_ready"], 1)
            v.tensor_copy(gsum[:, 0, :], ident[:, 0:PH]).then_inc(S["xbc_ready"], 1)
            add_residual(0)
            norm(0)
            with v.Fori(0, PH // 2) as j:
                for s in range(2):
                    choose(0, 2 * j + s, s)
            gates(0)
            next_indices(0, 0)

            with v.Fori(0, NB) as c:
                v.drain()
                v.tensor_copy(xbc[:], xbn[:]).then_inc(S["xbc_ready"], 1)
                next_indices(1, 1)
                next_gates(0, 0)
                v.drain()
                for q in range(PART):
                    if q == 16:
                        next_indices(2, 0)
                        next_gates(1, 1)
                        v.drain()
                    dot(c * STEPS, q)
                    if q == 9:
                        add_residual(c + 1)
                    if q == 12:
                        norm(c + 1)
                    if q == 22:
                        choose(c + 1, 0, 0)
                    if q == 29:
                        choose(c + 1, 1, 1)
                with v.Fori(1, STEPS) as j:
                    for q in range(PART):
                        if q == 0:
                            next_indices(2 * j + 1, 1)
                            next_gates(2 * j, 0)
                            v.drain()
                        if q == 16:
                            next_indices((2 * j + 2) % PH, 0)
                            next_gates(2 * j + 1, 1)
                            v.drain()
                        dot(c * STEPS + j, q)
                        if q == 7:
                            choose(c + 1, 2 * j, 0)
                        if q == 23:
                            choose(c + 1, 2 * j + 1, 1)
                gates(c + 1)
                final_scale(c, P)

            v.tensor_copy(rest[0:NS, 0:P], idx[0:NS].rearrange("p h c -> p (h c)")).then_inc(S["iT_ready"], 1)
            v.memset(wd, 0.0)
            v.wait_ge(S["pe_iT"], 1)
            v.tensor_copy(ab_T, SC[0][:, 0:NS])
            v.drain()
            v.tensor_copy(gate_T, SC[0][:, NS:2 * NS]).then_inc(S["last_idx"], 1)
            for b in range(NS):
                v.wait_ge(g_in[b], 16 * (NB * SLOTS // RING + 1))
                v.wait_ge(S["pe_xb"], b + 1)
                v.tensor_tensor_reduce(ring[:, b, 0:DM], ring[:, b, 0:DM], O[:], 1.0, 0.0, ALU.mult, ALU.add,
                                       dots[:, 0, b:b + 1]).then_inc(S["last_dot"], 1)
            v.wait_ge(S["last_ge"], 1)
            v.tensor_tensor(wd[:, 0:NS * NS:NS + 1], ge[:, 0, 0:NS], gate_T, ALU.mult).then_inc(S["last_w"], 1)
            final_scale(NB, NS)


def constants():
    tok = np.arange(P)
    masks = []
    for g in range(LEVELS):
        half = P >> (g + 1)
        same = (tok[:, None] // (2 * half)) == (tok[None, :] // (2 * half))
        masks.append(same & (tok[:, None] % (2 * half) < half) & (tok[None, :] % (2 * half) >= half))
    masks.append(tok[:, None] == tok[None, :])
    inv = np.float32(10000.0) ** (-np.arange(HD // 2, dtype=np.float32) * np.float32(2.0) / np.float32(HD))
    pos = np.arange((NB + 1) * P) - (P - META)
    pos[:NS] = 2048
    ang = pos.astype(np.float32)[:, None] * inv.astype(np.float32)[None, :]
    key, far = np.arange(2 * WIN)[None, :], -1.0e30
    wmask = np.zeros((NB, P, 2 * WIN), np.float32)
    wmask[:] = np.where((key <= tok[:, None] + WIN) & (key >= tok[:, None]), 0.0, far)
    wmask[0, :, 0:P - META] = far
    sel = np.zeros((NS, NS, P), np.float32)
    sel[np.arange(NS), np.arange(NS)] = 1.0
    reset = np.ones((P, HH, P), np.float32)
    reset[:, :, 0] = 0.0
    return {
        "ident": np.eye(P, dtype=np.float32),
        "level_masks": np.concatenate([m.astype(np.int32) for m in masks], axis=1),
        "rope": np.concatenate([np.cos(ang), np.sin(ang)], axis=1).astype(np.float32),
        "wmask": wmask.reshape(NB * P, 2 * WIN),
        "sel": sel.reshape(NS, NS * P),
        "reset": reset.reshape(P, HW),
    }


def lay_out(x_prompt, x_sample, state_hgrn, cache_k, cache_v, meta_tokens, lb_logits, norm_mix, w_in,
            hgrn_norm, attn_sink, w_out, norm_ffn, peer_wq, peer_keys, peer_u, peer_v, norm_final):
    a = {k: np.asarray(v) for k, v in locals().items()}
    tile0 = np.zeros((P, DM), np.float32)
    tile0[:NS] = a["x_sample"].reshape(NS, DM)
    sampled = tile0.copy()
    tile0[P - META:] = a["meta_tokens"]
    return {
        "x_all": np.concatenate([tile0, a["x_prompt"].reshape(NB * P, DM), sampled]),
        "state_s": a["state_hgrn"].reshape(NS * HH, DK, DK),
        "cache_k": a["cache_k"].reshape(NS, WIN, KV * HD),
        "cache_v": a["cache_v"].reshape(NS, WIN, KV * HD),
        "lb_logits": a["lb_logits"].reshape(2, HW),
        "norm_mix": a["norm_mix"].reshape(1, DM),
        "w_in": a["w_in"].reshape(DM, IN_W),
        "hgrn_norm": a["hgrn_norm"].reshape(1, HW),
        "attn_sink": a["attn_sink"].reshape(1, SH),
        "w_out": a["w_out"].reshape(DM, DM),
        "norm_ffn": a["norm_ffn"].reshape(1, DM),
        "wq_T": np.ascontiguousarray(a["peer_wq"].reshape(DM, 2 * PH * NKEY).T),
        "keys_T": np.ascontiguousarray(a["peer_keys"].reshape(2 * PH, NKEY, P).transpose(2, 0, 1).reshape(P, 2 * PH * NKEY)),
        "uv": np.concatenate([a["peer_u"].reshape(NEXP, DM), a["peer_v"].reshape(NEXP, DM)], axis=1),
        "norm_final": a["norm_final"].reshape(1, DM),
        **constants(),
    }


OUTS = {
    "y_p": (NB * P, DM), "y_s": (NS, DM), "new_state_p": (HH, DK, DK), "new_k_p": (WIN, KV * HD), "new_v_p": (WIN, KV * HD),
    "new_state_s": (NS * HH, DK, DK), "new_k_s": (NS, WIN, KV * HD), "new_v_s": (NS, WIN, KV * HD),
}


def program(nc, arrays, debug=False):
    io = {n: nc.dram_tensor(n, a.shape, mybir.dt.from_np(a.dtype), kind="ExternalInput").ap() for n, a in arrays.items()}
    io |= {n: nc.dram_tensor(n, s, F32, kind="ExternalOutput").ap() for n, s in OUTS.items()}
    scratch = {"kind": "ExternalOutput"} if debug else {}
    io["mix_scratch"] = nc.dram_tensor("mix_scratch", [NB + 1, P, KT, P], F32, **scratch).ap()
    mixer_program(nc, io)
    peer_program(nc, io)


def kernel(**inputs):
    from concourse import bacc
    from concourse.bass_utils import run_bass_kernel_spmd

    arrays = lay_out(**inputs)
    nc = bacc.Bacc("TRN2", target_bir_lowering=False, num_devices=1)
    program(nc, arrays)
    r = run_bass_kernel_spmd(nc, [arrays], core_ids=[0]).results[0]
    return (r["y_p"].reshape(1, NB * P, DM), r["y_s"].reshape(NS, 1, DM),
            r["new_state_p"].reshape(1, 1, HH, DK, DK), r["new_k_p"].reshape(1, 1, WIN, KV, HD),
            r["new_v_p"].reshape(1, 1, WIN, KV, HD), r["new_state_s"].reshape(1, NS, HH, DK, DK),
            r["new_k_s"].reshape(1, NS, WIN, KV, HD), r["new_v_s"].reshape(1, NS, WIN, KV, HD))
```

```python
from contextlib import ExitStack

import numpy as np

import concourse.bass as bass
from concourse import mybir

F32 = mybir.dt.float32
U32 = mybir.dt.uint32
I32 = mybir.dt.int32
ALU = mybir.AluOpType
ACT = mybir.ActivationFunctionType
AX = mybir.AxisListType

P = 128
DM = 1024
KT = DM // P
NB = 8
META = 16
NS = 8
HH = 4
DK = 128
HW = HH * DK
SH = 8
KV = 2
HD = 64
GQ = SH // KV
WIN = 128
EPS = 1e-6
SCALE = HD ** -0.5
OFF_Q, OFF_F, OFF_I, OFF_G = 0, HW, 2 * HW, 3 * HW
OFF_AQ, OFF_AK = 4 * HW, 4 * HW + SH * HD
IN_W = OFF_AK + 2 * KV * HD
LEVELS = 7
GRAMS = LEVELS + 1
PH = 8
TOPK = 16
NKEY = 128
NEXP = NKEY * NKEY
SLOTS = PH * TOPK
HALF = PH * NS
SAMP = (PH - 1) * NS
RING = 8
DIAGS = 4
LOW = -3.0e38
WK_W = 2 * PH * NKEY
BLOCKS = 2 * PH
KBUF = 4
OUT_K = KT * (IN_W - WK_W) // DM


def standalone(eng, idle):
    eng.sem_inc(idle, 1)


class Weights:

    def __init__(self, nc, ctx):
        self.all = ctx.enter_context(nc.sbuf_tensor("weights", [P, KT * IN_W], F32))
        self.w_in = self.all[:].rearrange("p (k n) -> p k n", k=KT)
        self.wk = self.all[:, 0:KT * WK_W].rearrange("p (k n) -> p k n", k=KT)
        beside = self.all[:, KT * WK_W:KT * IN_W]
        self.wq = beside[:, 0:KBUF * DM].rearrange("p (a n) -> p a n", a=KBUF)
        self.keys = beside[:, KBUF * DM:KBUF * DM + WK_W]
        self.w_out = beside.rearrange("p (k n) -> p k n", n=DM)
        self.keys_in = ctx.enter_context(nc.semaphore("keys_in"))
        self.k_in = [ctx.enter_context(nc.semaphore(f"k_in{a}")) for a in range(KBUF)]
        self.w_out_in = ctx.enter_context(nc.semaphore("w_out_in"))


def mixer_program(nc, io, weights):
    with ExitStack() as ctx:
        def sb(name, shape, dt=F32):
            return ctx.enter_context(nc.sbuf_tensor("a_" + name, shape, dt))

        def sem(name):
            return ctx.enter_context(nc.semaphore("a_" + name))

        def bank(name):
            return ctx.enter_context(nc.psum_tensor("a_" + name, [P, 512], F32))

        w_in, wk = weights.w_in, weights.wk
        ident = sb("ident", [P, P])
        lmask = sb("lmask", [P, GRAMS, P], I32)
        reset = sb("reset", [P, HH, P])
        gmix = sb("gmix", [P, DM])
        gnorm = sb("gnorm", [P, HW])
        sinkb = sb("sinkb", [P, SH])
        sinkc = sb("sinkc", [SH, 1])
        lbl = sb("lbl", [P, 2, HH])
        lbw = sb("lbw", [P, 4, HH])
        lb, oml = lbw[:, 2, :], lbw[:, 3, :]
        xs = sb("xs", [P, DM])
        xn_all = sb("xn", [P, DM + NS])
        xn = xn_all[:, 0:DM]
        xT = sb("xT", [P, KT, P])
        ss = sb("ss", [P, 3])
        rope = sb("rope", [P, 2, HD // 2])
        wmask = sb("wmask", [P, 2 * WIN])
        ef = sb("ef", [P, HH, P])
        ff = sb("ff", [P, HH, P])
        kk = sb("kk", [P, HH, P])
        qq = sb("qq", [P, HH, P])
        bb = sb("bb", [P, HH, P])
        dd = sb("dd", [P, 2, HH, P])
        mm = sb("mm", [P, 2, HH, P])
        at = sb("at", [P, HH, P])
        eb = sb("eb", [P, HH, P])
        qb = sb("qb", [P, HH, P])
        ket = sb("ket", [P, HH, DK])
        st = sb("st", [P, HH, DK])
        vv = sb("vv", [P, HW])
        gg = sb("gg", [P, 2, HW])
        sjunk = sb("sjunk", [P, HW], mybir.dt.bfloat16)
        rs = sb("rs", [P, 3, HH])
        sq = sb("sq", [P, HH, P])
        qr = sb("qr", [P, HH, P])
        vr = sb("vr", [P, KV * HD])
        mixr = sb("mixr", [P, 2 * 10 * HD])
        mixh, mixa = mixr[:, 0:HW], mixr[:, HW:2 * HW]
        qk = sb("qk", [P, 5, 2, HD])
        rt = mixr[:].rearrange("p (a b c) -> p a b c", a=2, b=10)
        qkr = sb("qkr", [P, 5, 2, HD])
        qT = sb("qT", [P, 4, P])
        kT = sb("kT", [P, 2, WIN])
        va = sb("va", [P, 2, KV * HD])
        sm = sb("sm", [P, SH, 2 * WIN])
        pT = sb("pT", [P, SH, 2, P])
        mx = sb("mx", [P, 6, SH])
        mixT = sb("mixT", [P, KT, P])

        s0 = sb("s0", [P, NS * HH, DK])
        sel = mm[0:NS].rearrange("p a h c -> p (a h) c")
        qd = sb("qd", [P, HH, NS * NS])
        qbd = sb("qbd", [P, NS, SH])
        sx = sb("sx", [SH, 6, NS])
        rn = sb("rn", [NS, NS, SH])
        vnd = sb("vnd", [NS, KV, 2, HD])
        kc = pT[:, 0:4].rearrange("p h a c -> p (h a) c")
        kcT = pT[:, 4:8].rearrange("p h a c -> p (h a) c")
        v2 = sm[:].rearrange("p h c -> p (h c)").rearrange("p (b s r d) -> p b s r d", b=NS, s=KV, r=2)
        sc = xn_all[0:SH, :].rearrange("p (b c) -> p b c", b=NS)
        pTs = qb[:].rearrange("p h c -> p (h c)")[:, 0:NS * SH]

        T0, T1, FA, FB, G0, G1, S0, S1 = (bank(n) for n in ("T0", "T1", "FA", "FB", "G0", "G1", "S0", "S1"))
        OO, DS, OA = S0, S1, G1
        GB = [G0, G1]

        def bank4(b):
            return b[:].rearrange("p (h c) -> p h c", h=4)

        c_in, m_in, w_fq, w_rest = sem("c_in"), sem("m_in"), sem("w_fq"), sem("w_rest")
        x_in, side_in = sem("x_in"), sem("side_in")
        keys_in, k_in = weights.keys_in, weights.k_in
        s_in, mix_out, s_out = sem("s_in"), sem("mix_out"), sem("s_out")
        names = ("r_ready xn_ready pe_xT xT_ready pe_F pe_Q pe_AQ pe_AKV pe_V pe_G ef_ready f_ready lf_ready eq_ready "
                 "q_ready b_ready eb_ready D_ready E_ready M_ready pe_gram A_ready qk_ready rot_ready va_ready pe_qkT qkT_ready "
                 "v_ready eg_ready  pe_S sm_ready m_ready p_ready kd_ready ke_exp ke_ready pe_KET "
                 "ket_ready pe_dS pe_O st_ready rr_ready mixh_ready pe_PT pT_ready pe_Oa mixa_ready pe_mix "
                 "mixT_ready lb_ready sam_ready pe_sam act_sam pe_wk wk_taken idle").split()
        S = {n: sem(n) for n in names}
        idle = S["idle"]
        NC_IN, NM_IN, NS_IN = 3, 5, 7

        block = ctx.enter_context(nc.Block())

        @block.sync
        def _(sp):
            sp.dma_start(xs[:], io["x_all"][0:P, :]).then_inc(x_in, 16)
            w = io["w_in"].rearrange("(k p) n -> p k n", p=P)
            for dst, src in ((ident[:], io["ident"]), (gmix[:], io["norm_mix"].broadcast_to([P, DM])),
                             (lbl[:], io["lb_logits"].rearrange("l (h p) -> p l h", p=P))):
                with nc.allow_non_contiguous_dma(reason="a few small constants"):
                    sp.dma_start(dst, src).then_inc(c_in, 16)
            for k in range(0, KT, 2):
                sp.dma_start(w_in[:, k:k + 2, OFF_Q:OFF_I], w[:, k:k + 2, OFF_Q:OFF_I]).then_inc(w_fq, 16)
            for dst, src in ((reset[:], io["reset"].rearrange("p (h c) -> p h c", h=HH)),
                             (lmask[:], io["level_masks"].rearrange("p (g c) -> p g c", g=GRAMS)),
                             (gnorm[:], io["hgrn_norm"].broadcast_to([P, HW])),
                             (sinkb[:], io["attn_sink"].broadcast_to([P, SH])),
                             (sinkc[:], io["attn_sink"].rearrange("a h -> h a"))):
                with nc.allow_non_contiguous_dma(reason="a few small constants"):
                    sp.dma_start(dst, src).then_inc(m_in, 16)
            for k in range(0, KT, 2):
                sp.dma_start(w_in[:, k:k + 2, OFF_I:IN_W], w[:, k:k + 2, OFF_I:IN_W]).then_inc(w_rest, 16)
            sp.wait_ge(S["xn_ready"], 1)
            sp.dma_start(xs[:], io["x_all"][P:2 * P, :]).then_inc(x_in, 16)
            sp.dma_start(s0[:], io["state_s"].rearrange("n k v -> k n v")).then_inc(s_in, 16)
            sp.dma_start(sel, io["sel"].rearrange("p (b c) -> p b c", b=NS)).then_inc(s_in, 16)
            sp.dma_start(kc, io["cache_k"].rearrange("b w c -> w b c")).then_inc(s_in, 16)
            for s in range(KV):
                for r in range(2):
                    sp.dma_start(v2[:, :, s, r, :], io["cache_v"].rearrange("b w c -> w b c")[:, :, s * HD:(s + 1) * HD]).then_inc(s_in, 16)
            sp.dma_start(rope[:], io["rope"][0:P].rearrange("p (a c) -> p a c", a=2)).then_inc(side_in, 16)
            sp.dma_start(wmask[:], io["wmask"][0:P, :]).then_inc(side_in, 16)
            for dst, src in (("new_k_s", "cache_k"), ("new_v_s", "cache_v")):
                sp.dma_start(io[dst][:, 0:WIN - 1, :], io[src][:, 1:WIN, :]).then_inc(s_out, 16)
            sp.wait_ge(S["rot_ready"], 1)
            sp.dma_start(io["new_k_s"][:, WIN - 1, :], qkr[0:NS, 4, :, :].rearrange("p a c -> p (a c)")).then_inc(s_out, 16)
            sp.wait_ge(S["va_ready"], 1)
            sp.dma_start(io["new_v_s"][:, WIN - 1, :], va[0:NS, 1, :]).then_inc(s_out, 16)
            sp.wait_ge(S["xn_ready"], 2)
            sp.dma_start(xs[:], io["x_all"][2 * P:3 * P, :]).then_inc(x_in, 16)
            sp.wait_ge(S["sam_ready"], 1 + NS)
            sp.dma_start(io["new_state_s"].rearrange("n k v -> k n v"), s0[:]).then_inc(s_out, 16)

            def loads(i, more):
                sp.wait_ge(S["xn_ready"], i + 3)
                sp.dma_start(rope[:], io["rope"][bass.ds((i + 1) * P, P), :].rearrange("p (a c) -> p a c", a=2)).then_inc(side_in, 16)
                sp.dma_start(wmask[:], io["wmask"][bass.ds(i * P, P), :]).then_inc(side_in, 16)
                if more:
                    sp.dma_start(xs[:], io["x_all"][bass.ds((i + 3) * P, P), :]).then_inc(x_in, 16)

            def store(t):
                sp.wait_ge(S["mixT_ready"], t + 1)
                sp.dma_start(io["mix_scratch"][bass.ds(t - 1, 1)].rearrange("a p k c -> (a p) k c"), mixT[:]).then_inc(mix_out, 16)

            loads(0, True)
            sp.wait_ge(S["mixT_ready"], 1)
            sp.dma_start(io["mix_scratch"][NB], mixT[:]).then_inc(mix_out, 16)
            with sp.Fori(1, NB - 1) as i:
                loads(i, True)
                store(i)
            loads(NB - 1, False)
            sp.wait_ge(S["pe_G"], NB + 1)
            sp.dma_start(weights.keys, io["keys_T"]).then_inc(keys_in, 16)
            for i in range(BLOCKS):
                if i >= KBUF:
                    sp.wait_ge(S["pe_wk"], 2 * (i - KBUF) + 2)
                sp.dma_start(weights.wq[:, i % KBUF, :], io["wq_T"][i * P:(i + 1) * P, :]).then_inc(k_in[i % KBUF], 16)
                if i == 2 * KBUF - 1:
                    store(NB - 1)
            sp.wait_ge(S["pe_wk"], 2 * BLOCKS)
            sp.dma_start(weights.w_out, io["w_out"][0:OUT_K * P, :].rearrange("(k p) n -> p k n", p=P)).then_inc(weights.w_out_in, 16)
            store(NB)
            sp.wait_ge(S["st_ready"], NB + 1)
            sp.dma_start(io["new_state_p"].rearrange("h p v -> p h v"), st[:]).then_inc(s_out, 16)
            sp.dma_start(io["new_k_p"], qkr[:, 4, :, :].rearrange("p a c -> p (a c)")).then_inc(s_out, 16)
            sp.dma_start(io["new_v_p"], va[:, 1, :]).then_inc(s_out, 16)
            sp.wait_ge(s_out, 16 * 8)
            sp.wait_ge(mix_out, 16 * (NB + 1))
            sp.wait_ge(x_in, 16 * (NB + 2))

        def sampled_pe(pe, first):
            pe.wait_ge(S["v_ready"], 1)
            pe.wait_ge(s_in, 16 * NS_IN)
            for b in range(NS):
                if b >= 2:
                    pe.wait_ge(S["sam_ready"], b)
                pe.matmul((G0, G1)[b % 2][:], sel[:, b, :], vv[0:NS, :], start=True, stop=True).then_inc(S["pe_sam"], 1)
                if b % 2 == 1:
                    first[b // 2]()
            pe.wait_ge(S["sam_ready"], 1 + NS)
            for h in range(HH):
                for b in range(NS):
                    m = pe.matmul(OO[0:NS, h * P:(h + 1) * P], qd[:, h, b * NS:(b + 1) * NS], s0[:, b * HH + h, :],
                                  start=(b == 0), stop=(b == NS - 1))
            m.then_inc(S["pe_O"], 1)
            for b in range(NS):
                m = pe.transpose((T0, T1)[b // 4][:, (b % 4) * P:(b % 4 + 1) * P], kc[:, b, :], ident[:])
            m.then_inc(S["pe_sam"], 1)
            pe.wait_ge(S["act_sam"], 1)
            for b in range(NS):
                pe.matmul((G0, G1)[b // 4][0:SH, (b % 4) * P:(b % 4 + 1) * P], qbd[:, b, :], kcT[:, b, :], start=True, stop=True)
                m = pe.matmul(S1[0:SH, b:b + 1], qbd[:, b, :], kT[:, 1, b:b + 1], start=True, stop=True)
            m.then_inc(S["pe_sam"], 1)
            first[4]()
            pe.wait_ge(S["sam_ready"], 3 + NS)
            for b in range(NS):
                pe.transpose(T0[:, b * SH:(b + 1) * SH], sc[:, b, 0:WIN], ident[0:SH, 0:SH])
            pe.transpose(T1[0:NS, 0:SH], sc[:, :, WIN], ident[0:SH, 0:SH]).then_inc(S["pe_sam"], 1)
            first[5]()
            pe.wait_ge(S["act_sam"], 3)
            pe.wait_ge(S["sam_ready"], 4 + NS)
            for b in range(NS):
                for s in range(KV):
                    lo = b * SH + s * GQ
                    pe.matmul(G0[:, lo:lo + GQ], v2[:, b, s].rearrange("p r d -> p (r d)"), pTs[:, lo:lo + GQ], start=True, stop=False)
                    m = pe.matmul(G0[:, lo:lo + GQ], vnd[:, s].rearrange("p r d -> p (r d)"), rn[:, b, s * GQ:(s + 1) * GQ],
                                  start=False, stop=True)
            m.then_inc(S["pe_sam"], 1)
            pe.wait_ge(S["mixh_ready"], 1)
            for k in range(4):
                m = pe.transpose(T1[:, 64 + k * NS:64 + (k + 1) * NS], mixh[0:NS, k * P:(k + 1) * P], ident[0:NS, 0:NS])
            m.then_inc(S["pe_mix"], 1)

        def sampled_act(act, readout_norm, take_v, gate_exp):
            readout_norm(0, NS)
            act.wait_ge(S["pe_sam"], NS + 1)
            act.activation(kcT[:, 0:4, :], bank4(T0), ACT.Copy)
            act.activation(kcT[:, 4:8, :], bank4(T1), ACT.Copy).then_inc(S["act_sam"], 1)
            take_v(1)
            act.wait_ge(S["sam_ready"], 2 + NS)
            act.activation(sc, sc, ACT.Exp)
            act.activation(sx[:, 2, :], sx[:, 1, :], ACT.Exp, scale=-1.0, bias=sinkc[:]).then_inc(S["act_sam"], 1)
            act.wait_ge(S["pe_sam"], NS + 3)
            act.activation(pTs, T0[:, 0:NS * SH], ACT.Copy).then_inc(S["act_sam"], 1)
            gate_exp(1)

        def sampled_vector(v, mix_a, forget_gate, query_sigmoid):
            v.memset(qd[:], 0.0)
            v.memset(qbd[:], 0.0)
            v.memset(mixT[:], 0.0)
            v.drain()
            v.tensor_copy(qd[:, :, 0:NS * NS:NS + 1], qq[:, :, 0:NS])
            for s in range(KV):
                lo = HD * s
                v.tensor_copy(qbd[lo:lo + HD, :, s * GQ:(s + 1) * GQ], qT[lo:lo + HD, :, 0:NS].rearrange("p j b -> p b j"))
            v.wait_ge(S["qk_ready"], 1)
            for r in range(2):
                m = v.tensor_copy(vnd[:, :, r, :], va[0:NS, 1, :].rearrange("p (s d) -> p s d", s=KV))
            m.then_inc(S["sam_ready"], 1)
            v.wait_ge(s_in, 16 * NS_IN)
            for b in range(NS):
                for h in range(HH):
                    v.tensor_scalar(s0[:, b * HH + h, :], s0[:, b * HH + h, :], ff[:, h, b:b + 1], None, ALU.mult)
            v.drain()
            for b in range(NS):
                v.wait_ge(S["pe_sam"], b + 1)
                for h in range(HH):
                    m = v.scalar_tensor_tensor(out=s0[:, b * HH + h, :], in0=(G0, G1)[b % 2][:, h * P:(h + 1) * P],
                                               scalar=kk[:, h, b:b + 1], in1=s0[:, b * HH + h, :], op0=ALU.mult, op1=ALU.add)
                m.then_inc(S["sam_ready"], 1)
            forget_gate(1)
            query_sigmoid(1)
            mix_a(0, NS)
            v.wait_ge(S["pe_sam"], NS + 2)
            for a, b in enumerate((G0, G1)):
                v.tensor_scalar(sc[:, 4 * a:4 * a + 4, 0:WIN], bank4(b)[0:SH], SCALE, None, ALU.mult)
            v.tensor_scalar(sc[:, :, WIN], S1[0:SH, 0:NS], SCALE, None, ALU.mult)
            v.drain()
            v.tensor_reduce(sx[:, 0, :], sc, AX.X, ALU.max)
            v.drain()
            v.tensor_scalar(sx[:, 1, :], sx[:, 0, :], sinkc[:], None, ALU.max)
            v.drain()
            v.tensor_tensor(sc, sc, sx[:, 1, :].rearrange("p (b c) -> p b c", c=1).broadcast_to([SH, NS, WIN + 1]),
                            ALU.subtract).then_inc(S["sam_ready"], 1)
            v.wait_ge(S["act_sam"], 2)
            v.tensor_reduce(sx[:, 3, :], sc, AX.X, ALU.add)
            v.drain()
            v.tensor_tensor(sx[:, 4, :], sx[:, 3, :], sx[:, 2, :], ALU.add)
            v.drain()
            v.reciprocal(sx[:, 5, :], sx[:, 4, :])
            v.drain()
            v.tensor_tensor(sc, sc, sx[:, 5, :].rearrange("p (b c) -> p b c", c=1).broadcast_to([SH, NS, WIN + 1]),
                            ALU.mult).then_inc(S["sam_ready"], 1)
            v.wait_ge(S["pe_sam"], NS + 3)
            v.tensor_tensor(rn[:], T1[0:NS, 0:SH].rearrange("p (a h) -> p a h", a=1).broadcast_to([NS, NS, SH]),
                            ident[0:NS, 0:NS].rearrange("p (b a) -> p b a", a=1).broadcast_to([NS, NS, SH]), ALU.mult)\
                .then_inc(S["sam_ready"], 1)
            v.wait_ge(S["pe_sam"], NS + 4)
            for r in range(2):
                lo = HD * r
                v.tensor_copy(mixT[lo:lo + HD, 4:8, SAMP:SAMP + NS],
                              G0[lo:lo + HD, 0:NS * SH].rearrange("p (b j r) -> p r j b", b=NS, r=2)[:, r])
            v.wait_ge(S["pe_mix"], 1)
            v.tensor_copy(mixT[:, 0:4, SAMP:SAMP + NS], T1[:, 64:64 + 4 * NS].rearrange("p (k b) -> p k b", k=4)).then_inc(S["mixT_ready"], 1)
            v.drain()
            v.tensor_copy(sx[:, 0, :], sx[:, 1, :]).then_inc(S["mixa_ready"], 1)

        @block.tensor
        def _(pe):
            def x_transposes(t):
                pe.wait_ge(S["xn_ready"], t + 1)
                for k in range(KT):
                    m = pe.transpose((T0 if k < 4 else T1)[:, (k % 4) * P:(k % 4 + 1) * P], xn[:, k * P:(k + 1) * P], ident[:])
                m.then_inc(S["pe_xT"], 1)

            def feature_projection(out, off, done, heads):
                for h in heads:
                    for k in range(KT):
                        m = pe.matmul(out[:, h * P:(h + 1) * P], w_in[:, k, off + h * P:off + (h + 1) * P], xT[:, k, :],
                                      start=(k == 0), stop=(k == KT - 1))
                if heads[-1] == HH - 1:
                    m.then_inc(done, 1)

            def token_projection(out, off, width, done, part):
                for k in part:
                    m = pe.matmul(out[:, 0:width], xT[:, k, :], w_in[:, k, off:off + width], start=(k == 0), stop=(k == KT - 1))
                if part[-1] == KT - 1:
                    m.then_inc(done, 1)

            def gram(t, g):
                if g < LEVELS:
                    pe.wait_ge(S["M_ready"], LEVELS * (t - 1) + g + 1)
                if g >= 2:
                    pe.wait_ge(S["A_ready"], GRAMS * (t - 1) + g - 1)
                for h in range(HH):
                    a = mm[:, g % 2, h, :] if g < LEVELS else kk[:, h, :]
                    b = mm[:, g % 2, h, :] if g < LEVELS else qq[:, h, :]
                    m = pe.matmul(GB[g % 2][:, h * P:(h + 1) * P], a, b, start=True, stop=True)
                m.then_inc(S["pe_gram"], 1)

            def qk_transposes(t):
                pe.wait_ge(S["rot_ready"], t + 1)
                for j in range(5):
                    m = pe.transpose(T0[:, j * P:(j + 1) * P] if j < 4 else T1[:, 0:P],
                                     qkr[:, j, :, :].rearrange("p a c -> p (a c)"), ident[:])
                m.then_inc(S["pe_qkT"], 1)

            def scores(t, n):
                if n == 0:
                    pe.wait_ge(S["qkT_ready"], t + 1)
                else:
                    pe.wait_ge(S["sm_ready"], 2 * (t - 1) + 1)
                for s, out in enumerate((S0, S1)):
                    for a in range(2):
                        lo = HD * s
                        m = pe.matmul(out[:, a * 256:(a + 1) * 256], qT[lo:lo + HD, 2 * n + a, :],
                                      kT[lo:lo + HD, :, :].rearrange("p a c -> p (a c)"), start=True, stop=True)
                m.then_inc(S["pe_S"], 1)

            def transpose_end_keys(t):
                pe.wait_ge(S["ke_ready"], t + 1)
                for h in range(HH):
                    m = pe.transpose(T0[:, h * P:(h + 1) * P], dd[:, 0, h, :], ident[:])
                m.then_inc(S["pe_KET"], 1)

            def state_products(t):
                pe.wait_ge(S["ket_ready"], t + 1)
                for h in range(HH):
                    m = pe.matmul(DS[:, h * P:(h + 1) * P], ket[:, h, :], vv[:, h * P:(h + 1) * P], start=True, stop=True)
                m.then_inc(S["pe_dS"], 1)

            def readout(t):
                pe.wait_ge(S["A_ready"], GRAMS * t)
                for h in range(HH):
                    pe.matmul(OO[:, h * P:(h + 1) * P], qb[:, h, :], st[:, h, :], start=True, stop=False)
                    m = pe.matmul(OO[:, h * P:(h + 1) * P], at[:, h, :], vv[:, h * P:(h + 1) * P], start=False, stop=True)
                m.then_inc(S["pe_O"], 1)

            def p_transposes(t, n):
                if n == 0:
                    pe.wait_ge(S["p_ready"], t)
                if n >= 2:
                    pe.wait_ge(S["pT_ready"], 4 * (t - 1) + n - 1)
                b = T0 if n % 2 == 0 else T1
                for a in range(4):
                    h, kb = 2 * n + a // 2, a % 2
                    m = pe.transpose(b[:, a * P:(a + 1) * P], sm[:, h, kb * P:(kb + 1) * P], ident[:])
                m.then_inc(S["pe_PT"], 1)

            def values(t):
                pe.wait_ge(S["pT_ready"], 4 * t)
                for h in range(SH):
                    lo = HD * (h // GQ)
                    for kb in range(2):
                        m = pe.matmul(OA[:, h * HD:(h + 1) * HD], pT[:, h, kb, :], va[:, kb, lo:lo + HD],
                                      start=(kb == 0), stop=(kb == 1))
                m.then_inc(S["pe_Oa"], 1)

            def mix_transposes(t):
                pe.wait_ge(S["mixh_ready"], t + 1)
                for k in range(4):
                    pe.transpose(T0[:, k * P:(k + 1) * P], mixh[:, k * P:(k + 1) * P], ident[:])
                pe.wait_ge(S["mixa_ready"], t + 1)
                for k in range(4):
                    m = pe.transpose(T1[:, k * P:(k + 1) * P], mixa[:, k * P:(k + 1) * P], ident[:])
                m.then_inc(S["pe_mix"], 1)

            def project_f(n, heads=range(HH)):
                if heads[0] == 0:
                    pe.wait_ge(S["xT_ready"], n + 1)
                feature_projection(FA, OFF_F, S["pe_F"], heads)

            def project_q(n, heads=range(HH)):
                feature_projection(FB, OFF_Q, S["pe_Q"], heads)

            def project_aq(n, part=range(KT)):
                if part[0] == 0:
                    pe.wait_ge(S["ef_ready"], n + 1)
                token_projection(FA, OFF_AQ, 512, S["pe_AQ"], part)

            def project_akv(n, part=range(KT)):
                if part[0] == 0:
                    pe.wait_ge(S["eq_ready"], n + 1)
                token_projection(FB, OFF_AK, 256, S["pe_AKV"], part)

            def project_v(n, part=range(KT)):
                if part[0] == 0:
                    pe.wait_ge(S["qk_ready"], n + 1)
                token_projection(FA, OFF_I, 512, S["pe_V"], part)

            def project_g(n, part=range(KT)):
                token_projection(FB, OFF_G, 512, S["pe_G"], part)

            def key_weights(i):
                if i == 0:
                    pe.wait_ge(S["v_ready"], NB + 1)
                    pe.wait_ge(S["eg_ready"], NB + 1)
                    pe.wait_ge(keys_in, 16)
                pe.wait_ge(k_in[i % KBUF], 16 * (i // KBUF) + 16)
                for a, out in enumerate((FA, FB)):
                    if i >= 1:
                        pe.wait_ge(S["wk_taken"], 2 * (i - 1) + a + 1)
                    for k in range(4):
                        m = pe.matmul(out[:, k * P:(k + 1) * P], weights.wq[:, i % KBUF, (4 * a + k) * P:(4 * a + k + 1) * P],
                                      weights.keys[:, i * P:(i + 1) * P], start=True, stop=True)
                    m.then_inc(S["pe_wk"], 1)

            def first_q():
                pe.wait_ge(S["eg_ready"], 1)
                project_q(1)

            first = [lambda: project_f(1), first_q, lambda: project_aq(1), lambda: project_akv(1),
                     lambda: project_v(1), lambda: project_g(1)]

            pe.wait_ge(c_in, 16 * NC_IN)
            x_transposes(0)
            pe.wait_ge(w_fq, 64)
            project_f(0)
            project_q(0)
            pe.wait_ge(w_rest, 64)
            project_aq(0)
            project_akv(0)
            project_v(0)
            project_g(0)
            qk_transposes(0)
            pe.wait_ge(S["qkT_ready"], 1)
            transpose_end_keys(0)
            state_products(0)
            x_transposes(1)
            sampled_pe(pe, first)

            def tile(t, behind, ahead):
                if ahead:
                    x_transposes(t + 1)
                pe.wait_ge(S["q_ready"], t + 1)
                gram(t, 0)
                if ahead:
                    pe.wait_ge(S["v_ready"], t + 1)
                    project_f(t + 1, range(0, 1))
                else:
                    key_weights(0)
                if behind:
                    mix_transposes(t - 1)
                if ahead:
                    project_f(t + 1, range(1, 2))
                else:
                    key_weights(1)
                gram(t, 1)
                if ahead:
                    project_f(t + 1, range(2, 4))
                    pe.wait_ge(S["eg_ready"], t + 1)
                    project_q(t + 1, range(0, 1))
                else:
                    key_weights(2)
                    key_weights(3)
                pe.wait_ge(S["mixT_ready"], t)
                qk_transposes(t)
                if ahead:
                    project_q(t + 1, range(1, 2))
                else:
                    key_weights(4)
                gram(t, 2)
                if ahead:
                    project_q(t + 1, range(2, 4))
                else:
                    key_weights(5)
                gram(t, 3)
                scores(t, 0)
                if ahead:
                    project_aq(t + 1, range(0, 4))
                else:
                    key_weights(6)
                    key_weights(7)
                gram(t, 4)
                if ahead:
                    project_aq(t + 1, range(4, 8))
                else:
                    key_weights(8)
                gram(t, 5)
                scores(t, 1)
                if ahead:
                    project_akv(t + 1, range(0, 8))
                else:
                    key_weights(9)
                gram(t, 6)
                if not ahead:
                    key_weights(10)
                gram(t, 7)
                if ahead:
                    project_v(t + 1)
                else:
                    key_weights(11)
                    key_weights(12)
                pe.wait_ge(S["m_ready"], t)
                transpose_end_keys(t)
                if ahead:
                    project_g(t + 1, range(0, 3))
                else:
                    key_weights(13)
                    key_weights(14)
                state_products(t)
                readout(t)
                p_transposes(t, 0)
                p_transposes(t, 1)
                if ahead:
                    project_g(t + 1, range(3, 6))
                else:
                    key_weights(15)
                p_transposes(t, 2)
                p_transposes(t, 3)
                if ahead:
                    project_g(t + 1, range(6, 8))
                values(t)

            tile(1, False, True)
            with pe.Fori(2, NB) as t:
                tile(t, True, True)
            tile(NB, True, False)
            mix_transposes(NB)

        @block.scalar
        def _(act):
            def norm(t):
                act.wait_ge(x_in, 16 * t + 16)
                if not isinstance(t, int) or t > 0:
                    act.wait_ge(S["pe_xT"], t)
                act.activation(xn[:], xs[:], ACT.Square, accum_out=ss[:, 0:1])
                act.drain()
                act.activation(ss[:, 1:2], ss[:, 0:1], ACT.Ln, bias=EPS, scale=1.0 / DM)
                act.drain()
                act.activation(ss[:, 2:3], ss[:, 1:2], ACT.Exp, scale=-0.5).then_inc(S["r_ready"], 1)
                act.drain()

            def take_xT(t):
                act.wait_ge(S["pe_xT"], t + 1)
                act.activation(xT[:, 0:4, :], bank4(T0), ACT.Copy)
                act.activation(xT[:, 4:8, :], bank4(T1), ACT.Copy).then_inc(S["xT_ready"], 1)
                act.drain()

            def forget_exp(n):
                act.wait_ge(S["pe_F"], n + 1)
                act.activation(ef[:], bank4(FA), ACT.Exp, scale=-1.0).then_inc(S["ef_ready"], 1)
                act.drain()

            def forget_log(n):
                act.wait_ge(S["f_ready"], n + 1)
                act.activation(ef[:], ff[:], ACT.Ln).then_inc(S["lf_ready"], 1)
                act.drain()

            def query_exp(n):
                act.wait_ge(S["pe_Q"], n + 1)
                act.activation(qr[:], bank4(FB), ACT.Copy)
                act.activation(sq[:], bank4(FB), ACT.Exp, scale=-1.0).then_inc(S["eq_ready"], 1)
                act.drain()

            def decay(t):
                act.wait_ge(S["b_ready"], t)
                act.activation(eb[:], bb[:], ACT.Exp).then_inc(S["eb_ready"], 1)
                act.drain()

            def level_exp(t, g):
                act.wait_ge(S["D_ready"], LEVELS * (t - 1) + g + 1)
                act.activation(dd[:, g % 2], dd[:, g % 2], ACT.Exp).then_inc(S["E_ready"], 1)
                act.drain()

            def take_aq(n):
                act.wait_ge(S["pe_AQ"], n + 1)
                act.activation(qk[:, 0:4, :, :].rearrange("p j s c -> p s j c"),
                               FA[:].rearrange("p (s j c) -> p s j c", s=2, j=4), ACT.Copy)
                act.drain()

            def take_akv(n):
                act.wait_ge(S["pe_AKV"], n + 1)
                act.activation(qk[:, 4, :, :].rearrange("p s c -> p (s c)"), FB[:, 0:128], ACT.Copy)
                act.activation(vr[:], FB[:, 128:256], ACT.Copy).then_inc(S["qk_ready"], 1)
                act.drain()

            def take_qkT(t):
                act.wait_ge(S["pe_qkT"], t + 1)
                act.activation(qT[:], bank4(T0), ACT.Copy)
                act.activation(kT[:, 1, :], T1[:, 0:P], ACT.Copy).then_inc(S["qkT_ready"], 1)
                act.drain()

            def take_v(t):
                act.wait_ge(S["pe_V"], t + 1)
                act.activation(vv[:], FA[:], ACT.Copy).then_inc(S["v_ready"], 1)
                act.drain()

            def gate_exp(t):
                act.wait_ge(S["pe_G"], t + 1)
                if not isinstance(t, int) or t > 0:
                    act.wait_ge(S["mixh_ready"], t)
                act.activation(gg[:, 1, :], FB[:], ACT.Copy)
                act.activation(gg[:, 0, :], FB[:], ACT.Exp, scale=-1.0).then_inc(S["eg_ready"], 1)
                act.drain()

            def end_decay(t):
                act.wait_ge(S["kd_ready"], t + 1)
                act.activation(dd[:, 1], dd[:, 1], ACT.Exp).then_inc(S["ke_exp"], 1)
                act.wait_ge(S["pe_KET"], t + 1)
                act.activation(ket[:], bank4(T0), ACT.Copy).then_inc(S["ket_ready"], 1)
                act.drain()

            def softmax(t):
                act.wait_ge(S["m_ready"], t)
                for h in range(SH):
                    act.activation(sm[:, h, :], sm[:, h, :], ACT.Exp, bias=mx[:, 2, h:h + 1], accum_out=mx[:, 3, h:h + 1])
                act.activation(mx[:, 4, :], mx[:, 4, :], ACT.Exp).then_inc(S["p_ready"], 1)
                act.drain()

            def readout_norm(t, n):
                act.wait_ge(S["pe_O"], t + 1)
                for h in range(HH):
                    act.activation(sjunk[0:n, h * P:(h + 1) * P], OO[0:n, h * P:(h + 1) * P], ACT.Square,
                                   accum_out=rs[0:n, 0, h:h + 1])
                act.drain()
                act.activation(rs[0:n, 1, :], rs[0:n, 0, :], ACT.Ln, bias=EPS, scale=1.0 / DK)
                act.drain()
                act.activation(rs[0:n, 2, :], rs[0:n, 1, :], ACT.Exp, scale=-0.5).then_inc(S["rr_ready"], 1)
                act.drain()

            def take_pT(t, n):
                act.wait_ge(S["pe_PT"], 4 * (t - 1) + n + 1)
                act.activation(pT[:, 2 * n:2 * n + 2, :, :].rearrange("p h a c -> p (h a) c"),
                               bank4(T0 if n % 2 == 0 else T1), ACT.Copy).then_inc(S["pT_ready"], 1)
                act.drain()

            def take_mix(t):
                act.wait_ge(S["pe_mix"], t + 1)
                act.wait_ge(mix_out, 16 * t)
                act.activation(mixT[:, 0:4, :], bank4(T0), ACT.Copy)
                act.activation(mixT[:, 4:8, :], bank4(T1), ACT.Copy).then_inc(S["mixT_ready"], 1)
                act.drain()

            def take_wk(i):
                for a, b in enumerate((FA, FB)):
                    act.wait_ge(S["pe_wk"], 2 * i + a + 1)
                    act.activation(wk[:, 4 * a:4 * a + 4, i * P:(i + 1) * P], bank4(b), ACT.Copy).then_inc(S["wk_taken"], 1)

            act.preload_act_table_set("natural_log_exp_and_others")
            act.wait_ge(c_in, 16 * NC_IN)
            act.wait_ge(S["lb_ready"], 1)
            act.activation(lbw[:, 0:2, :], lbw[:, 0:2, :], ACT.Exp).then_inc(S["lb_ready"], 1)
            norm(0)
            take_xT(0)
            forget_exp(0)
            query_exp(0)
            forget_log(0)
            take_aq(0)
            take_akv(0)
            take_v(0)
            gate_exp(0)
            take_qkT(0)
            end_decay(0)
            norm(1)
            take_xT(1)
            forget_exp(1)
            query_exp(1)
            take_aq(1)
            take_akv(1)
            forget_log(1)
            act.wait_ge(m_in, 16 * NM_IN)
            sampled_act(act, readout_norm, take_v, gate_exp)
            act.wait_ge(S["mixa_ready"], 1)
            norm(2)

            def tile(t, behind, ahead):
                def beside_last(*blocks):
                    if not ahead:
                        for i in blocks:
                            take_wk(i)

                level_exp(t, 0)
                level_exp(t, 1)
                if ahead:
                    take_xT(t + 1)
                level_exp(t, 2)
                if ahead:
                    act.wait_ge(S["b_ready"], t)
                    forget_exp(t + 1)
                beside_last(0)
                if behind:
                    take_mix(t - 1)
                beside_last(1, 2, 3)
                take_qkT(t)
                level_exp(t, 3)
                if ahead:
                    forget_log(t + 1)
                beside_last(4)
                level_exp(t, 4)
                beside_last(5)
                decay(t)
                if ahead:
                    query_exp(t + 1)
                level_exp(t, 5)
                if ahead:
                    take_aq(t + 1)
                beside_last(6, 7)
                level_exp(t, 6)
                if ahead:
                    take_akv(t + 1)
                beside_last(8, 9, 10, 11, 12)
                softmax(t)
                end_decay(t)
                beside_last(13, 14)
                if ahead:
                    norm(t + 2)
                readout_norm(t, P)
                if ahead:
                    take_v(t + 1)
                take_pT(t, 0)
                take_pT(t, 1)
                beside_last(15)
                take_pT(t, 2)
                take_pT(t, 3)
                if ahead:
                    gate_exp(t + 1)

            tile(1, False, True)
            with act.Fori(2, NB) as t:
                tile(t, True, True)
            tile(NB, True, False)
            take_mix(NB)

        @block.vector
        def _(v):
            def norm(t):
                v.wait_ge(S["r_ready"], t + 1)
                v.scalar_tensor_tensor(out=xn[:], in0=xs[:], scalar=ss[:, 2:3], in1=gmix[:], op0=ALU.mult,
                                       op1=ALU.mult).then_inc(S["xn_ready"], 1)
                v.drain()

            def forget_gate(n):
                v.wait_ge(S["ef_ready"], n + 1)
                v.tensor_scalar(ef[:], ef[:], 1.0, None, ALU.add)
                v.drain()
                v.reciprocal(ff[:], ef[:])
                v.drain()
                for h in range(HH):
                    m = v.tensor_scalar(ff[:, h, :], ff[:, h, :], oml[:, h:h + 1], lb[:, h:h + 1], ALU.mult, ALU.add)
                m.then_inc(S["f_ready"], 1)
                v.drain()

            def query_sigmoid(n):
                v.wait_ge(S["eq_ready"], n + 1)
                v.tensor_scalar(sq[:], sq[:], 1.0, None, ALU.add)
                v.drain()
                v.reciprocal(sq[:], sq[:])
                v.drain()

            def features(t):
                v.tensor_scalar(kk[:], ff[:], -1.0, 1.0, ALU.mult, ALU.add)
                v.tensor_tensor(qq[:], sq[:], qr[:], ALU.mult).then_inc(S["q_ready"], 1)
                v.drain()

            def take_values(t):
                v.wait_ge(S["qk_ready"], t + 1)
                v.tensor_copy(va[:, 1, :], vr[:]).then_inc(S["va_ready"], 1)
                v.drain()

            def cumulate(t):
                v.wait_ge(S["lf_ready"], t + 1)
                v.tensor_tensor_scan(bb[:].rearrange("p h c -> p (h c)"), reset[:].rearrange("p h c -> p (h c)"),
                                     ef[:].rearrange("p h c -> p (h c)"), 0.0, ALU.mult, ALU.add).then_inc(S["b_ready"], 1)
                v.drain()

            def halves(x, g):
                half = P >> (g + 1)
                y = x.rearrange("p h c -> p (h c)").rearrange("p (n a c) -> p n a c", a=2, c=half)
                return y[:, :, 0, :], y[:, :, 1, :], half

            def level_gap(t, g):
                bl, br, half = halves(bb[:], g)
                dl, dr, _ = halves(dd[:, g % 2], g)
                mid = bl[:, :, half - 1:half].broadcast_to([P, bl.shape[1], half])
                v.tensor_tensor(dl, mid, bl, ALU.subtract)
                v.tensor_tensor(dr, br, mid, ALU.subtract).then_inc(S["D_ready"], 1)
                v.drain()

            def level_operands(t, g):
                v.wait_ge(S["E_ready"], LEVELS * (t - 1) + g + 1)
                if g >= 2:
                    v.wait_ge(S["pe_gram"], GRAMS * (t - 1) + g - 1)
                el, er, _ = halves(dd[:, g % 2], g)
                kl, _, _ = halves(kk[:], g)
                _, qr, _ = halves(qq[:], g)
                ml, mr, _ = halves(mm[:, g % 2], g)
                v.tensor_tensor(ml, el, kl, ALU.mult)
                v.tensor_tensor(mr, er, qr, ALU.mult).then_inc(S["M_ready"], 1)
                v.drain()

            def level_take(t, g):
                v.wait_ge(S["pe_gram"], GRAMS * (t - 1) + g + 1)
                mask = lmask[:, g:g + 1, :].broadcast_to([P, HH, P])
                if g == 0:
                    v.tensor_tensor(at[:], bank4(GB[0]), mask, ALU.mult).then_inc(S["A_ready"], 1)
                else:
                    standalone(v, idle)
                    v.copy_predicated(at[:], mask, bank4(GB[g % 2])).then_inc(S["A_ready"], 1)
                v.drain()

            def rotate(t):
                v.wait_ge(S["qk_ready"], t + 1)
                if not isinstance(t, int) or t > 0:
                    v.wait_ge(S["pe_mix"], t)
                v.wait_ge(side_in, 32 * t + 32)
                x = qk[:].rearrange("p j s c -> p (j s) c")
                lo, hi = x[:, :, 0:32], x[:, :, 32:64]
                o = qkr[:].rearrange("p j s c -> p (j s) c")
                cos, sin = (rope[:, a:a + 1, :].broadcast_to([P, 10, 32]) for a in (0, 1))
                v.tensor_tensor(rt[:, 0, :, 0:32], lo, cos, ALU.mult)
                v.tensor_tensor(rt[:, 0, :, 32:64], hi, cos, ALU.mult)
                v.tensor_tensor(rt[:, 1, :, 0:32], hi, sin, ALU.mult)
                v.tensor_tensor(rt[:, 1, :, 32:64], lo, sin, ALU.mult)
                v.drain()
                v.tensor_tensor(o[:, :, 0:32], rt[:, 0, :, 0:32], rt[:, 1, :, 0:32], ALU.subtract)
                v.tensor_tensor(o[:, :, 32:64], rt[:, 0, :, 32:64], rt[:, 1, :, 32:64], ALU.add).then_inc(S["rot_ready"], 1)
                v.drain()

            def mask_scores(t, n):
                v.wait_ge(S["pe_S"], 2 * (t - 1) + n + 1)
                for s, b in enumerate((S0, S1)):
                    h = GQ * s + 2 * n
                    m = v.scalar_tensor_tensor(out=sm[:, h:h + 2, :], in0=b[:].rearrange("p (a c) -> p a c", a=2), scalar=SCALE,
                                               in1=wmask[:].rearrange("p (a c) -> p a c", a=1).broadcast_to([P, 2, 2 * WIN]),
                                               op0=ALU.mult, op1=ALU.add)
                m.then_inc(S["sm_ready"], 1)
                v.drain()

            def row_max(t):
                v.drain()
                v.tensor_reduce(mx[:, 0, :], sm[:], AX.X, ALU.max)
                v.drain()
                v.tensor_tensor(mx[:, 1, :], mx[:, 0, :], sinkb[:], ALU.max)
                v.drain()
                v.tensor_scalar(mx[:, 2, :], mx[:, 1, :], -1.0, None, ALU.mult)
                v.tensor_tensor(mx[:, 4, :], sinkb[:], mx[:, 1, :], ALU.subtract).then_inc(S["m_ready"], 1)
                v.drain()

            def end_gap(t):
                v.tensor_tensor(dd[:, 1], bb[:, :, P - 1:P].broadcast_to([P, HH, P]), bb[:], ALU.subtract).then_inc(S["kd_ready"], 1)
                v.drain()

            def query_decay(t):
                v.wait_ge(S["eb_ready"], t)
                v.tensor_tensor(qb[:], qq[:], eb[:], ALU.mult)
                v.drain()

            def end_keys(t):
                v.wait_ge(S["ke_exp"], t + 1)
                v.tensor_tensor(dd[:, 0], kk[:], dd[:, 1], ALU.mult).then_inc(S["ke_ready"], 1)
                v.drain()

            def gate(t):
                v.wait_ge(S["eg_ready"], t + 1)
                v.tensor_scalar(gg[:, 0, :], gg[:, 0, :], 1.0, None, ALU.add)
                v.tensor_tensor(gg[:, 1, :], gg[:, 1, :], gnorm[:], ALU.mult)
                v.drain()
                v.reciprocal(gg[:, 0, :], gg[:, 0, :])
                v.drain()
                v.tensor_tensor(gg[:, 1, :], gg[:, 1, :], gg[:, 0, :], ALU.mult)
                v.drain()

            def new_state(t):
                v.wait_ge(S["pe_dS"], t + 1)
                v.wait_ge(S["pe_O"], t + 1)
                for h in range(HH):
                    m = v.scalar_tensor_tensor(out=st[:, h, :], in0=st[:, h, :], scalar=eb[:, h, P - 1:P],
                                               in1=DS[:, h * P:(h + 1) * P], op0=ALU.mult, op1=ALU.add)
                m.then_inc(S["st_ready"], 1)
                v.drain()

            def mix_a(t, n):
                v.wait_ge(S["rr_ready"], t + 1)
                for h in range(HH):
                    m = v.scalar_tensor_tensor(out=mixh[0:n, h * P:(h + 1) * P], in0=OO[0:n, h * P:(h + 1) * P],
                                               scalar=rs[0:n, 2, h:h + 1], in1=gg[0:n, 1, h * P:(h + 1) * P],
                                               op0=ALU.mult, op1=ALU.mult)
                m.then_inc(S["mixh_ready"], 1)
                v.drain()

            def mix_b(t):
                v.wait_ge(S["p_ready"], t)
                v.tensor_tensor(mx[:, 5, :], mx[:, 3, :], mx[:, 4, :], ALU.add)
                v.drain()
                v.reciprocal(mx[:, 0, :], mx[:, 5, :])
                v.drain()
                v.wait_ge(S["pe_Oa"], t)
                v.tensor_tensor(mixa.rearrange("p (h c) -> p h c", h=SH), OA[:].rearrange("p (h c) -> p h c", h=SH),
                                mx[:, 0, :].rearrange("p (h c) -> p h c", c=1).broadcast_to([P, SH, HD]), ALU.mult).then_inc(S["mixa_ready"], 1)
                v.tensor_copy(kT[:, 0, :], kT[:, 1, :])
                v.tensor_copy(va[:, 0, :], va[:, 1, :])
                v.drain()

            v.wait_ge(c_in, 16 * NC_IN)
            v.tensor_tensor(lbw[:, 2, :], lbl[:, 0, :], lbl[:, 1, :], ALU.max)
            v.drain()
            v.tensor_tensor(lbw[:, 0:2, :], lbl[:], lbw[:, 2:3, :].broadcast_to([P, 2, HH]), ALU.subtract).then_inc(S["lb_ready"], 1)
            v.wait_ge(S["lb_ready"], 2)
            v.tensor_tensor(lbw[:, 1, :], lbw[:, 0, :], lbw[:, 1, :], ALU.add)
            v.drain()
            v.reciprocal(lbw[:, 3, :], lbw[:, 1, :])
            v.drain()
            v.tensor_tensor(lb, lbw[:, 0, :], lbw[:, 3, :], ALU.mult)
            v.drain()
            v.tensor_scalar(oml, lb, -1.0, 1.0, ALU.mult, ALU.add)
            norm(0)
            forget_gate(0)
            query_sigmoid(0)
            features(0)
            take_values(0)
            v.wait_ge(S["lf_ready"], 1)
            v.memset(bb[:], 0.0)
            v.memset(ef[:, :, 0:P - META], 0.0)
            v.wait_ge(m_in, 16 * NM_IN)
            v.drain()
            v.tensor_tensor_scan(bb[:].rearrange("p h c -> p (h c)"), reset[:].rearrange("p h c -> p (h c)"),
                                 ef[:].rearrange("p h c -> p (h c)"), 0.0, ALU.mult, ALU.add)
            v.drain()
            end_gap(0)
            rotate(0)
            v.wait_ge(S["ke_exp"], 1)
            v.memset(dd[:, 0, :, 0:P - META], 0.0)
            v.tensor_tensor(dd[:, 0, :, P - META:P], kk[:, :, P - META:P], dd[:, 1, :, P - META:P], ALU.mult).then_inc(S["ke_ready"], 1)
            gate(0)
            norm(1)
            v.wait_ge(S["pe_dS"], 1)
            v.tensor_copy(st[:], bank4(DS)).then_inc(S["st_ready"], 1)
            v.wait_ge(S["qkT_ready"], 1)
            v.tensor_copy(kT[:, 0, :], kT[:, 1, :])
            v.tensor_copy(va[:, 0, :], va[:, 1, :])
            sampled_vector(v, mix_a, forget_gate, query_sigmoid)

            norm(2)

            def tile(t, behind, ahead):
                features(t)
                cumulate(t)
                level_gap(t, 0)
                level_gap(t, 1)
                level_operands(t, 0)
                if behind:
                    mix_b(t - 1)
                take_values(t)
                level_gap(t, 2)
                level_operands(t, 1)
                level_take(t, 0)
                rotate(t)
                level_gap(t, 3)
                level_operands(t, 2)
                if ahead:
                    forget_gate(t + 1)
                level_take(t, 1)
                level_gap(t, 4)
                level_operands(t, 3)
                level_take(t, 2)
                mask_scores(t, 0)
                level_gap(t, 5)
                level_operands(t, 4)
                level_take(t, 3)
                level_gap(t, 6)
                level_operands(t, 5)
                level_take(t, 4)
                level_operands(t, 6)
                if ahead:
                    query_sigmoid(t + 1)
                mask_scores(t, 1)
                level_take(t, 5)
                row_max(t)
                end_gap(t)
                query_decay(t)
                level_take(t, 6)
                level_take(t, 7)
                end_keys(t)
                if ahead:
                    norm(t + 2)
                gate(t)
                new_state(t)
                mix_a(t, P)

            tile(1, False, True)
            with v.Fori(2, NB) as t:
                tile(t, True, True)
            tile(NB, True, False)
            mix_b(NB)


def peer_program(nc, io, weights):
    with ExitStack() as ctx:
        def sb(name, shape, dt=F32):
            return ctx.enter_context(nc.sbuf_tensor("b_" + name, shape, dt))

        def sem(name):
            return ctx.enter_context(nc.semaphore("b_" + name))

        def bank(name, n=1):
            return ctx.enter_context(nc.psum_tensor("b_" + name, [P, 512 * n], F32))

        wk = weights.wk
        w_rest = sb("w_rest", [P, KT - OUT_K, DM])
        ring = sb("ring", [P, RING, 2 * DM])
        ident = sb("ident", [P, P])
        gffn = sb("gffn", [P, DM])
        gfin = sb("gfin", [P, DM])
        mixT = sb("mixT", [P, KT, P])
        hn = sb("hn", [P, DM])
        xbn = sb("xbn", [P, DM])
        xbT = sb("xbT", [P, KT, P])
        xbc = sb("xbc", [P, DM])
        yo = sb("yo", [P, DM])
        junk = sb("junk", [P, DM], mybir.dt.bfloat16)
        diag = sb("diag", [P, DIAGS, P])
        dots = sb("dots", [P, 2, TOPK])
        ge = sb("ge", [P, 2, TOPK])
        wt = sb("wt", [P, 2, TOPK])
        nrm = sb("nrm", [P, 6])
        tops = sb("tops", [P, 2, TOPK])
        topi = sb("topi", [P, 2, TOPK], U32)
        topf = sb("topf", [P, 2, TOPK])
        rest = sb("rest", [P, 256])
        cand = sb("cand", [P, TOPK, TOPK])
        bc = sb("bc", [P, TOPK], U32)
        ab = sb("ab", [P, 2, TOPK], U32)
        hot = sb("hot", [P, 2, TOPK, TOPK])
        pick = sb("pick", [P, 2, TOPK])
        iota = sb("iota", [P, TOPK])
        best = sb("best", [P, 2, TOPK])
        idx = sb("idx", [P, 2, TOPK], U32)
        gate = sb("gate", [P, 2, TOPK])
        gsum = sb("gsum", [P, 2, 2])
        icur = sb("icur", [P, 2, TOPK], U32)
        gcur = sb("gcur", [P, 2, TOPK])
        spread = sb("spread", [P, 2 * PH, NS])
        unite = sb("unite", [P, NS])
        twice = sb("twice", [HALF, 2, HALF])
        chosen = sb("chosen", [HALF, TOPK])

        Y, O = bank("Y", 2), bank("O", 2)
        SC = [bank("SA"), bank("SB")]

        c_in, w_rest_in = sem("c_in"), sem("w_rest_in")
        mix_in, hn_in, y_out = sem("mix_in"), sem("hn_in"), sem("y_out")
        g_in = [sem(f"g_in{r}") for r in range(RING)]
        names = ("pe_op h_ready r_ready xb_ready pe_xbT xbT_ready pe_sc top_done idx_ready gate_ready "
                 "dot_done diag_ready slot_free pe_res y_free gd_ready ge_ready fr_ready y_ready xbc_ready "
                 "yo_free iota_ready pe_spread pair_ready pe_pair idle").split()
        S = {n: sem(n) for n in names}
        idle = S["idle"]
        NC_IN = 3
        PART = 32
        STEPS = SLOTS // PART
        LAST = NB * STEPS

        block = ctx.enter_context(nc.Block())

        @block.sync
        def _(sp):
            def load_mixed(n):
                if not isinstance(n, int):
                    sp.wait_ge(S["pe_op"], n)
                sp.dma_start(mixT[:], io["mix_scratch"][bass.ds(n, 1)].rearrange("a p k c -> (a p) k c")).then_inc(mix_in, 16)

            def load_input(n):
                if not isinstance(n, int) or n > 0:
                    sp.wait_ge(S["pe_res"], n)
                sp.dma_start(hn[:], io["x_all"][bass.ds((n + 1) * P, P), :]).then_inc(hn_in, 16)

            load_mixed(0)
            sp.dma_start(w_rest[:], io["w_out"][OUT_K * P:, :].rearrange("(k p) n -> p k n", p=P)).then_inc(w_rest_in, 16)
            load_input(0)
            for dst, src in ((ident[:], io["ident"]), (gffn[:], io["norm_ffn"].broadcast_to([P, DM])),
                             (gfin[:], io["norm_final"].broadcast_to([P, DM]))):
                sp.dma_start(dst, src).then_inc(c_in, 16)
            sp.wait_ge(S["pe_op"], 1)
            sp.dma_start(mixT[:], io["mix_scratch"][1]).then_inc(mix_in, 16)
            load_input(1)
            with sp.Fori(1, NB) as c:
                load_mixed(c + 1)
                sp.wait_ge(S["y_ready"], c)
                sp.dma_start(io["y_p"][bass.ds((c - 1) * P, P), :], yo[:]).then_inc(y_out, 16)
                load_input(c + 1)
                sp.wait_ge(y_out, 16 * c)
                sp.sem_inc(S["yo_free"], 1)
            sp.wait_ge(S["y_ready"], NB)
            sp.dma_start(io["y_p"][(NB - 1) * P:NB * P, :], yo[:]).then_inc(y_out, 16)
            sp.wait_ge(y_out, 16 * NB)
            sp.sem_inc(S["yo_free"], 1)
            sp.wait_ge(S["y_ready"], NB + 1)
            sp.dma_start(io["y_s"], yo[0:NS, :]).then_inc(y_out, 16)
            sp.wait_ge(y_out, 16 * (NB + 1))

        @block.gpsimd
        def _(pool):
            def gather(s, q):
                p, r = q // TOPK, q % RING
                if q % TOPK == 0:
                    pool.wait_ge(S["idx_ready"], 2 * s + p + 1)
                pool.wait_ge(S["slot_free"], PART * s + q + 1)
                standalone(pool, idle)
                pool.indirect_dma_start(ring[:, r, :], None, io["uv"],
                                        bass.IndirectOffsetOnAxis(ap=icur[:, p, q % TOPK:q % TOPK + 1], axis=0),
                                        bounds_check=NEXP - 1, oob_is_err=False).then_inc(g_in[r], 16)

            pool.iota(iota[:], [[1, TOPK]], base=0, channel_multiplier=0,
                      allow_small_or_imprecise_dtypes=True).then_inc(S["iota_ready"], 1)
            with pool.Fori(0, LAST) as s:
                for q in range(PART):
                    gather(s, q)
            for q in range(TOPK // 2):
                gather(LAST, q)

        @block.tensor
        def _(pe):
            def out_projection(k):
                w = weights.w_out[:, k] if k < OUT_K else w_rest[:, k - OUT_K]
                for a in range(2):
                    m = pe.matmul(O[:, a * 512:(a + 1) * 512], mixT[:, k, :], w[:, a * 512:(a + 1) * 512],
                                  start=(k == 0), stop=(k == KT - 1))
                if k == KT - 1:
                    m.then_inc(S["pe_op"], 1)

            def x_transposes(n):
                pe.wait_ge(S["xb_ready"], n + 1)
                for k in range(KT):
                    m = pe.transpose(O[:, k * P:(k + 1) * P], xbn[:, k * P:(k + 1) * P], ident[:])
                m.then_inc(S["pe_xbT"], 1)

            def scores(n, m, slot, h):
                pe.wait_ge(S["xbT_ready"], n + 1)
                pe.wait_ge(S["top_done"], m + 1)
                for k in range(KT):
                    t = pe.matmul(SC[slot][:, 0:2 * NKEY], xbT[:, k, :], wk[:, k, bass.ds(h * 2 * NKEY, 2 * NKEY)],
                                  start=(k == 0), stop=(k == KT - 1))
                t.then_inc(S["pe_sc"], 1)

            def sampled_scores(h, lo, hi):
                if h == 0 and lo == 0:
                    pe.wait_ge(S["xbT_ready"], NB + 1)
                    pe.wait_ge(S["top_done"], 2 * LAST + 1)
                for k in range(lo, hi):
                    t = pe.matmul(SC[0][0:PH * NS, 0:2 * NKEY], xbT[:, k, SAMP - h * NS:SAMP - h * NS + PH * NS],
                                  wk[:, k, h * 2 * NKEY:(h + 1) * 2 * NKEY], start=(h == 0 and k == 0), stop=(h == PH - 1 and k == KT - 1))
                if h == PH - 1 and hi == KT:
                    t.then_inc(S["pe_sc"], 1)

            def residual(c):
                pe.wait_ge(S["xb_ready"], c + 1)
                pe.wait_ge(S["y_free"], c + 1)
                for a in range(2):
                    m = pe.matmul(Y[:, a * 512:(a + 1) * 512], ident[:], hn[:, a * 512:(a + 1) * 512], start=True, stop=False,
                                  skip_group_check=True)
                m.then_inc(S["pe_res"], 1)

            def apply(s, q):
                pe.wait_ge(S["diag_ready"], PART * s + q + 1)
                for a in range(2):
                    m = pe.matmul(Y[:, a * 512:(a + 1) * 512], diag[:, q % DIAGS, :], ring[:, q % RING, DM + a * 512:DM + (a + 1) * 512],
                                  start=False, stop=False, skip_group_check=True)
                m.then_inc(S["slot_free"], 1)

            def step(c, j):
                s = c * STEPS + j
                for q in range(PART):
                    if q == 2:
                        scores(c, 2 * s + 2, 0, 2 * j + 2)
                    if q == 18:
                        scores(c, 2 * s + 3, 1, 2 * j + 3)
                    apply(s, q)

            def copy_down(n, x):
                pe.wait_ge(S["pair_ready"], n + 1)
                pe.matmul(SC[1][:, n * TOPK:(n + 1) * TOPK], twice[:].rearrange("p a b -> p (a b)"), x, start=True, stop=True)\
                    .then_inc(S["pe_pair"], 1)

            def last_step(c, sampled):
                s = c * STEPS + STEPS - 1
                for q in range(PART):
                    if q == 0:
                        pe.wait_ge(mix_in, 16 * c + 32)
                    if 2 * q < KT:
                        out_projection(2 * q)
                        out_projection(2 * q + 1)
                    if q == 9:
                        x_transposes(c + 1)
                    if sampled and 12 <= q < 12 + 2 * PH:
                        sampled_scores((q - 12) // 2, (q % 2) * (KT // 2), (q % 2 + 1) * (KT // 2))
                    if not sampled and q == 12:
                        scores(c + 1, 2 * s + 2, 0, 0)
                    if not sampled and q == 14:
                        scores(c + 1, 2 * s + 3, 1, 1)
                    if sampled and q == PART - 1:
                        copy_down(0, chosen[:])
                    apply(s, q)

            pe.sem_inc(S["slot_free"], RING)
            pe.sem_inc(S["y_free"], 1)
            pe.sem_inc(S["top_done"], 2)
            pe.wait_ge(mix_in, 16)
            pe.wait_ge(weights.w_out_in, 16)
            for k in range(OUT_K):
                out_projection(k)
            pe.wait_ge(w_rest_in, 16)
            for k in range(OUT_K, KT):
                out_projection(k)
            pe.wait_ge(c_in, 16 * NC_IN)
            x_transposes(0)
            scores(0, 0, 0, 0)
            scores(0, 1, 1, 1)

            with pe.Fori(0, NB - 1) as c:
                residual(c)
                with pe.Fori(0, STEPS - 1) as j:
                    step(c, j)
                last_step(c, False)
            residual(NB - 1)
            with pe.Fori(0, STEPS - 1) as j:
                step(NB - 1, j)
            last_step(NB - 1, True)

            copy_down(1, gate[0:HALF, 0, :])
            pe.wait_ge(S["y_free"], NB + 1)
            for a in range(2):
                cols = slice(a * 512, (a + 1) * 512)
                pe.matmul(Y[0:NS, cols], ident[:, SAMP:SAMP + NS], hn[:, cols], start=True, stop=False, skip_group_check=True)
                m = pe.matmul(O[:, cols], spread[:].rearrange("p h b -> p (h b)"), xbn[:, cols], start=True, stop=True)
            m.then_inc(S["pe_spread"], 1)
            for q in range(TOPK // 2):
                pe.wait_ge(S["diag_ready"], PART * LAST + q + 1)
                for a in range(2):
                    m = pe.matmul(Y[0:NS, a * 512:(a + 1) * 512], diag[:, q % DIAGS, 0:NS],
                                  ring[:, q % RING, DM + a * 512:DM + (a + 1) * 512],
                                  start=False, stop=(q == TOPK // 2 - 1), skip_group_check=True)
                m.then_inc(S["slot_free"], 1)

        @block.scalar
        def _(act):
            def norm(n):
                act.wait_ge(S["h_ready"], n + 1)
                act.wait_ge(S["xbc_ready"], n + 1)
                act.activation(xbn[:], hn[:], ACT.Square, accum_out=nrm[:, 0:1])
                act.drain()
                act.preload_act_table_set("natural_log_exp_and_others")
                act.activation(nrm[:, 1:2], nrm[:, 0:1], ACT.Ln, bias=EPS, scale=1.0 / DM)
                act.drain()
                act.activation(nrm[:, 2:3], nrm[:, 1:2], ACT.Exp, scale=-0.5).then_inc(S["r_ready"], 1)

            def take_xbT(n):
                act.wait_ge(S["pe_xbT"], n + 1)
                act.activation(xbT[:].rearrange("p k c -> p (k c)"), O[:], ACT.Copy).then_inc(S["xbT_ready"], 1)

            def weigh(s, q, pattern):
                p, k = q // TOPK, q % TOPK
                if k == 0:
                    act.wait_ge(S["gate_ready"], 2 * s + p + 1)
                act.wait_ge(S["dot_done"], PART * s + q + 1)
                act.activation(ge[:, p, k:k + 1], dots[:, p, k:k + 1], ACT.Gelu)
                act.drain()
                act.activation(wt[:, p, k:k + 1], ge[:, p, k:k + 1], ACT.Copy, scale=gcur[:, p, k:k + 1])
                act.drain()
                act.wait_ge(S["slot_free"], PART * s + q + 1 + RING - DIAGS)
                act.activation(diag[:, q % DIAGS, 0:pattern.shape[1]], pattern, ACT.Copy,
                               scale=wt[:, p, k:k + 1]).then_inc(S["diag_ready"], 1)

            def gate_exp(s):
                act.preload_act_table_set("natural_log_exp_and_others")
                act.wait_ge(S["gd_ready"], s + 1)
                act.activation(gate[:], gate[:], ACT.Exp).then_inc(S["ge_ready"], 1)

            def step(c, j):
                s = c * STEPS + j
                for q in range(PART):
                    weigh(s, q, ident[:])
                    if q == 26:
                        gate_exp(s + 1)

            def last_step(c, sampled):
                s = c * STEPS + STEPS - 1
                for q in range(PART):
                    if q == 6:
                        norm(c + 1)
                    if q == 11:
                        take_xbT(c + 1)
                    weigh(s, q, ident[:])
                    if q == (PART - 1 if sampled else 26):
                        gate_exp(s + 1)
                final_norm(c, P)

            def final_norm(c, n):
                act.wait_ge(S["slot_free"], SLOTS * c + RING + (SLOTS if n == P else TOPK // 2))
                act.wait_ge(S["yo_free"], c + 1)
                act.activation(yo[0:n, :], Y[0:n, :], ACT.Copy).then_inc(S["y_free"], 1)
                act.drain()
                act.activation(junk[0:n, :], yo[0:n, :], ACT.Square, accum_out=nrm[0:n, 3:4])
                act.drain()
                act.preload_act_table_set("natural_log_exp_and_others")
                act.activation(nrm[0:n, 4:5], nrm[0:n, 3:4], ACT.Ln, bias=EPS, scale=1.0 / DM)
                act.drain()
                act.activation(nrm[0:n, 5:6], nrm[0:n, 4:5], ACT.Exp, scale=-0.5).then_inc(S["fr_ready"], 1)

            act.sem_inc(S["yo_free"], 1)
            norm(0)
            take_xbT(0)
            gate_exp(0)
            with act.Fori(0, NB - 1) as c:
                with act.Fori(0, STEPS - 1) as j:
                    step(c, j)
                last_step(c, False)
            with act.Fori(0, STEPS - 1) as j:
                step(NB - 1, j)
            last_step(NB - 1, True)
            for q in range(TOPK // 2):
                weigh(LAST, q, unite[:])
            final_norm(NB, NS)

        @block.vector
        def _(v):
            def add_residual(n):
                v.wait_ge(hn_in, 16 * n + 16)
                v.wait_ge(S["pe_op"], n + 1)
                v.tensor_tensor(hn[:], hn[:], O[:], ALU.add).then_inc(S["h_ready"], 1)

            def norm(n):
                v.wait_ge(S["r_ready"], n + 1)
                v.scalar_tensor_tensor(out=xbn[:], in0=hn[:], scalar=nrm[:, 2:3], in1=gffn[:], op0=ALU.mult,
                                       op1=ALU.mult).then_inc(S["xb_ready"], 1)

            def top16(vals, nums, src, width):
                tmp = rest[:, 0:width]
                v.max(vals[:, 0:8], src)
                v.drain()
                v.max_index(nums[:, 0:8], vals[:, 0:8], src)
                v.match_replace(tmp, vals[:, 0:8], src, LOW)
                v.drain()
                v.max(vals[:, 8:16], tmp)
                v.drain()
                v.max_index(nums[:, 8:16], vals[:, 8:16], tmp)
                v.drain()

            def choose(m, slot):
                v.wait_ge(S["pe_sc"], m + 1)
                standalone(v, idle)
                for p in range(2):
                    top16(tops[:, p, :], topi[:, p, :], SC[slot][:, p * NKEY:(p + 1) * NKEY], NKEY)
                v.tensor_copy(topf[:], topi[:]).then_inc(S["top_done"], 1)
                a0 = tops[:, 0, :].rearrange("p (a b) -> p a b", b=1).broadcast_to([P, TOPK, TOPK])
                v.tensor_tensor(cand[:], a0, tops[:, 1:2, :].broadcast_to([P, TOPK, TOPK]), ALU.add)
                v.drain()
                b16 = pick[:, 0, :]
                top16(b16, bc[:], cand[:].rearrange("p a b -> p (a b)"), TOPK * TOPK)
                v.tensor_copy(best[:, slot, :], pick[:, 0, :])
                v.tensor_scalar(ab[:, 0, :], bc[:], 4, None, ALU.logical_shift_right)
                v.tensor_scalar(ab[:, 1, :], bc[:], TOPK - 1, None, ALU.bitwise_and)
                v.drain()
                full = [P, 2, TOPK, TOPK]
                v.tensor_tensor(hot[:], ab[:].rearrange("p a (k i) -> p a k i", i=1).broadcast_to(full),
                                iota[:].rearrange("p (a k i) -> p a k i", a=1, k=1).broadcast_to(full), ALU.is_equal)
                v.drain()
                v.tensor_tensor(hot[:], hot[:], topf[:].rearrange("p a (k i) -> p a k i", k=1).broadcast_to(full), ALU.mult)
                v.drain()
                v.tensor_reduce(pick[:], hot[:], AX.X, ALU.add)
                v.drain()
                v.scalar_tensor_tensor(out=idx[:, slot, :], in0=pick[:, 0, :], scalar=float(NKEY), in1=pick[:, 1, :],
                                       op0=ALU.mult, op1=ALU.add)
                v.drain()

            def gate_gaps():
                v.tensor_tensor(gate[:], best[:], best[:, :, 0:1].broadcast_to([P, 2, TOPK]), ALU.subtract).then_inc(S["gd_ready"], 1)

            def gates(s):
                v.wait_ge(S["ge_ready"], s + 1)
                v.tensor_reduce(gsum[:, 0, :], gate[:], AX.X, ALU.add)
                v.drain()
                v.reciprocal(gsum[:, 1, :], gsum[:, 0, :])
                v.drain()
                v.tensor_tensor(gate[:], gate[:], gsum[:, 1, :].rearrange("p (h c) -> p h c", c=1).broadcast_to([P, 2, TOPK]), ALU.mult)
                v.drain()

            def next_indices(slot):
                v.tensor_copy(icur[:, slot, :], idx[:, slot, :]).then_inc(S["idx_ready"], 1)

            def next_gates(slot):
                v.tensor_copy(gcur[:, slot, :], gate[:, slot, :]).then_inc(S["gate_ready"], 1)

            def dot(s, q, rows):
                r = q % RING
                v.wait_ge(g_in[r], (PART // RING * s + q // RING + 1) * 16)
                v.tensor_tensor_reduce(ring[:, r, 0:DM], ring[:, r, 0:DM], rows, 1.0, 0.0, ALU.mult, ALU.add,
                                       dots[:, q // TOPK, q % TOPK:q % TOPK + 1]).then_inc(S["dot_done"], 1)

            def take_pair(x, n, done):
                v.tensor_copy(x[0:HALF, 0, 0:TOPK // 2], SC[1][0:HALF, n * TOPK:n * TOPK + TOPK // 2])
                v.tensor_copy(x[HALF:P, 0, 0:TOPK // 2], SC[1][HALF:P, n * TOPK + TOPK // 2:(n + 1) * TOPK]).then_inc(done, 1)

            def tile_start():
                v.drain()
                v.tensor_copy(xbc[:], xbn[:]).then_inc(S["xbc_ready"], 1)
                v.drain()

            def step(c, j):
                s = c * STEPS + j
                for q in range(PART):
                    if q == 0:
                        next_indices(1)
                        next_gates(0)
                        v.drain()
                    if q == 16:
                        next_indices(0)
                        next_gates(1)
                        v.drain()
                    dot(s, q, xbc[:])
                    if q == 7:
                        choose(2 * s + 2, 0)
                    if q == 23:
                        choose(2 * s + 3, 1)
                        gate_gaps()
                    if q == 28:
                        gates(s + 1)

            def last_step(c, sampled):
                s = c * STEPS + STEPS - 1
                for q in range(PART):
                    if q == 0:
                        next_indices(1)
                        next_gates(0)
                        v.drain()
                    if q == 16:
                        if not sampled:
                            next_indices(0)
                        next_gates(1)
                        v.drain()
                    dot(s, q, xbc[:])
                    if q == 5:
                        add_residual(c + 1)
                    if q == 7:
                        norm(c + 1)
                    if not sampled and q == 15:
                        choose(2 * s + 2, 0)
                    if not sampled and q == 24:
                        choose(2 * s + 3, 1)
                        gate_gaps()
                    if not sampled and q == 28:
                        gates(s + 1)
                    if sampled and q == 30:
                        choose(2 * s + 2, 0)
                        v.tensor_copy(chosen[:], idx[0:HALF, 0, :]).then_inc(S["pair_ready"], 1)
                        gate_gaps()
                        v.wait_ge(S["pe_pair"], 1)
                        take_pair(icur, 0, S["idx_ready"])
                if sampled:
                    gates(s + 1)
                    v.tensor_copy(gsum[:, 0, :], gsum[:, 1, :]).then_inc(S["pair_ready"], 1)
                    v.wait_ge(S["pe_pair"], 2)
                    take_pair(gcur, 1, S["gate_ready"])
                final_scale(c, P)

            def final_scale(c, n):
                v.wait_ge(S["fr_ready"], c + 1)
                v.scalar_tensor_tensor(out=yo[0:n, :], in0=yo[0:n, :], scalar=nrm[0:n, 5:6], in1=gfin[0:n, :], op0=ALU.mult,
                                       op1=ALU.mult).then_inc(S["y_ready"], 1)

            v.wait_ge(c_in, 16 * NC_IN)
            v.wait_ge(S["iota_ready"], 1)
            v.tensor_reduce(unite[:], ident[:].rearrange("p (h b) -> p b h", b=NS), AX.X, ALU.add)
            v.tensor_copy(twice[:], ident[0:HALF, 0:HALF].rearrange("p (a b) -> p a b", a=1).broadcast_to([HALF, 2, HALF]))
            v.tensor_copy(spread[:], ident[:, SAMP:SAMP + NS].rearrange("p (h b) -> p h b", h=1).broadcast_to([P, 2 * PH, NS]))\
                .then_inc(S["xbc_ready"], 1)
            add_residual(0)
            norm(0)
            choose(0, 0)
            next_indices(0)
            choose(1, 1)
            gate_gaps()
            gates(0)

            with v.Fori(0, NB - 1) as c:
                tile_start()
                with v.Fori(0, STEPS - 1) as j:
                    step(c, j)
                last_step(c, False)
            tile_start()
            with v.Fori(0, STEPS - 1) as j:
                step(NB - 1, j)
            last_step(NB - 1, True)
            v.wait_ge(S["pe_spread"], 1)
            for q in range(TOPK // 2):
                dot(LAST, q, O[:])
            final_scale(NB, NS)


def constants():
    tok = np.arange(P)
    masks = []
    for g in range(LEVELS):
        half = P >> (g + 1)
        same = (tok[:, None] // (2 * half)) == (tok[None, :] // (2 * half))
        masks.append(same & (tok[:, None] % (2 * half) < half) & (tok[None, :] % (2 * half) >= half))
    masks.append(tok[:, None] == tok[None, :])
    inv = np.float32(10000.0) ** (-np.arange(HD // 2, dtype=np.float32) * np.float32(2.0) / np.float32(HD))
    pos = np.arange((NB + 1) * P) - (P - META)
    pos[:NS] = 2048
    ang = pos.astype(np.float32)[:, None] * inv.astype(np.float32)[None, :]
    key, far = np.arange(2 * WIN)[None, :], -1.0e30
    wmask = np.zeros((NB, P, 2 * WIN), np.float32)
    wmask[:] = np.where((key <= tok[:, None] + WIN) & (key >= tok[:, None]), 0.0, far)
    wmask[0, :, 0:P - META] = far
    sel = np.zeros((NS, NS, P), np.float32)
    sel[np.arange(NS), np.arange(NS)] = 1.0
    reset = np.ones((P, HH, P), np.float32)
    reset[:, :, 0] = 0.0
    return {
        "ident": np.eye(P, dtype=np.float32),
        "level_masks": np.concatenate([m.astype(np.int32) for m in masks], axis=1),
        "rope": np.concatenate([np.cos(ang), np.sin(ang)], axis=1).astype(np.float32),
        "wmask": wmask.reshape(NB * P, 2 * WIN),
        "sel": sel.reshape(NS, NS * P),
        "reset": reset.reshape(P, HW),
    }


def lay_out(x_prompt, x_sample, state_hgrn, cache_k, cache_v, meta_tokens, lb_logits, norm_mix, w_in,
            hgrn_norm, attn_sink, w_out, norm_ffn, peer_wq, peer_keys, peer_u, peer_v, norm_final):
    a = {k: np.asarray(v) for k, v in locals().items()}
    tile0 = np.zeros((P, DM), np.float32)
    tile0[:NS] = a["x_sample"].reshape(NS, DM)
    sampled = np.zeros((P, DM), np.float32)
    sampled[SAMP:SAMP + NS] = tile0[:NS]
    tile0[P - META:] = a["meta_tokens"]
    return {
        "x_all": np.concatenate([tile0, a["x_prompt"].reshape(NB * P, DM), sampled]),
        "state_s": a["state_hgrn"].reshape(NS * HH, DK, DK),
        "cache_k": a["cache_k"].reshape(NS, WIN, KV * HD),
        "cache_v": a["cache_v"].reshape(NS, WIN, KV * HD),
        "lb_logits": a["lb_logits"].reshape(2, HW),
        "norm_mix": a["norm_mix"].reshape(1, DM),
        "w_in": a["w_in"].reshape(DM, IN_W),
        "hgrn_norm": a["hgrn_norm"].reshape(1, HW),
        "attn_sink": a["attn_sink"].reshape(1, SH),
        "w_out": a["w_out"].reshape(DM, DM),
        "norm_ffn": a["norm_ffn"].reshape(1, DM),
        "wq_T": np.ascontiguousarray(a["peer_wq"].reshape(DM, 2 * PH * NKEY).T),
        "keys_T": np.ascontiguousarray(a["peer_keys"].reshape(2 * PH, NKEY, P).transpose(2, 0, 1).reshape(P, 2 * PH * NKEY)),
        "uv": np.concatenate([a["peer_u"].reshape(NEXP, DM), a["peer_v"].reshape(NEXP, DM)], axis=1),
        "norm_final": a["norm_final"].reshape(1, DM),
        **constants(),
    }


OUTS = {
    "y_p": (NB * P, DM), "y_s": (NS, DM), "new_state_p": (HH, DK, DK), "new_k_p": (WIN, KV * HD), "new_v_p": (WIN, KV * HD),
    "new_state_s": (NS * HH, DK, DK), "new_k_s": (NS, WIN, KV * HD), "new_v_s": (NS, WIN, KV * HD),
}


def program(nc, arrays, debug=False):
    io = {n: nc.dram_tensor(n, a.shape, mybir.dt.from_np(a.dtype), kind="ExternalInput").ap() for n, a in arrays.items()}
    io |= {n: nc.dram_tensor(n, s, F32, kind="ExternalOutput").ap() for n, s in OUTS.items()}
    scratch = {"kind": "ExternalOutput"} if debug else {}
    io["mix_scratch"] = nc.dram_tensor("mix_scratch", [NB + 1, P, KT, P], F32, **scratch).ap()
    with ExitStack() as ctx:
        weights = Weights(nc, ctx)
        mixer_program(nc, io, weights)
        peer_program(nc, io, weights)


def kernel(**inputs):
    from concourse import bacc
    from concourse.bass_utils import run_bass_kernel_spmd

    arrays = lay_out(**inputs)
    nc = bacc.Bacc("TRN2", target_bir_lowering=False, num_devices=1)
    program(nc, arrays)
    r = run_bass_kernel_spmd(nc, [arrays], core_ids=[0]).results[0]
    return (r["y_p"].reshape(1, NB * P, DM), r["y_s"].reshape(NS, 1, DM),
            r["new_state_p"].reshape(1, 1, HH, DK, DK), r["new_k_p"].reshape(1, 1, WIN, KV, HD),
            r["new_v_p"].reshape(1, 1, WIN, KV, HD), r["new_state_s"].reshape(1, NS, HH, DK, DK),
            r["new_k_s"].reshape(1, NS, WIN, KV, HD), r["new_v_s"].reshape(1, NS, WIN, KV, HD))
```
